# Optimizing a Trainium2 kernel written in Bass

```python
import jax, jax.numpy as jnp
from jax import lax
import numpy as np

D_MODEL = 1024
BATCH = 1
SEQ = 256
DEPTH = 2

N_A_LAYERS = DEPTH // 2
N_B_LAYERS = DEPTH - N_A_LAYERS

EPS = 1e-6
PLE_DIM = 256
D_FF = ((8 * D_MODEL // 3 + 255) // 256) * 256

A_KEY_DIM = 128
A_HEADS = D_MODEL // A_KEY_DIM
A_VAL_DIM = D_MODEL // A_HEADS
A_WIDTH = A_HEADS * A_KEY_DIM
A_CHUNK = 64

B_HEADS = 16
B_NOPE = 128
B_ROPE = 64
B_VDIM = 128
B_Q_LORA = 512
B_KV_LORA = 256
Q_BLOCK = 128
ROPE_THETA = 10000.0


def _rmsnorm(x, g):
    x32 = x.astype(jnp.float32)
    y = x32 * lax.rsqrt(jnp.mean(x32 * x32, axis=-1, keepdims=True) + EPS)
    return (y * g.astype(jnp.float32)).astype(x.dtype)

def _swiglu(h, w_in, w_out):
    gate, up = jnp.split(h @ w_in, 2, axis=-1)
    return (jax.nn.silu(gate) * up) @ w_out

def _rope(x, positions):
    d = x.shape[-1]
    inv_freq = 1.0 / (ROPE_THETA ** (jnp.arange(0, d, 2, dtype=jnp.float32) / d))
    ang = positions.astype(jnp.float32)[..., None] * inv_freq
    ang = ang.reshape(ang.shape[:2] + (1,) * (x.ndim - 3) + (d // 2,))
    cos, sin = jnp.cos(ang), jnp.sin(ang)
    x32 = x.astype(jnp.float32)
    x1, x2 = x32[..., : d // 2], x32[..., d // 2:]
    return jnp.concatenate([x1 * cos - x2 * sin, x2 * cos + x1 * sin], axis=-1).astype(x.dtype)

def _hgrn2_chunk(state, inp):
    q, k, v, g = inp
    b = jnp.cumsum(g, axis=2)
    o_inter = jnp.einsum('bhtk,bhkv->bhtv', q * jnp.exp(b), state)
    causal = jnp.tril(jnp.ones((A_CHUNK, A_CHUNK), dtype=bool))[:, :, None]
    diff = b[:, :, :, None, :] - b[:, :, None, :, :]
    decay = jnp.where(causal, jnp.exp(jnp.where(causal, diff, 0.0)), 0.0)
    scores = jnp.einsum('bhtk,bhsk,bhtsk->bhts', q, k, decay)
    o_intra = jnp.einsum('bhts,bhsv->bhtv', scores, v)
    b_last = b[:, :, -1:, :]
    new_state = jnp.exp(b_last[:, :, 0, :])[..., None] * state + jnp.einsum(
        'bhsk,bhsv->bhkv', k * jnp.exp(b_last - b), v)
    return new_state, o_inter + o_intra

def _hgrn2_mixer(h, w_in, lb, out_gain, w_out):
    bsz, seq, _ = h.shape
    q, f_logit, i, g = jnp.split(h @ w_in, 4, axis=-1)
    f_logit = f_logit.astype(jnp.float32)
    lb = lb.astype(jnp.float32)
    log_f = jnp.log(lb + (1.0 - lb) * jax.nn.sigmoid(f_logit))
    k = (1.0 - lb) * jax.nn.sigmoid(-f_logit)
    n_chunks = seq // A_CHUNK

    def to_chunks(t, d):
        t = t.astype(jnp.float32).reshape(bsz, n_chunks, A_CHUNK, A_HEADS, d)
        return t.transpose(1, 0, 3, 2, 4)

    qc = to_chunks(q, A_KEY_DIM) * (A_KEY_DIM ** -0.5)
    kc = to_chunks(k, A_KEY_DIM)
    vc = to_chunks(i, A_VAL_DIM)
    gc = to_chunks(log_f, A_KEY_DIM)
    s0 = jnp.zeros((bsz, A_HEADS, A_KEY_DIM, A_VAL_DIM), jnp.float32)
    _, o = lax.scan(_hgrn2_chunk, s0, (qc, kc, vc, gc))
    o = o.transpose(1, 0, 3, 2, 4).reshape(bsz, seq, A_HEADS, A_VAL_DIM)
    o = _rmsnorm(o, out_gain).reshape(bsz, seq, A_HEADS * A_VAL_DIM)
    o = o * jax.nn.sigmoid(g.astype(jnp.float32))
    return o.astype(h.dtype) @ w_out

def _mla_shared_kv(x, positions, norm_in, w_down, latent_norm, w_up):
    bsz, seq, _ = x.shape
    h = _rmsnorm(x, norm_in)
    c_kv, k_r = jnp.split(h @ w_down, [B_KV_LORA], axis=-1)
    c_kv = _rmsnorm(c_kv, latent_norm)
    kv = (c_kv @ w_up).reshape(bsz, seq, B_HEADS, B_NOPE + B_VDIM)
    k_nope, v = jnp.split(kv, [B_NOPE], axis=-1)
    k_rope = _rope(k_r, positions)
    return k_nope, k_rope, v

def _mla_mixer(h, positions, k_nope, k_rope, v, w_dq, q_norm, w_uq, w_out):
    bsz, seq, _ = h.shape
    c_q = _rmsnorm(h @ w_dq, q_norm)
    q = (c_q @ w_uq).reshape(bsz, seq, B_HEADS, B_NOPE + B_ROPE)
    q_nope, q_rope = jnp.split(q, [B_NOPE], axis=-1)
    q_rope = _rope(q_rope, positions)
    n_blocks = seq // Q_BLOCK
    scale = (B_NOPE + B_ROPE) ** -0.5

    def blocks(t):
        return t.reshape((bsz, n_blocks, Q_BLOCK) + t.shape[2:]).swapaxes(0, 1)

    key_idx = jnp.arange(seq)

    def attend(args):
        qn, qr, blk = args
        s = (jnp.einsum('bqhd,bkhd->bhqk', qn, k_nope)
             + jnp.einsum('bqhd,bkd->bhqk', qr, k_rope)).astype(jnp.float32) * scale
        q_idx = blk * Q_BLOCK + jnp.arange(Q_BLOCK)
        mask = q_idx[:, None] >= key_idx[None, :]
        s = jnp.where(mask[None, None], s, -jnp.inf)
        pr = jax.nn.softmax(s, axis=-1).astype(v.dtype)
        return jnp.einsum('bhqk,bkhd->bqhd', pr, v)

    o = lax.map(attend, (blocks(q_nope), blocks(q_rope), jnp.arange(n_blocks, dtype=jnp.int32)))
    o = o.swapaxes(0, 1).reshape(bsz, seq, B_HEADS * B_VDIM)
    return o @ w_out

def first_inputs(seed: int = 0) -> dict:
    key = jax.random.key(seed)
    ks = jax.random.split(key, 24)
    f32 = jnp.float32

    def w(k, shape, fan_in):
        return jax.random.normal(k, shape, f32) * (fan_in ** -0.5)

    def gain(k, shape):
        return 1.0 + 0.02 * jax.random.normal(k, shape, f32)

    offset = jax.random.randint(ks[2], (BATCH, 1), 0, 1024, dtype=jnp.int32)
    positions = offset + jnp.arange(SEQ, dtype=jnp.int32)[None, :]
    return {
        'x': jax.random.normal(ks[0], (BATCH, SEQ, D_MODEL), f32),
        'p': jax.random.normal(ks[1], (DEPTH, BATCH, SEQ, PLE_DIM), f32),
        'positions': positions,
        'norm_gains': gain(ks[3], (DEPTH, 4, D_MODEL)),
        'ffn_w_in': w(ks[4], (DEPTH, 2, D_MODEL, 2 * D_FF), D_MODEL),
        'ffn_w_out': w(ks[5], (DEPTH, 2, D_FF, D_MODEL), D_FF),
        'ple_w_gate': w(ks[6], (DEPTH, D_MODEL, D_MODEL), D_MODEL),
        'ple_w_in': w(ks[7], (DEPTH, PLE_DIM, D_MODEL), PLE_DIM),
        'a_w_in': w(ks[8], (N_A_LAYERS, D_MODEL, 4 * A_WIDTH), D_MODEL),
        'a_lb_logits': 0.1 * jax.random.normal(ks[9], (N_A_LAYERS + 1, A_WIDTH), f32),
        'a_out_gain': gain(ks[10], (N_A_LAYERS, A_VAL_DIM)),
        'a_w_out': w(ks[11], (N_A_LAYERS, A_WIDTH, D_MODEL), A_WIDTH),
        'kv_norm_in': gain(ks[12], (D_MODEL,)),
        'kv_w_down': w(ks[13], (D_MODEL, B_KV_LORA + B_ROPE), D_MODEL),
        'kv_latent_norm': gain(ks[14], (B_KV_LORA,)),
        'kv_w_up': w(ks[15], (B_KV_LORA, B_HEADS * (B_NOPE + B_VDIM)), B_KV_LORA),
        'b_w_dq': w(ks[16], (N_B_LAYERS, D_MODEL, B_Q_LORA), D_MODEL),
        'b_q_norm': gain(ks[17], (N_B_LAYERS, B_Q_LORA)),
        'b_w_uq': w(ks[18], (N_B_LAYERS, B_Q_LORA, B_HEADS * (B_NOPE + B_ROPE)), B_Q_LORA),
        'b_w_out': w(ks[19], (N_B_LAYERS, B_HEADS * B_VDIM, D_MODEL), B_HEADS * B_VDIM),
        'final_norm': gain(ks[20], (D_MODEL,)),
    }

def first_block(x, p, positions, norm_gains, ffn_w_in, ffn_w_out, ple_w_gate, ple_w_in,
              a_w_in, a_lb_logits, a_out_gain, a_w_out,
              kv_norm_in, kv_w_down, kv_latent_norm, kv_w_up,
              b_w_dq, b_q_norm, b_w_uq, b_w_out, final_norm):
    lower_bounds = jnp.cumsum(jax.nn.softmax(a_lb_logits.astype(jnp.float32), axis=0), axis=0)
    shared = None
    if N_A_LAYERS == 0:
        shared = _mla_shared_kv(x, positions, kv_norm_in, kv_w_down, kv_latent_norm, kv_w_up)
    for li in range(DEPTH):
        g = norm_gains[li]
        x = x + 0.5 * _swiglu(_rmsnorm(x, g[0]), ffn_w_in[li, 0], ffn_w_out[li, 0])
        h = _rmsnorm(x, g[1])
        if li < N_A_LAYERS:
            x = x + _hgrn2_mixer(h, a_w_in[li], lower_bounds[li], a_out_gain[li], a_w_out[li])
        else:
            bi = li - N_A_LAYERS
            k_nope, k_rope, v = shared
            x = x + _mla_mixer(h, positions, k_nope, k_rope, v,
                               b_w_dq[bi], b_q_norm[bi], b_w_uq[bi], b_w_out[bi])
        x = x + 0.5 * _swiglu(_rmsnorm(x, g[2]), ffn_w_in[li, 1], ffn_w_out[li, 1])
        gate = jax.nn.sigmoid((_rmsnorm(x, g[3]) @ ple_w_gate[li]).astype(jnp.float32))
        x = x + (gate * (p[li] @ ple_w_in[li]).astype(jnp.float32)).astype(x.dtype)
        if li == N_A_LAYERS - 1:
            shared = _mla_shared_kv(x, positions, kv_norm_in, kv_w_down, kv_latent_norm, kv_w_up)
    return _rmsnorm(x, final_norm)


HEAD_DIM = 64
SB_HEADS = 8
MOBA_HEADS = 8
SB_WIDTH = SB_HEADS * HEAD_DIM
MOBA_WIDTH = MOBA_HEADS * HEAD_DIM
SB_Q_BLOCK = 128
MOBA_BLOCK = 256
MOBA_TOPK = 3
MOBA_Q_CHUNK = 128
ROPE_THETA_2 = 500000.0
ROPE_DIM = HEAD_DIM // 4
D_FF_2 = -(-8 * D_MODEL // (3 * 256)) * 256
DEEPNORM_ALPHA = (2 * DEPTH) ** 0.25
DEEPNORM_BETA = (8 * DEPTH) ** -0.25
LN_EPS = 1e-5
IN_COLS = 3 * SB_WIDTH + 3 * MOBA_WIDTH + 2 * D_MODEL


def layer_norm(x, g, b):
    xf = x.astype(jnp.float32)
    mu = jnp.mean(xf, axis=-1, keepdims=True)
    var = jnp.mean(jnp.square(xf - mu), axis=-1, keepdims=True)
    y = (xf - mu) * lax.rsqrt(var + LN_EPS) * g.astype(jnp.float32) + b.astype(jnp.float32)
    return y.astype(x.dtype)

def partial_rope(x, pos):
    half = ROPE_DIM // 2
    inv_freq = ROPE_THETA_2 ** (-jnp.arange(0, ROPE_DIM, 2, dtype=jnp.float32) / ROPE_DIM)
    ang = pos.astype(jnp.float32)[:, None] * inv_freq[None, :]
    cos, sin = jnp.cos(ang), jnp.sin(ang)
    xf = x.astype(jnp.float32)
    x1, x2, rest = xf[..., :half], xf[..., half:ROPE_DIM], xf[..., ROPE_DIM:]
    out = jnp.concatenate([x1 * cos - x2 * sin, x2 * cos + x1 * sin, rest], axis=-1)
    return out.astype(x.dtype)

def stick_breaking_attention(q, k, v):
    B, H, S, dh = q.shape
    nblk = S // SB_Q_BLOCK
    scale = dh ** -0.5
    kpos = jnp.arange(S)
    qb = q.reshape(B, H, nblk, SB_Q_BLOCK, dh).transpose(2, 0, 1, 3, 4)

    def block(args):
        qi, i = args
        qpos = i * SB_Q_BLOCK + jnp.arange(SB_Q_BLOCK)
        z = jnp.einsum('bhqd,bhkd->bhqk', qi, k).astype(jnp.float32) * scale
        past = kpos[None, :] < qpos[:, None]
        log_keep = jnp.where(past, jax.nn.log_sigmoid(-z), 0.0)
        suffix = lax.cumsum(log_keep, axis=3, reverse=True) - log_keep
        w = jnp.where(past, jnp.exp(jax.nn.log_sigmoid(z) + suffix), 0.0)
        return jnp.einsum('bhqk,bhkd->bhqd', w.astype(v.dtype), v)

    out = lax.map(block, (qb, jnp.arange(nblk)))
    return out.transpose(1, 2, 0, 3, 4).reshape(B, H, S, dh)

def moba_attention(q, k, v):
    B, H, S, dh = q.shape
    nb = -(-S // MOBA_BLOCK)
    pad = nb * MOBA_BLOCK - S
    kp = jnp.pad(k, ((0, 0), (0, 0), (0, pad), (0, 0)))
    vp = jnp.pad(v, ((0, 0), (0, 0), (0, pad), (0, 0)))
    kb = kp.reshape(B, H, nb, MOBA_BLOCK, dh)
    vb = vp.reshape(B, H, nb, MOBA_BLOCK, dh)
    kmean = jnp.mean(kb.astype(jnp.float32), axis=3).astype(k.dtype)
    topk = min(MOBA_TOPK, nb)
    nchunk = S // MOBA_Q_CHUNK
    qc = q.reshape(B, H, nchunk, MOBA_Q_CHUNK, dh).transpose(2, 0, 1, 3, 4)
    bi = jnp.arange(B)[:, None, None, None]
    hi = jnp.arange(H)[None, :, None, None]
    blk_ids = jnp.arange(nb)
    scale = dh ** -0.5

    def chunk(args):
        qi, c = args
        qpos = c * MOBA_Q_CHUNK + jnp.arange(MOBA_Q_CHUNK)
        own = (c * MOBA_Q_CHUNK) // MOBA_BLOCK
        gate = jnp.einsum('bhqd,bhnd->bhqn', qi, kmean).astype(jnp.float32)
        gate = jnp.where(blk_ids < own, gate, -jnp.inf)
        _, idx = lax.top_k(gate, topk)
        valid = idx < own
        k_sel = kb[bi, hi, idx]
        v_sel = vb[bi, hi, idx]
        s_sel = jnp.einsum('bhqd,bhqnkd->bhqnk', qi, k_sel).astype(jnp.float32) * scale
        s_sel = jnp.where(valid[..., None], s_sel, -jnp.inf).reshape(B, H, MOBA_Q_CHUNK, topk * MOBA_BLOCK)
        k_own = lax.dynamic_slice_in_dim(kb, own, 1, axis=2)[:, :, 0]
        v_own = lax.dynamic_slice_in_dim(vb, own, 1, axis=2)[:, :, 0]
        s_own = jnp.einsum('bhqd,bhkd->bhqk', qi, k_own).astype(jnp.float32) * scale
        own_pos = own * MOBA_BLOCK + jnp.arange(MOBA_BLOCK)
        s_own = jnp.where(own_pos[None, :] <= qpos[:, None], s_own, -jnp.inf)
        p = jax.nn.softmax(jnp.concatenate([s_sel, s_own], axis=-1), axis=-1).astype(v.dtype)
        p_sel = p[..., :topk * MOBA_BLOCK].reshape(B, H, MOBA_Q_CHUNK, topk, MOBA_BLOCK)
        p_own = p[..., topk * MOBA_BLOCK:]
        return (jnp.einsum('bhqnk,bhqnkd->bhqd', p_sel, v_sel)
                + jnp.einsum('bhqk,bhkd->bhqd', p_own, v_own))

    out = lax.map(chunk, (qc, jnp.arange(nchunk)))
    return out.transpose(1, 2, 0, 3, 4).reshape(B, H, S, dh)

def heads(t, n_heads):
    B, S, _ = t.shape
    return t.reshape(B, S, n_heads, HEAD_DIM).transpose(0, 2, 1, 3)

def merge_heads(t):
    B, H, S, dh = t.shape
    return t.transpose(0, 2, 1, 3).reshape(B, S, H * dh)

def hybrid_mixer(x, w_in, w_branch_sb, w_branch_moba, w_out):
    S = x.shape[1]
    proj = x @ w_in
    cuts = np.cumsum([SB_WIDTH, SB_WIDTH, SB_WIDTH, MOBA_WIDTH, MOBA_WIDTH, MOBA_WIDTH, D_MODEL]).tolist()
    q_sb, k_sb, v_sb, q_mb, k_mb, v_mb, g_sb, g_mb = jnp.split(proj, cuts, axis=-1)
    pos = jnp.arange(S)
    o_sb = stick_breaking_attention(heads(q_sb, SB_HEADS), heads(k_sb, SB_HEADS), heads(v_sb, SB_HEADS))
    o_mb = moba_attention(partial_rope(heads(q_mb, MOBA_HEADS), pos),
                          partial_rope(heads(k_mb, MOBA_HEADS), pos),
                          heads(v_mb, MOBA_HEADS))
    branch_sb = merge_heads(o_sb) @ w_branch_sb
    branch_mb = merge_heads(o_mb) @ w_branch_moba
    merged = jax.nn.sigmoid(g_sb) * branch_sb + jax.nn.sigmoid(g_mb) * branch_mb
    return merged @ w_out

def swiglu(x, w_gate, w_up, w_down):
    return (jax.nn.silu(x @ w_gate) * (x @ w_up)) @ w_down

def second_inputs(seed: int = 0) -> dict:
    key = jax.random.key(seed)
    ks = jax.random.split(key, 12)
    nrm = lambda k, shape, s: jax.random.normal(k, shape, jnp.float32) * s
    L = DEPTH
    return {
        "x": jax.random.normal(ks[0], (BATCH, SEQ, D_MODEL), jnp.float32),
        "w_in": nrm(ks[1], (L, D_MODEL, IN_COLS), D_MODEL ** -0.5),
        "w_branch_sb": nrm(ks[2], (L, SB_WIDTH, D_MODEL), SB_WIDTH ** -0.5),
        "w_branch_moba": nrm(ks[3], (L, MOBA_WIDTH, D_MODEL), MOBA_WIDTH ** -0.5),
        "w_out": nrm(ks[4], (L, D_MODEL, D_MODEL), D_MODEL ** -0.5 * DEEPNORM_BETA),
        "ln_mix_g": 1.0 + nrm(ks[5], (L, D_MODEL), 0.02),
        "ln_mix_b": nrm(ks[6], (L, D_MODEL), 0.02),
        "w_ffn_gate": nrm(ks[7], (L, D_MODEL, D_FF_2), D_MODEL ** -0.5),
        "w_ffn_up": nrm(ks[8], (L, D_MODEL, D_FF_2), D_MODEL ** -0.5),
        "w_ffn_down": nrm(ks[9], (L, D_FF_2, D_MODEL), D_FF_2 ** -0.5 * DEEPNORM_BETA),
        "ln_ffn_g": 1.0 + nrm(ks[10], (L, D_MODEL), 0.02),
        "ln_ffn_b": nrm(ks[11], (L, D_MODEL), 0.02),
    }

def second_block(x, w_in, w_branch_sb, w_branch_moba, w_out, ln_mix_g, ln_mix_b,
              w_ffn_gate, w_ffn_up, w_ffn_down, ln_ffn_g, ln_ffn_b):
    for l in range(DEPTH):
        mix = hybrid_mixer(x, w_in[l], w_branch_sb[l], w_branch_moba[l], w_out[l])
        x = layer_norm(DEEPNORM_ALPHA * x + mix, ln_mix_g[l], ln_mix_b[l])
        ffn = swiglu(x, w_ffn_gate[l], w_ffn_up[l], w_ffn_down[l])
        x = layer_norm(DEEPNORM_ALPHA * x + ffn, ln_ffn_g[l], ln_ffn_b[l])
    return x


def setup_inputs(seed=0):
    out = dict(first_inputs(seed))
    for name, value in second_inputs(seed + 1).items():
        if name != "x":
            out[name + "_2"] = value
    return out


def reference(
    x, p, positions, norm_gains, ffn_w_in, ffn_w_out, ple_w_gate, ple_w_in, a_w_in, a_lb_logits,
    a_out_gain, a_w_out, kv_norm_in, kv_w_down, kv_latent_norm, kv_w_up, b_w_dq, b_q_norm,
    b_w_uq, b_w_out, final_norm, w_in_2, w_branch_sb_2, w_branch_moba_2, w_out_2, ln_mix_g_2,
    ln_mix_b_2, w_ffn_gate_2, w_ffn_up_2, w_ffn_down_2, ln_ffn_g_2, ln_ffn_b_2,
):
    x = first_block(
        x, p, positions, norm_gains, ffn_w_in, ffn_w_out, ple_w_gate, ple_w_in, a_w_in,
        a_lb_logits, a_out_gain, a_w_out, kv_norm_in, kv_w_down, kv_latent_norm, kv_w_up,
        b_w_dq, b_q_norm, b_w_uq, b_w_out, final_norm,
    )
    return second_block(
        x, w_in_2, w_branch_sb_2, w_branch_moba_2, w_out_2, ln_mix_g_2, ln_mix_b_2,
        w_ffn_gate_2, w_ffn_up_2, w_ffn_down_2, ln_ffn_g_2, ln_ffn_b_2,
    )


_drawn_inputs = setup_inputs


def setup_inputs(seed=0):
    import zlib

    import numpy as np

    out = dict(_drawn_inputs(seed))
    spreads = {}
    factors = {'a_out_gain': 5.269,
     'kv_norm_in': 8.0,
     'kv_latent_norm': 8.0,
     'b_q_norm': 8.0,
     'final_norm': 2.798}
    for name, (base, spread) in spreads.items():
        noise = np.random.default_rng([zlib.crc32(name.encode()), seed]).standard_normal(out[name].shape)
        drawn = base * np.exp(spread * noise) if base else spread * noise
        out[name] = __import__('jax').numpy.asarray(drawn.astype(out[name].dtype))
    for name, factor in factors.items():
        out[name] = (out[name] * factor).astype(out[name].dtype)
    return out
```

```python
from contextlib import ExitStack, contextmanager

import numpy as np

import concourse.bass as bass
from concourse import mybir

F32 = mybir.dt.float32
F32R = mybir.dt.float32r
I32 = mybir.dt.int32
U32 = mybir.dt.uint32
ALU = mybir.AluOpType
ACT = mybir.ActivationFunctionType
AX = mybir.AxisListType

P = 128
S = 256
TB = S // P
D = 1024
KD = D // P
DFF = 2816
FC = 256
NFF = DFF // FC
PLE = 256
SLOT = 2048
RING = 3
A_HEADS, A_DIM = 8, 128
LEVELS = 8
B_HEADS, B_NOPE, B_ROPE, B_VDIM = 16, 128, 64, 128
B_Q, B_KV = 512, 256
C_HEADS, C_DIM = 8, 64
C_WIDTH = C_HEADS * C_DIM
EPS, LN_EPS = 1e-6, 1e-5
ALPHA = 4 ** 0.25
SEG = P + S
TWO_PI = 2 * np.pi
PI_HI = 6.28125
PI_MID = float(np.float32(int((TWO_PI - PI_HI) * 2 ** 21) / 2 ** 21))
PI_LO = float(TWO_PI - PI_HI - PI_MID)
MAGIC = 1.5 * 2.0 ** 23
LN_FLOOR = 2.0 ** -60

GAIN_ROWS = [("norm_gains", 64), ("kv_norm_in", 8), ("kv_latent_norm", 2), ("b_q_norm", 4),
             ("a_out_gain", 1), ("a_lb_logits", 16)]
GAIN_AT = {}
_n = 0
for _name, _rows in GAIN_ROWS:
    GAIN_AT[_name] = _n
    _n += _rows
N_GAINS = _n

CONST_AT = {}
_n = 0
for _name, _w in [("identity", P), ("rotate_mla", P), ("rotate_moba", P), ("causal", SEG), ("strict", SEG),
                  ("later", P), ("ones", S), ("levels", LEVELS * P), ("restart", S), ("moba_cos", S),
                  ("moba_sin", S), ("inv_freq", 1)]:
    CONST_AT[_name] = (_n, _w)
    _n += _w
N_CONST = _n


def constants():
    c = np.zeros((P, N_CONST), np.float32)

    def put(name, a):
        at, w = CONST_AT[name]
        c[:, at:at + w] = a

    i = np.arange(P)
    put("identity", np.eye(P))

    def rotation(group, half):
        r = np.zeros((P, P))
        for g in range(0, P, group):
            for j in range(half):
                r[g + half + j, g + j] = -1.0
                r[g + j, g + half + j] = 1.0
        return r

    put("rotate_mla", rotation(B_ROPE, B_ROPE // 2))
    put("rotate_moba", rotation(C_DIM, C_DIM // 8))
    tri = np.where(i[:, None] >= i[None, :], 0.0, -1e30)
    put("causal", np.concatenate([tri, np.zeros((P, P)), tri], 1))
    past = (i[:, None] < i[None, :]).astype(np.float32)
    put("strict", np.concatenate([past, np.ones((P, P)), past], 1))
    put("later", (i[:, None] > i[None, :]))
    put("ones", 1.0)
    levels = [np.eye(P)]
    for level in range(LEVELS - 1):
        m = 1 << level
        same = (i[:, None] // (2 * m)) == (i[None, :] // (2 * m))
        levels.append(same & (i[:, None] % (2 * m) < m) & (i[None, :] % (2 * m) >= m))
    put("levels", np.concatenate(levels, 1))
    put("restart", (np.arange(S) % 64 != 0).astype(np.float32)[None])
    pos = np.arange(S, dtype=np.float32)
    rope = C_DIM // 4
    freq = (np.float32(500000.0) ** (-np.arange(0, rope, 2, dtype=np.float32) / np.float32(rope))).astype(np.float32)
    ang = pos[None, :] * freq[:, None]
    cos, sin = np.ones((C_DIM, S), np.float32), np.zeros((C_DIM, S), np.float32)
    for h in (0, rope // 2):
        cos[h:h + rope // 2], sin[h:h + rope // 2] = np.cos(ang), np.sin(ang)
    put("moba_cos", np.tile(cos, (2, 1)))
    put("moba_sin", np.tile(sin, (2, 1)))
    e = np.arange(0, B_ROPE, 2, dtype=np.float32) / np.float32(B_ROPE)
    inv = (np.float32(1.0) / np.float32(10000.0) ** e).astype(np.float32)
    put("inv_freq", np.tile(inv, P // len(inv))[:, None])
    return c


def unit_sizes(kind):
    return {"ffn": (SLOT, SLOT, SLOT), "hgrn": (SLOT, SLOT, D), "mla": (D, 4 * 384, SLOT),
            "branch": (SLOT, D, D)}[kind]


def stream(w):
    def cut(a, k0, nk, *cols):
        b = np.concatenate([a[k0 * P:(k0 + nk) * P, c:c + n] for c, n in cols], 1)
        return b.reshape(nk, P, -1).transpose(1, 0, 2).reshape(P, -1)

    def ffn(gate, up, at, down):
        for j in range(NFF + 1):
            if j < NFF:
                for k0 in (0, 4):
                    a = cut(gate, k0, 4, (j * FC, FC)).reshape(P, 4, FC)
                    b = cut(up, k0, 4, (j * FC + at, FC)).reshape(P, 4, FC)
                    yield np.concatenate([a, b], 2).reshape(P, -1)
            if j:
                yield cut(down, 2 * (j - 1), 2, (0, D))

    def close(a, blocks):
        for k in range(0, blocks, 2):
            yield cut(a, k, 2, (0, D))

    for layer in range(2):
        w_in, w_out = w["ffn_w_in"][layer], w["ffn_w_out"][layer]
        yield from ffn(w_in[0], w_in[0], DFF, w_out[0])
        if layer == 0:
            a = w["a_w_in"][0]
            for h in range(A_HEADS):
                yield cut(a, 0, KD, (h * P, P), (h * P + D, P))
                yield cut(a, 0, KD, (h * P + 2 * D, P), (h * P + 3 * D, P))
                yield cut(w["a_w_out"][0], h, 1, (0, D))
        else:
            for k0 in (0, 4):
                yield cut(w["b_w_dq"][0], k0, 4, (0, B_Q))
            for j in range(B_HEADS // 2):
                yield cut(w["kv_w_up"], 0, 2, (j * 512, 512))
                c = j * 384
                yield cut(w["b_w_uq"][0], 0, 4, (c, 128), (c + 192, 128), (c + 128, 64), (c + 320, 64))
                yield cut(w["b_w_out"][0], 2 * j, 2, (0, D))
        yield from ffn(w_in[1], w_in[1], DFF, w_out[1])
        yield from close(w["ple_w_gate"][layer], KD)
        yield from close(w["ple_w_in"][layer], 2)
        if layer == 0:
            yield cut(w["kv_w_down"], 0, KD, (0, B_KV))
            yield cut(w["kv_w_down"], 0, KD, (B_KV, B_ROPE), (B_KV, B_ROPE))
    for layer in range(2):
        a = w["w_in_2"][layer]
        for base, b in ((0, w["w_branch_sb_2"][layer]), (3 * C_WIDTH, w["w_branch_moba_2"][layer])):
            for j in range(C_HEADS // 2):
                c = base + j * P
                yield cut(a, 0, KD, (c, P), (c + C_WIDTH, P))
                yield cut(a, 0, KD, (c + 2 * C_WIDTH, P))
                yield cut(b, j, 1, (0, D))
        for c in range(4):
            for k0 in (0, 4):
                yield cut(a, k0, 4, (6 * C_WIDTH + c * 512, 512))
        yield from close(w["w_out_2"][layer], KD)
        yield from ffn(w["w_ffn_gate_2"][layer], w["w_ffn_up_2"][layer], 0, w["w_ffn_down_2"][layer])


class Stages:

    def __init__(self, setup, norm, ffn, hgrn, mla, ple, latent, final_norm, turn_residual, branch, merge,
                 layer_norm, finish):
        self.setup, self.norm, self.ffn, self.hgrn, self.mla = setup, norm, ffn, hgrn, mla
        self.ple, self.latent, self.final_norm, self.turn_residual = ple, latent, final_norm, turn_residual
        self.branch, self.merge, self.layer_norm, self.finish = branch, merge, layer_norm, finish


class Follow:

    def __init__(self, sems, **behind):
        self.sems, self.n, self.rate, self.i = sems, {k: -v for k, v in behind.items()}, None, None

    def __call__(self, name, k=1):
        self.n[name] = self.n.get(name, 0) + k
        if self.i is None:
            return self.sems.get(name), self.n[name]
        return self.sems.get(name), self.i * self.rate.get(name, 0) + self.n[name]

    @contextmanager
    def loop(self, engine, start, end, rate):
        before = dict(self.n)
        with engine.Fori(0, end - start) as i:
            self.i, self.rate = i, rate
            yield i + start
            self.i = None
        for name, n in self.n.items():
            assert n - before.get(name, 0) == rate.get(name, 0), (name, n, before, rate)
            self.n[name] = before.get(name, 0) + rate.get(name, 0) * (end - start)

    def repeat(self, engine, body, start, end, peel_last=False):
        before = dict(self.n)
        body(start)
        rate = {name: n - before.get(name, 0) for name, n in self.n.items()}
        stop = end - peel_last
        with self.loop(engine, start + 1, stop, rate) as i:
            body(i)
        if peel_last:
            body(end - 1)


SIGNALS = """
landed0 landed1 landed2 hi_ready lo_ready unit_done
const_landed gains_landed x_landed p_landed pos_landed norm_rows0_landed norm_rows1_landed norm_rows_used
out_ready out_landed gains_turned gains_ready bounds_in_ready bounds_exp angle_ready sin_ready zeros_ready
square_ready deviation_ready tokens_ready turned features_hi features_lo p_turned p_hi p_lo ple_gate_ready
gate_up_done silu_ready hidden_ready hidden_turned hidden_hi hidden_lo
kr_raw_ready kr_rotated kr_ready
sigmoids_ready ig_ready q_ready forget_ready log_ready decay_in_ready decay_ready
level_in_ready level_done level_merged cross_done cross_ready o_done o_dev_ready o_gated
kn_ready v_ready qn_ready qr_raw_ready qr_rotated qr_ready scores_done max_ready exp_ready
probs_ready probs_turned probsT0_ready probsT1_ready attn_done
qk_ready qk_roped z_done abs_ready softplus_ready keep_ready suffix_done weight_in_ready weight_exp weight_ready
branch_ready gate_ready gate_used dve_step act_step
""".split()


def build(nc, x, p, positions, norm_gains, a_lb_logits, a_out_gain, kv_norm_in, kv_latent_norm, b_q_norm,
          final_norm, ln_mix_g_2, ln_mix_b_2, ln_ffn_g_2, ln_ffn_b_2, weights, const, out, stop_after=None):
    ctx = ExitStack()
    with ctx:
        def sb(name, shape, dt=F32):
            return ctx.enter_context(nc.sbuf_tensor(name, shape, dt))

        raw = sb("raw", [P, RING, SLOT])
        w_hi = sb("w_hi", [P, RING, SLOT], F32R)
        w_lo = sb("w_lo", [P, RING, SLOT], F32R)
        res = sb("res", [P, TB, D])
        tok = sb("tok", [P, TB, D])
        fT_hi = sb("fT_hi", [P, KD, S], F32R)
        fT_lo = sb("fT_lo", [P, KD, S], F32R)
        hT_hi = sb("hT_hi", [P, 2, S], F32R)
        hT_lo = sb("hT_lo", [P, 2, S], F32R)
        pT_hi, pT_lo = hT_hi, hT_lo
        cT_hi = sb("cT_hi", [P, 2, S], F32R)
        cT_lo = sb("cT_lo", [P, 2, S], F32R)
        silu = sb("silu", [P, TB, FC])
        hid = sb("hid", [P, TB, FC])
        p_sb = sb("p_sb", [P, 2, TB, PLE])
        kc = sb("kc", [P, N_CONST])
        gain_rows = sb("gain_rows", [N_GAINS, P])
        gains = sb("gains", [P, N_GAINS])
        norm_g = sb("norm_g", [P, 2, D])
        norm_b = sb("norm_b", [P, 2, D])
        gate_sb = sb("gate_sb", [P, TB, D])
        stat = sb("stat", [P, 16])
        eps_sb = sb("eps_sb", [P, 4])
        bn = sb("bn", [P, TB, 2, 6])
        mv = sb("mv", [P, TB, 2])
        pos_i = sb("pos_i", [P, S], I32)
        mla_cos, mla_sin = sb("mla_cos", [P, S]), sb("mla_sin", [P, S])
        krz = sb("krz", [P, 2, S])
        q_sb, k_sb, f_sb = sb("q_sb", [P, 2, S]), sb("k_sb", [P, 2, S]), sb("f_sb", [P, 2, S])
        sg_sb, v_sb = sb("sg_sb", [P, TB, 2 * P]), sb("v_sb", [P, TB, 2 * P])
        lg_sb, b64, b256 = sb("lg_sb", [P, S]), sb("b64", [P, S]), sb("b256", [P, S])
        qr_sb = sb("qr_sb", [P, S])
        levels = sb("levels", [P, LEVELS, S])
        at_sb, cross = sb("at_sb", [P, TB, P]), sb("cross", [P, P])
        ang = levels[:, 0:4, :]
        kr_raw = qr_sb
        flat = levels[:, :, :].rearrange("p a n -> p (a n)")
        soft, keep = [flat[:, i * 2 * SEG:(i + 1) * 2 * SEG].rearrange("p (h n) -> p h n", h=2) for i in range(2)]
        gates4 = levels[:, :, :].rearrange("p a n -> p (a n)").rearrange("p (b n) -> p b n", b=4)
        rot1, rot2 = sb("rot1", [P, 2, S]), sb("rot2", [P, 2, S])
        kz, vz = sb("kz", [P, 2, S]), sb("vz", [P, TB, 2, P])
        sc, prob, probT = sb("sc", [P, 2, SEG]), sb("prob", [P, 2, SEG]), sb("probT", [P, 2, SEG])
        acc = ctx.enter_context(nc.psum_tensor("acc", [P, 4, 512], F32))
        wk = ctx.enter_context(nc.psum_tensor("wk", [P, 4, 512], F32))
        sems = {name: ctx.enter_context(nc.semaphore(name)) for name in SIGNALS}

        def kcol(name):
            at, w = CONST_AT[name]
            return kc[:, at:at + w]

        ident = kcol("identity")

        def gcol(name, n=0):
            c = GAIN_AT[name] + n
            return gains[:, c:c + 1]

        lower = sb("lower", [P, 4, A_HEADS])

        def tile2(a):
            return a.unsqueeze(1).to_broadcast([P, 2, a.shape[-1]])

        def network(e):
            e.setup()
            for layer in range(2):
                e.norm("norm_gains", (4 * layer) * KD)
                e.ffn(0)
                if stop_after == "ffn":
                    e.finish()
                    return
                e.norm("norm_gains", (4 * layer + 1) * KD)
                if layer == 0:
                    e.hgrn()
                    if stop_after == "hgrn":
                        e.finish()
                        return
                else:
                    e.mla()
                    if stop_after == "mla":
                        e.finish()
                        return
                e.norm("norm_gains", (4 * layer + 2) * KD)
                e.ffn(0)
                e.norm("norm_gains", (4 * layer + 3) * KD)
                e.ple(layer)
                if stop_after == "ple":
                    e.finish()
                    return
                if layer == 0:
                    e.norm("kv_norm_in", 0)
                    e.latent()
            e.final_norm()
            for layer in range(2):
                e.turn_residual()
                e.branch("sb", layer)
                if stop_after == "sb":
                    e.finish()
                    return
                e.branch("moba", layer)
                if stop_after == "moba":
                    e.finish()
                    return
                e.merge(layer)
                e.layer_norm(2 * layer)
                e.turn_residual()
                e.ffn(1, last=layer == 1)
                e.layer_norm(2 * layer + 1)
            e.finish()

        n_units = [0]

        block = ctx.enter_context(nc.Block())

        @block.sync
        def _(sp):
            at = Follow(sems, lo_ready=RING)

            def unit(n):
                slot = at.n.get("unit", 0) % RING
                at.n["unit"] = at.n.get("unit", 0) + 1
                sem, value = at("lo_ready")
                if at.i is not None or value > 0:
                    sp.wait_ge(sem, value)
                start = at("floats", P * n)[1] - P * n
                sp.dma_start(raw[:, slot, 0:n], weights[bass.ds(start, P * n)].rearrange("(p n) -> p n", p=P))\
                    .then_inc(sems[f"landed{slot}"], 16)

            def rounds(kind, start, end):
                def body(_):
                    for n in unit_sizes(kind):
                        unit(n)
                at.repeat(sp, body, start, end)

            def setup():
                sp.dma_start(kc[:, :], const).then_inc(sems["const_landed"], 16)
                sp.dma_start(res[:, :, :], x[0].rearrange("(t p) d -> p t d", p=P)).then_inc(sems["x_landed"], 16)
                views = {"norm_gains": norm_gains.rearrange("l i (k d) -> (l i k) d", d=P),
                         "kv_norm_in": kv_norm_in.rearrange("(k d) -> k d", d=P),
                         "kv_latent_norm": kv_latent_norm.rearrange("(k d) -> k d", d=P),
                         "b_q_norm": b_q_norm.rearrange("o (k d) -> (o k) d", d=P),
                         "a_out_gain": a_out_gain, "a_lb_logits": a_lb_logits.rearrange("l (k d) -> (l k) d", d=P)}
                for name, n in GAIN_ROWS:
                    r = GAIN_AT[name]
                    sp.dma_start(gain_rows[r:r + n, :], views[name]).then_inc(sems["gains_landed"], 16)
                sp.dma_start(pos_i[:, :], positions.to_broadcast([P, S])).then_inc(sems["pos_landed"], 16)
                for layer in range(2):
                    sp.dma_start(p_sb[:, layer, :, :], p[layer, 0].rearrange("(t p) d -> p t d", p=P))\
                        .then_inc(sems["p_landed"], 16)

            def norm_row(n):
                g, b = [(final_norm, None), (ln_mix_g_2[0], ln_mix_b_2[0]), (ln_ffn_g_2[0], ln_ffn_b_2[0]),
                        (ln_mix_g_2[1], ln_mix_b_2[1]), (ln_ffn_g_2[1], ln_ffn_b_2[1])][n]
                if n >= 2:
                    sp.wait_ge(*at("norm_rows_used"))
                for dst, src in ((norm_g, g), (norm_b, b if b is not None else g)):
                    sp.dma_start(dst[:, n % 2, :], src.rearrange("(o d) -> o d", o=1).to_broadcast([P, D]))\
                        .then_inc(sems[f"norm_rows{n % 2}_landed"], 16)

            def ffn(second, last=False):
                unit(SLOT)
                unit(SLOT)
                rounds("ffn", 1, NFF)
                unit(SLOT)

            def hgrn():
                rounds("hgrn", 0, A_HEADS)

            def ple(layer):
                for _ in range(5):
                    unit(SLOT)

            def latent():
                unit(SLOT)
                unit(KD * P)

            def mla():
                unit(SLOT)
                unit(SLOT)
                rounds("mla", 0, B_HEADS // 2)
                norm_row(0)
                norm_row(1)

            def branch(kind, layer):
                rounds("branch", 0, C_HEADS // 2)
                if kind == "sb" and layer == 1:
                    norm_row(3)

            def merge(layer):
                for _ in range(12):
                    unit(SLOT)
                norm_row(2 * layer + 2)

            def finish():
                if stop_after:
                    for _ in range(3):
                        unit(SLOT)
                n_units[0] = at.n["unit"]
                sp.wait_ge(*at("out_ready"))
                sp.dma_start(out[0].rearrange("(t p) d -> p t d", p=P), res[:, :, :]).then_inc(sems["out_landed"], 16)
                sp.wait_ge(*at("out_landed", 16))

            none = lambda *a: None
            network(Stages(setup=setup, norm=none, ffn=ffn, hgrn=hgrn, mla=mla, ple=ple, latent=latent,
                                    final_norm=none, turn_residual=none, branch=branch, merge=merge,
                                    layer_norm=none, finish=finish))

        @block.tensor
        def _(pe):
            at = Follow(sems)

            def next_unit():
                slot = at.n.get("unit", 0) % RING
                at.n["unit"] = at.n.get("unit", 0) + 1
                pe.wait_ge(*at("hi_ready"))
                pe.wait_ge(*at("lo_ready"))
                return slot

            def product(o, lhs, rhs, start, stop):
                nc.tensor.matmul(o, lhs[0], rhs[0], start=start, stop=False, skip_group_check=True)
                nc.tensor.matmul(o, lhs[0], rhs[1], start=False, stop=False, skip_group_check=True)
                return nc.tensor.matmul(o, lhs[1], rhs[0], start=False, stop=stop, skip_group_check=True)

            def whole(o, lhs, rhs, start, stop):
                return nc.tensor.matmul(o, lhs, rhs, start=start, stop=stop, skip_group_check=True)

            def wt(slot, shape):
                k, n = shape
                return [t[:, slot, 0:k * n].rearrange("p (k n) -> p k n", k=k) for t in (w_hi, w_lo)]

            def done(ins):
                ins.then_inc(sems["unit_done"], 1)

            def setup():
                pe.wait_ge(*at("const_landed", 16))
                pe.wait_ge(*at("gains_landed", 16 * len(GAIN_ROWS)))
                nc.tensor.transpose(wk[:, 0, 0:N_GAINS], gain_rows[:, :], ident[0:N_GAINS, 0:N_GAINS])\
                    .then_inc(sems["gains_turned"], 1)
                pe.wait_ge(*at("gains_ready"))

            def turn(src, nf, banks, n_ready=2):
                pe.wait_ge(*at("tokens_ready", n_ready))
                for b in range(nf // 2):
                    for f in range(2):
                        for tb in range(TB):
                            c = (2 * b + f) * P
                            last = nc.tensor.transpose(wk[:, banks[b], f * S + tb * P:f * S + (tb + 1) * P],
                                                       src[:, tb, c:c + P], ident)
                    last.then_inc(sems["turned"], 1)
                pe.wait_ge(*at("features_hi", nf // 2))
                pe.wait_ge(*at("features_lo", nf // 2))

            def norm(name, n):
                turn(tok, KD, (0, 1, 2, 3))

            def turn_residual():
                turn(res, KD, (0, 1, 2, 3))

            def close(nk, first):
                slot = next_unit()
                w = wt(slot, (nk, D))
                for k in range(nk):
                    for tb in range(TB):
                        lhs = [t[:, k, tb * P:(tb + 1) * P] for t in (hT_hi, hT_lo)]
                        for half in range(2):
                            last = product(acc[:, 2 * tb + half, :], lhs,
                                           [t[:, k, half * 512:(half + 1) * 512] for t in w],
                                           start=first and k == 0, stop=True)
                done(last)

            def ffn(second, last=False):
                def half(k0):
                    slot = next_unit()
                    w = wt(slot, (4, 2 * FC))
                    for tb in range(TB):
                        for k in range(4):
                            ins = product(wk[:, tb, :], [t[:, k0 + k, tb * P:(tb + 1) * P] for t in (fT_hi, fT_lo)],
                                          [t[:, k, :] for t in w], start=k0 + k == 0, stop=k0 + k == KD - 1)
                        if tb:
                            done(ins)
                        elif k0:
                            ins.then_inc(sems["gate_up_done"], 1)

                def turn_hidden():
                    for f in range(2):
                        for tb in range(TB):
                            last = nc.tensor.transpose(wk[:, 2, f * S + tb * P:f * S + (tb + 1) * P],
                                                       hid[:, tb, f * P:(f + 1) * P], ident)
                    last.then_inc(sems["hidden_turned"], 1)

                def down(first):
                    pe.wait_ge(*at("hidden_hi"))
                    pe.wait_ge(*at("hidden_lo"))
                    close(2, first)

                def body(j):
                    pe.wait_ge(*at("hidden_ready", 2))
                    half(0)
                    turn_hidden()
                    half(4)
                    down(isinstance(j, int) and j == 1)

                half(0)
                half(4)
                at.repeat(pe, body, 1, NFF)
                pe.wait_ge(*at("hidden_ready", 2))
                turn_hidden()
                pe.wait_ge(*at("hidden_hi"))
                pe.wait_ge(*at("hidden_lo"))
                close(2, False)

            def hgrn():
                def body(h):
                    w = wt(next_unit(), (KD, 2 * P))
                    for c in range(2):
                        for k in range(KD):
                            last = product(wk[:, 0, c * S:(c + 1) * S], [t[:, k, c * P:(c + 1) * P] for t in w],
                                           [t[:, k, :] for t in (fT_hi, fT_lo)], start=k == 0, stop=k == KD - 1)
                    done(last)
                    w = wt(next_unit(), (KD, 2 * P))
                    for tb in range(TB):
                        for k in range(KD):
                            last = product(wk[:, 1, tb * S:(tb + 1) * S],
                                           [t[:, k, tb * P:(tb + 1) * P] for t in (fT_hi, fT_lo)],
                                           [t[:, k, :] for t in w], start=k == 0, stop=k == KD - 1)
                    done(last)
                    pe.wait_ge(*at("level_in_ready"))
                    for r in range(4):
                        if r >= 2:
                            pe.wait_ge(*at("level_merged"))
                        for i in range(2):
                            n = 2 * r + i
                            for tb in range(TB):
                                c = slice(tb * P, (tb + 1) * P)
                                a, b = (k_sb[:, 0, c], q_sb[:, 0, c]) if n == 0 else \
                                    (levels[:, n - 1, c], levels[:, n - 1, c])
                                last = whole(wk[:, 2 + r % 2, (2 * i + tb) * P:(2 * i + tb + 1) * P], a, b, True, True)
                        last.then_inc(sems["level_done"], 1)
                    pe.wait_ge(*at("level_merged"))
                    whole(wk[:, 2, 0:P], levels[:, 7, 0:P], levels[:, 7, P:S], True, True)\
                        .then_inc(sems["cross_done"], 1)
                    pe.wait_ge(*at("level_merged"))
                    pe.wait_ge(*at("ig_ready"))
                    whole(wk[:, 3, 0:P], at_sb[:, 0, :], v_sb[:, 0, 0:P], True, True)
                    whole(wk[:, 3, P:2 * P], at_sb[:, 1, :], v_sb[:, 1, 0:P], True, False)
                    pe.wait_ge(*at("cross_ready"))
                    whole(wk[:, 3, P:2 * P], cross[:, :], v_sb[:, 0, 0:P], False, True).then_inc(sems["o_done"], 1)
                    pe.wait_ge(*at("o_gated", 2))
                    for tb in range(TB):
                        last = nc.tensor.transpose(wk[:, 2, tb * P:(tb + 1) * P], hid[:, tb, 0:P], ident)
                    last.then_inc(sems["hidden_turned"], 1)
                    pe.wait_ge(*at("hidden_hi"))
                    pe.wait_ge(*at("hidden_lo"))
                    close(1, isinstance(h, int) and h == 0)

                at.repeat(pe, body, 0, A_HEADS)

            def ple(layer):
                if layer == 0:
                    pe.wait_ge(*at("p_landed", 32))
                for f in range(2):
                    for tb in range(TB):
                        last = nc.tensor.transpose(wk[:, 2, f * S + tb * P:f * S + (tb + 1) * P],
                                                   p_sb[:, layer, tb, f * P:(f + 1) * P], ident)
                last.then_inc(sems["p_turned"], 1)
                for c in range(4):
                    w = wt(next_unit(), (2, D))
                    for k in range(2):
                        for tb in range(TB):
                            for half in range(2):
                                last = product(acc[:, 2 * tb + half, :],
                                               [t[:, 2 * c + k, tb * P:(tb + 1) * P] for t in (fT_hi, fT_lo)],
                                               [t[:, k, half * 512:(half + 1) * 512] for t in w],
                                               start=c + k == 0, stop=c == 3 and k == 1)
                    done(last)
                pe.wait_ge(*at("p_hi"))
                pe.wait_ge(*at("p_lo"))
                w = wt(next_unit(), (2, D))
                for k in range(2):
                    for tb in range(TB):
                        for half in range(2):
                            last = product(wk[:, 2 * tb + half, :],
                                           [t[:, k, tb * P:(tb + 1) * P] for t in (pT_hi, pT_lo)],
                                           [t[:, k, half * 512:(half + 1) * 512] for t in w],
                                           start=k == 0, stop=k == 1)
                done(last)

            def latent():
                w = wt(next_unit(), (KD, B_KV))
                for tb in range(TB):
                    for k in range(KD):
                        last = product(wk[:, 0, tb * S:(tb + 1) * S],
                                       [t[:, k, tb * P:(tb + 1) * P] for t in (fT_hi, fT_lo)],
                                       [t[:, k, :] for t in w], start=k == 0, stop=k == KD - 1)
                done(last)
                w = wt(next_unit(), (KD, P))
                for k in range(KD):
                    last = product(wk[:, 1, 0:S], [t[:, k, :] for t in w],
                                   [t[:, k, :] for t in (fT_hi, fT_lo)], start=k == 0, stop=k == KD - 1)
                done(last)
                pe.wait_ge(*at("kr_raw_ready"))
                whole(wk[:, 1, S:2 * S], kcol("rotate_mla"), kr_raw[:, :], True, True).then_inc(sems["kr_rotated"], 1)
                turn(tok, 2, (2,))
                pe.wait_ge(*at("kr_ready"))

            def softmax_turn():
                pe.wait_ge(*at("probs_ready", 4))
                for h in range(2):
                    for dst, src in ((0, 0), (P, P), (2 * P, 2 * P)):
                        last = nc.tensor.transpose(wk[:, 2 + h, dst:dst + P], prob[:, h, src:src + P], ident)
                    last.then_inc(sems["probs_turned"], 1)
                pe.wait_ge(*at("probsT0_ready"))
                pe.wait_ge(*at("probsT1_ready"))

            def mla():
                for k0 in (0, 4):
                    w = wt(next_unit(), (4, B_Q))
                    for tb in range(TB):
                        for k in range(4):
                            last = product(wk[:, tb, :], [t[:, k0 + k, tb * P:(tb + 1) * P] for t in (fT_hi, fT_lo)],
                                           [t[:, k, :] for t in w], start=k0 + k == 0, stop=k0 + k == KD - 1)
                    done(last)
                turn(tok, 4, (2, 3))

                def body(j):
                    w = wt(next_unit(), (2, 512))
                    cT = (cT_hi, cT_lo)
                    for h in range(2):
                        for k in range(2):
                            product(wk[:, 0, h * S:(h + 1) * S], [t[:, k, h * 256:h * 256 + P] for t in w],
                                    [t[:, k, :] for t in cT], start=k == 0, stop=k == 1)
                    vw = [t.rearrange("p k (h n) -> p k h n", h=2)[:, :, :, P:2 * P] for t in w]
                    for tb in range(TB):
                        for k in range(2):
                            last = product(wk[:, 1, tb * S:(tb + 1) * S], [t[:, k, tb * P:(tb + 1) * P] for t in cT],
                                           [t[:, k] for t in vw], start=k == 0, stop=k == 1)
                    done(last)
                    w = wt(next_unit(), (4, 384))
                    for h in range(2):
                        for k in range(4):
                            product(wk[:, 2, h * S:(h + 1) * S], [t[:, k, h * P:(h + 1) * P] for t in w],
                                    [t[:, k, :] for t in (fT_hi, fT_lo)], start=k == 0, stop=k == 3)
                    for k in range(4):
                        last = product(wk[:, 3, 0:S], [t[:, k, 2 * P:3 * P] for t in w], [t[:, k, :] for t in (fT_hi, fT_lo)],
                                       start=k == 0, stop=k == 3)
                    done(last)
                    pe.wait_ge(*at("qr_raw_ready"))
                    whole(wk[:, 3, S:2 * S], kcol("rotate_mla"), qr_sb[:, :], True, True)\
                        .then_inc(sems["qr_rotated"], 1)
                    pe.wait_ge(*at("kn_ready"))
                    pe.wait_ge(*at("v_ready"))
                    pe.wait_ge(*at("qn_ready"))
                    pe.wait_ge(*at("qr_ready"))
                    for h in range(2):
                        for tb in range(TB):
                            nk = (tb + 1) * P
                            o = wk[:, h, tb * P:tb * P + nk]
                            whole(o, q_sb[:, h, tb * P:(tb + 1) * P], k_sb[:, h, 0:nk], True, False)
                            last = whole(o, rot2[:, 0, tb * P:(tb + 1) * P], krz[:, h, 0:nk], False, True)
                    last.then_inc(sems["scores_done"], 1)
                    softmax_turn()
                    for h in range(2):
                        whole(wk[:, 0, h * S:(h + 1) * S], v_sb[:, 0, h * P:(h + 1) * P], probT[:, h, 0:S], True, False)
                        last = whole(wk[:, 0, h * S + P:(h + 1) * S], v_sb[:, 1, h * P:(h + 1) * P],
                                     probT[:, h, S:SEG], False, True)
                    last.then_inc(sems["attn_done"], 1)
                    pe.wait_ge(*at("hidden_hi"))
                    pe.wait_ge(*at("hidden_lo"))
                    close(2, isinstance(j, int) and j == 0)

                at.repeat(pe, body, 0, B_HEADS // 2)

            def branch(kind, layer):
                def qkv():
                    w = wt(next_unit(), (KD, 2 * P))
                    for c in range(2):
                        for k in range(KD):
                            last = product(wk[:, 0, c * S:(c + 1) * S], [t[:, k, c * P:(c + 1) * P] for t in w],
                                           [t[:, k, :] for t in (fT_hi, fT_lo)], start=k == 0, stop=k == KD - 1)
                    done(last)
                    w = wt(next_unit(), (KD, P))
                    for tb in range(TB):
                        for k in range(KD):
                            last = product(wk[:, 1, tb * P:(tb + 1) * P],
                                           [t[:, k, tb * P:(tb + 1) * P] for t in (fT_hi, fT_lo)],
                                           [t[:, k, :] for t in w], start=k == 0, stop=k == KD - 1)
                    done(last)

                def values(bank, weights):
                    for h in range(2):
                        whole(wk[:, bank, 0:S], vz[:, 0, h, :], weights[:, h, 0:S], h == 0, False)
                        last = whole(wk[:, bank, P:S], vz[:, 1, h, :], weights[:, h, S:SEG], False, h == 1)
                    last.then_inc(sems["attn_done"], 1)
                    pe.wait_ge(*at("hidden_hi"))
                    pe.wait_ge(*at("hidden_lo"))

                def body_sb(j):
                    qkv()
                    pe.wait_ge(*at("qk_ready", 3))
                    pe.wait_ge(*at("v_ready", 2))
                    for h in range(2):
                        whole(wk[:, 2 + h, 0:S], kz[:, h, 0:P], q_sb[:, 0, :], True, True)
                        last = whole(wk[:, 2 + h, S:SEG], kz[:, h, P:S], q_sb[:, 0, P:S], True, True)
                    last.then_inc(sems["z_done"], 1)
                    pe.wait_ge(*at("keep_ready"))
                    for h in range(2):
                        whole(wk[:, h, 0:S], kcol("later"), keep[:, h, 0:S], True, False)
                        whole(wk[:, h, P:S], kcol("ones")[:, 0:P], keep[:, h, S:SEG], False, True)
                        last = whole(wk[:, h, S:SEG], kcol("later"), keep[:, h, S:SEG], True, True)
                    last.then_inc(sems["suffix_done"], 1)
                    pe.wait_ge(*at("weight_ready"))
                    values(2, probT)
                    close(1, isinstance(j, int) and j == 0)

                def body_moba(j):
                    qkv()
                    pe.wait_ge(*at("qr_raw_ready"))
                    whole(wk[:, 2, :].rearrange("p (a n) -> p a n", a=2), kcol("rotate_moba"), rot1[:, :, :], True, True).then_inc(sems["qr_rotated"], 1)
                    pe.wait_ge(*at("qk_roped", 3))
                    pe.wait_ge(*at("v_ready", 2))
                    for h in range(2):
                        for tb in range(TB):
                            nk = (tb + 1) * P
                            last = whole(wk[:, h, tb * P:tb * P + nk], q_sb[:, 0, tb * P:(tb + 1) * P],
                                         kz[:, h, 0:nk], True, True)
                    last.then_inc(sems["scores_done"], 1)
                    softmax_turn()
                    values(0, probT)
                    close(1, isinstance(j, int) and j == 0)

                if kind == "moba":
                    pe.wait_ge(*at("branch_ready", 4))
                at.repeat(pe, body_sb if kind == "sb" else body_moba, 0, C_HEADS // 2)

            def merge(layer):
                for q in range(4):
                    bank = 2 * (q % 2)
                    if q >= 2:
                        pe.wait_ge(*at("gate_ready", 2))
                    for k0 in (0, 4):
                        w = wt(next_unit(), (4, 512))
                        for tb in range(TB):
                            for k in range(4):
                                last = product(wk[:, bank + tb, :],
                                               [t[:, k0 + k, tb * P:(tb + 1) * P] for t in (fT_hi, fT_lo)],
                                               [t[:, k, :] for t in w], start=k0 + k == 0, stop=k0 + k == KD - 1)
                        done(last)
                pe.wait_ge(*at("gate_ready", 4))
                turn(tok, KD, (0, 1, 2, 3))
                for c in range(4):
                    w = wt(next_unit(), (2, D))
                    for k in range(2):
                        for tb in range(TB):
                            for half in range(2):
                                last = product(acc[:, 2 * tb + half, :],
                                               [t[:, 2 * c + k, tb * P:(tb + 1) * P] for t in (fT_hi, fT_lo)],
                                               [t[:, k, half * 512:(half + 1) * 512] for t in w],
                                               start=c + k == 0, stop=c == 3 and k == 1)
                    done(last)

            none = lambda *a: None
            network(Stages(setup=setup, norm=norm, ffn=ffn, hgrn=hgrn, mla=mla, ple=ple, latent=latent,
                                    final_norm=none, turn_residual=turn_residual, branch=branch, merge=merge,
                                    layer_norm=none, finish=none))

        @block.scalar
        def _(act):
            at = Follow(sems)
            total = n_units[0]

            def seq(ins):
                ins.then_inc(sems["act_step"], 1)
                act.wait_ge(*at("act_step"))

            def split():
                n = at.n.get("unit", 0)
                if n >= total:
                    return
                at.n["unit"] = n + 1
                slot = n % RING
                act.wait_ge(*at(f"landed{slot}", 16))
                act.copy(w_hi[:, slot, :], raw[:, slot, :]).then_inc(sems["hi_ready"], 1)

            def unit_done():
                act.wait_ge(*at("unit_done"))

            def upper(dst, src, scale=None):
                if scale is None:
                    return act.copy(dst, src)
                return act.activation(dst, src, ACT.Copy, scale=scale)

            def setup():
                for _ in range(RING):
                    split()
                act.wait_ge(*at("gains_turned"))
                act.copy(gains[:, :], wk[:, 0, 0:N_GAINS]).then_inc(sems["gains_ready"], 1)
                act.wait_ge(*at("bounds_in_ready"))
                act.activation(lower[:, 0:2, :], lower[:, 0:2, :], ACT.Exp).then_inc(sems["bounds_exp"], 1)
                act.wait_ge(*at("angle_ready"))
                act.activation(mla_sin[:, :], ang[:, 2, :], ACT.Sin).then_inc(sems["sin_ready"], 1)
                act.activation(mla_cos[:, :], ang[:, 3, :], ACT.Sin).then_inc(sems["sin_ready"], 1)

            def deviation(n, eps):
                act.wait_ge(*at("square_ready"))
                act.activation(stat[:, 2:2 + n], stat[:, 0:n], ACT.Sqrt, bias=eps_sb[:, eps:eps + 1])\
                    .then_inc(sems["deviation_ready"], 1)

            def turn(nf, banks, hi, name=None, c0=0):
                for b in range(nf // 2):
                    act.wait_ge(*at("turned"))
                    if name is None:
                        act.copy(hi[:, 2 * b:2 * b + 2, :], wk[:, banks[b], :].rearrange("p (f n) -> p f n", f=2))\
                            .then_inc(sems["features_hi"], 1)
                        continue
                    for f in range(2):
                        last = upper(hi[:, 2 * b + f, :], wk[:, banks[b], f * S:(f + 1) * S],
                                     gcol(name, c0 + 2 * b + f))
                    last.then_inc(sems["features_hi"], 1)

            def norm(name, c0):
                deviation(TB, 0)
                turn(KD, (0, 1, 2, 3), fT_hi, name, c0)

            def turn_residual():
                turn(KD, (0, 1, 2, 3), fT_hi)

            def layer_norm(n):
                deviation(TB, 1)

            def final_norm():
                deviation(TB, 0)

            def hidden(src, nk=2, scale=None):
                upper(hT_hi[:, 0:nk, :], src.rearrange("p (f n) -> p f n", f=nk), scale)\
                    .then_inc(sems["hidden_hi"], 1)

            def ffn(second, last=False):
                def gate():
                    act.wait_ge(*at("gate_up_done"))
                    act.activation(silu[:, 0, :], wk[:, 0, 0:FC], ACT.Silu).then_inc(sems["silu_ready"], 1)
                    unit_done()
                    act.activation(silu[:, 1, :], wk[:, 1, 0:FC], ACT.Silu).then_inc(sems["silu_ready"], 1)
                    split()

                def body(j):
                    unit_done()
                    act.wait_ge(*at("hidden_turned"))
                    hidden(wk[:, 2, :])
                    split()
                    gate()
                    unit_done()
                    split()

                unit_done()
                split()
                gate()
                at.repeat(act, body, 1, NFF, peel_last=last)
                act.wait_ge(*at("hidden_turned"))
                hidden(wk[:, 2, :])
                unit_done()
                split()

            def hgrn():
                def body(h):
                    unit_done()
                    act.activation(f_sb[:, 0, :], wk[:, 0, S:2 * S], ACT.Sigmoid).then_inc(sems["sigmoids_ready"], 1)
                    act.activation(f_sb[:, 1, :], wk[:, 0, S:2 * S], ACT.Sigmoid, scale=-1.0)\
                        .then_inc(sems["sigmoids_ready"], 1)
                    act.activation(q_sb[:, 0, :], wk[:, 0, 0:S], ACT.Copy, scale=A_DIM ** -0.5)\
                        .then_inc(sems["q_ready"], 1)
                    split()
                    unit_done()
                    act.activation(sg_sb[:, :, 0:P], wk[:, 1, :].rearrange("p (t n) -> p t n", t=TB)[:, :, P:2 * P],
                                   ACT.Sigmoid)
                    act.copy(v_sb[:, :, 0:P], wk[:, 1, :].rearrange("p (t n) -> p t n", t=TB)[:, :, 0:P])\
                        .then_inc(sems["ig_ready"], 1)
                    split()
                    act.wait_ge(*at("forget_ready"))
                    act.activation(lg_sb[:, :], f_sb[:, 0, :], ACT.Ln).then_inc(sems["log_ready"], 1)
                    act.wait_ge(*at("decay_in_ready"))
                    act.activation(levels[:, :, :], levels[:, :, :], ACT.Exp).then_inc(sems["decay_ready"], 1)
                    act.wait_ge(*at("cross_done"))
                    act.copy(cross[:, :], wk[:, 2, 0:P]).then_inc(sems["cross_ready"], 1)
                    act.wait_ge(*at("o_done"))
                    for tb in range(TB):
                        seq(act.activation(rot1[:, tb, 0:P], wk[:, 3, tb * P:(tb + 1) * P], ACT.Square,
                                           scale=A_DIM ** -0.5, accum_out=stat[:, tb:tb + 1]))
                    act.activation(stat[:, 2:4], stat[:, 0:2], ACT.Sqrt, bias=eps_sb[:, 0:1])\
                        .then_inc(sems["o_dev_ready"], 1)
                    act.wait_ge(*at("hidden_turned"))
                    hidden(wk[:, 2, 0:S], 1, gcol("a_out_gain"))
                    unit_done()
                    split()

                at.repeat(act, body, 0, A_HEADS)

            def ple(layer):
                act.wait_ge(*at("p_turned"))
                act.copy(pT_hi[:, :, :], wk[:, 2, :].rearrange("p (f n) -> p f n", f=2)).then_inc(sems["p_hi"], 1)
                for c in range(4):
                    unit_done()
                    if c == 3:
                        for b in range(4):
                            act.activation(gate_sb[:, b // 2, (b % 2) * 512:(b % 2 + 1) * 512], acc[:, b, :],
                                           ACT.Sigmoid).then_inc(sems["ple_gate_ready"], 1)
                    split()
                unit_done()
                split()

            def latent():
                unit_done()
                split()
                unit_done()
                act.copy(kr_raw[:, :], wk[:, 1, 0:S]).then_inc(sems["kr_raw_ready"], 1)
                deviation(TB, 0)
                split()
                turn(2, (2,), cT_hi, "kv_latent_norm")

            def softmax(scale):
                act.wait_ge(*at("max_ready"))
                for h in range(2):
                    for seg, (a, b) in enumerate(((0, P), (P, SEG))):
                        c = 2 * seg + h
                        last = act.activation(prob[:, h, a:b], sc[:, h, a:b], ACT.Exp, bias=stat[:, 4 + c:5 + c],
                                              scale=scale, accum_out=stat[:, 8 + c:9 + c])
                last.then_inc(sems["exp_ready"], 1)
                act.wait_ge(*at("probs_turned"))
                act.copy(probT[:, 0, :], wk[:, 2, 0:SEG]).then_inc(sems["probsT0_ready"], 1)
                at("probs_turned")

            def mla():
                unit_done()
                split()
                unit_done()
                deviation(TB, 0)
                split()
                turn(4, (2, 3), fT_hi, "b_q_norm")

                def body(j):
                    unit_done()
                    act.copy(k_sb[:, :, :], wk[:, 0, :].rearrange("p (h n) -> p h n", h=2))\
                        .then_inc(sems["kn_ready"], 1)
                    split()
                    unit_done()
                    act.copy(qr_sb[:, :], wk[:, 3, 0:S]).then_inc(sems["qr_raw_ready"], 1)
                    act.copy(q_sb[:, :, :], wk[:, 2, :].rearrange("p (h n) -> p h n", h=2))\
                        .then_inc(sems["qn_ready"], 1)
                    split()
                    softmax((B_NOPE + B_ROPE) ** -0.5)
                    act.wait_ge(*at("attn_done"))
                    hidden(wk[:, 0, :])
                    unit_done()
                    split()

                at.repeat(act, body, 0, B_HEADS // 2)

            def branch(kind, layer):
                scale = C_DIM ** -0.5

                def body_sb(j):
                    unit_done()
                    act.copy(q_sb[:, 0, :], wk[:, 0, 0:S]).then_inc(sems["qk_ready"], 1)
                    for h in range(2):
                        r = slice(h * C_DIM, (h + 1) * C_DIM)
                        act.copy(kz[r, h, :], wk[r, 0, S:2 * S]).then_inc(sems["qk_ready"], 1)
                    split()
                    unit_done()
                    split()
                    act.wait_ge(*at("z_done"))
                    act.activation(sc[:, :, :], wk[:, 2:4, 0:SEG], ACT.Abs).then_inc(sems["abs_ready"], 1)
                    act.wait_ge(*at("abs_ready"))
                    seq(act.activation(sc[:, :, :], sc[:, :, :], ACT.Exp, scale=-scale))
                    act.activation(soft[:, :, :], sc[:, :, :], ACT.Ln, bias=1.0).then_inc(sems["softplus_ready"], 1)
                    act.wait_ge(*at("weight_in_ready"))
                    act.activation(soft[:, :, :], sc[:, :, :], ACT.Exp).then_inc(sems["weight_exp"], 1)
                    act.wait_ge(*at("attn_done"))
                    hidden(wk[:, 2, 0:S], 1)
                    unit_done()
                    split()

                def body_moba(j):
                    unit_done()
                    act.copy(rot1[:, :, :], wk[:, 0, :].rearrange("p (a n) -> p a n", a=2))\
                        .then_inc(sems["qr_raw_ready"], 1)
                    split()
                    unit_done()
                    split()
                    softmax(scale)
                    act.wait_ge(*at("attn_done"))
                    hidden(wk[:, 0, 0:S], 1)
                    unit_done()
                    split()

                if kind == "sb" and layer == 0:
                    act.wait_ge(*at("zeros_ready", 3))
                at.repeat(act, body_sb if kind == "sb" else body_moba, 0, C_HEADS // 2)
                if kind == "sb":
                    for b in range(4):
                        act.copy(gate_sb[:, b // 2, (b % 2) * 512:(b % 2 + 1) * 512], acc[:, b, :])\
                            .then_inc(sems["branch_ready"], 1)

            def merge(layer):
                for q in range(4):
                    unit_done()
                    split()
                    unit_done()
                    if q >= 2:
                        act.wait_ge(*at("gate_used", 2))
                    for tb in range(TB):
                        act.activation(gates4[:, 2 * (q % 2) + tb, :], wk[:, 2 * (q % 2) + tb, :], ACT.Sigmoid)\
                            .then_inc(sems["gate_ready"], 1)
                    split()
                at("gate_used", 4)
                turn(KD, (0, 1, 2, 3), fT_hi)
                for _ in range(4):
                    unit_done()
                    split()

            none = lambda *a: None
            network(Stages(setup=setup, norm=norm, ffn=ffn, hgrn=hgrn, mla=mla, ple=ple, latent=latent,
                                    final_norm=final_norm, turn_residual=turn_residual, branch=branch,
                                    merge=merge, layer_norm=layer_norm, finish=none))

        @block.gpsimd
        def _(pool):
            for t in (kz, vz, krz):
                pool.memset(t[:], 0.0).then_inc(sems["zeros_ready"], 1)

        @block.vector
        def _(dve):
            at = Follow(sems)
            total = n_units[0]

            def seq(ins):
                ins.then_inc(sems["dve_step"], 1)
                dve.wait_ge(*at("dve_step"))

            def split():
                n = at.n.get("unit", 0)
                if n >= total:
                    return
                at.n["unit"] = n + 1
                slot = n % RING
                dve.wait_ge(*at("hi_ready"))
                dve.tensor_tensor(w_lo[:, slot, :], raw[:, slot, :], w_hi[:, slot, :].bitcast(F32), ALU.subtract)\
                    .then_inc(sems["lo_ready"], 1)

            def unit_done():
                dve.wait_ge(*at("unit_done"))

            def lower_part(lo, src, hi, scale=None):
                hi = hi.bitcast(F32)
                if scale is None:
                    return dve.tensor_tensor(lo, src, hi, ALU.subtract)
                return dve.scalar_tensor_tensor(lo, src, scale, hi, ALU.mult, ALU.subtract)

            def setup():
                dve.memset(eps_sb[:, 0:1], EPS)
                dve.memset(eps_sb[:, 1:2], LN_EPS)
                dve.memset(eps_sb[:, 2:3], 1.0)
                dve.memset(eps_sb[:, 3:4], 0.0).then_inc(sems["dve_step"], 1)
                dve.wait_ge(*at("dve_step"))
                for _ in range(RING):
                    split()
                dve.wait_ge(*at("gains_ready"))
                c = GAIN_AT["a_lb_logits"]
                l0, l1 = gains[:, c:c + 8], gains[:, c + 8:c + 16]
                seq(dve.tensor_tensor(lower[:, 2, :], l0, l1, ALU.max))
                dve.tensor_tensor(lower[:, 0, :], l0, lower[:, 2, :], ALU.subtract)
                dve.tensor_tensor(lower[:, 1, :], l1, lower[:, 2, :], ALU.subtract)\
                    .then_inc(sems["bounds_in_ready"], 1)
                dve.wait_ge(*at("bounds_exp"))
                seq(dve.tensor_tensor(lower[:, 2, :], lower[:, 0, :], lower[:, 1, :], ALU.add))
                seq(dve.reciprocal(lower[:, 3, :], lower[:, 2, :]))
                seq(dve.tensor_tensor(lower[:, 2, :], lower[:, 0, :], lower[:, 3, :], ALU.mult))
                seq(dve.tensor_scalar(lower[:, 3, :], lower[:, 2, :], -1.0, 1.0, ALU.mult, ALU.add))
                dve.wait_ge(*at("pos_landed", 16))
                dve.wait_ge(*at("const_landed", 16))
                seq(dve.tensor_copy(ang[:, 0, :], pos_i[:, :]))
                seq(dve.tensor_scalar(ang[:, 1, :], ang[:, 0, :], kcol("inv_freq"), None, ALU.mult))
                seq(dve.tensor_scalar(ang[:, 0, :], ang[:, 1, :], 1.0 / TWO_PI, MAGIC, ALU.mult, ALU.add))
                seq(dve.tensor_scalar(ang[:, 0, :], ang[:, 0, :], MAGIC, None, ALU.subtract))
                for part in (PI_HI, PI_MID, PI_LO):
                    seq(dve.scalar_tensor_tensor(ang[:, 1, :], ang[:, 0, :], -part, ang[:, 1, :], ALU.mult, ALU.add))
                pi = float(np.nextafter(np.float32(np.pi), np.float32(0)))
                seq(dve.tensor_scalar(ang[:, 2, :], ang[:, 1, :], pi, -pi, ALU.min, ALU.max))
                seq(dve.tensor_scalar(ang[:, 0, :], ang[:, 2, :], np.pi / 2, -TWO_PI, ALU.is_gt, ALU.mult))
                seq(dve.scalar_tensor_tensor(ang[:, 3, :], ang[:, 2, :], np.pi / 2, ang[:, 0, :], ALU.add, ALU.add))
                dve.tensor_scalar(ang[:, 3, :], ang[:, 3, :], pi, -pi, ALU.min, ALU.max)\
                    .then_inc(sems["angle_ready"], 1)
                dve.wait_ge(*at("x_landed", 16))

            def squares(src, n):
                for tb in range(TB):
                    last = dve.tensor_tensor_reduce(gate_sb[:, tb, 0:n], src(tb), src(tb), 1.0 / n, 0.0,
                                                    ALU.mult, ALU.add, stat[:, tb:tb + 1])
                last.then_inc(sems["square_ready"], 1)
                dve.wait_ge(*at("deviation_ready"))
                seq(dve.reciprocal(stat[:, 4:6], stat[:, 2:4]))

            def scaled(src, n, banks=False):
                if banks:
                    for tb in range(TB):
                        last = dve.tensor_copy(tok[:, tb, 0:n], src(tb))
                    seq(last)
                    src = lambda tb: tok[:, tb, 0:n]
                squares(src, n)
                for tb in range(TB):
                    dve.tensor_scalar(tok[:, tb, 0:n], src(tb), stat[:, 4 + tb:5 + tb], None, ALU.mult)\
                        .then_inc(sems["tokens_ready"], 1)

            def turn(nf, banks, hi, lo, name=None, c0=0):
                for b in range(nf // 2):
                    dve.wait_ge(*at("features_hi"))
                    if name is None:
                        lower_part(lo[:, 2 * b:2 * b + 2, :], wk[:, banks[b], :].rearrange("p (f n) -> p f n", f=2),
                                   hi[:, 2 * b:2 * b + 2, :]).then_inc(sems["features_lo"], 1)
                        continue
                    for f in range(2):
                        last = lower_part(lo[:, 2 * b + f, :], wk[:, banks[b], f * S:(f + 1) * S],
                                          hi[:, 2 * b + f, :], gcol(name, c0 + 2 * b + f))
                    last.then_inc(sems["features_lo"], 1)

            def norm(name, c0):
                scaled(lambda tb: res[:, tb, :], D)
                turn(KD, (0, 1, 2, 3), fT_hi, fT_lo, name, c0)

            def turn_residual():
                turn(KD, (0, 1, 2, 3), fT_hi, fT_lo)

            def norm_row(n):
                dve.wait_ge(*at(f"norm_rows{n % 2}_landed", 32))

            def final_norm():
                squares(lambda tb: res[:, tb, :], D)
                norm_row(0)
                for tb in range(TB):
                    last = dve.scalar_tensor_tensor(res[:, tb, :], res[:, tb, :], stat[:, 4 + tb:5 + tb],
                                                    norm_g[:, 0, :], ALU.mult, ALU.mult)
                    last.then_inc(sems["tokens_ready"], 1)
                seq(dve.tensor_copy(stat[:, 0:1], stat[:, 1:2]))
                dve.tensor_copy(stat[:, 0:1], stat[:, 1:2]).then_inc(sems["norm_rows_used"], 1)

            def layer_norm(n):
                for tb in range(TB):
                    for half in range(2):
                        last = dve.bn_stats(bn[:, tb, half, :], res[:, tb, half * 512:(half + 1) * 512])
                seq(last)
                for tb in range(TB):
                    last = dve.bn_aggr(mv[:, tb, :], bn[:, tb, :, :])
                seq(last)
                dve.tensor_copy(stat[:, 0:2], mv[:, :, 1]).then_inc(sems["square_ready"], 1)
                dve.wait_ge(*at("deviation_ready"))
                seq(dve.reciprocal(stat[:, 4:6], stat[:, 2:4]))
                norm_row(n + 1)
                for tb in range(TB):
                    last = dve.tensor_scalar(res[:, tb, :], res[:, tb, :], mv[:, tb, 0:1], stat[:, 4 + tb:5 + tb],
                                             ALU.subtract, ALU.mult)
                seq(last)
                for tb in range(TB):
                    last = dve.tensor_tensor(res[:, tb, :], res[:, tb, :], norm_g[:, (n + 1) % 2, :], ALU.mult)
                seq(last)
                for tb in range(TB):
                    last = dve.tensor_tensor(res[:, tb, :], res[:, tb, :], norm_b[:, (n + 1) % 2, :], ALU.add)
                    last.then_inc(sems["out_ready" if n == 3 and tb else "tokens_ready"], 1)
                if n < 3:
                    dve.tensor_copy(stat[:, 0:1], stat[:, 1:2]).then_inc(sems["norm_rows_used"], 1)

            def residual(second, scale=1.0):
                for b in range(4):
                    r = res[:, b // 2, (b % 2) * 512:(b % 2 + 1) * 512]
                    if second:
                        last = dve.scalar_tensor_tensor(r, r, ALPHA, acc[:, b, :], ALU.mult, ALU.add)
                    else:
                        last = dve.scalar_tensor_tensor(r, acc[:, b, :], scale, r, ALU.mult, ALU.add)
                seq(last)

            def hidden(src, nk=2, scale=None):
                dve.wait_ge(*at("hidden_hi"))
                lower_part(hT_lo[:, 0:nk, :], src.rearrange("p (f n) -> p f n", f=nk), hT_hi[:, 0:nk, :], scale)\
                    .then_inc(sems["hidden_lo"], 1)

            def ffn(second, last=False):
                def gate():
                    for tb in range(TB):
                        dve.wait_ge(*at("silu_ready"))
                        dve.tensor_tensor(hid[:, tb, :], silu[:, tb, :], wk[:, tb, FC:2 * FC], ALU.mult)\
                            .then_inc(sems["hidden_ready"], 1)
                    unit_done()
                    split()

                def body(j):
                    unit_done()
                    hidden(wk[:, 2, :])
                    split()
                    gate()
                    unit_done()
                    split()

                unit_done()
                split()
                gate()
                at.repeat(dve, body, 1, NFF, peel_last=last)
                hidden(wk[:, 2, :])
                unit_done()
                residual(second, 0.5)
                split()

            def hgrn():
                def halves(t, m):
                    v = t.rearrange("p (n a m) -> p n a m", a=2, m=m)
                    return v[:, :, 0, :], v[:, :, 1, :]

                def body(h):
                    unit_done()
                    dve.wait_ge(*at("sigmoids_ready", 2))
                    one_minus = lower[:, 3, bass.ds(h, 1)]
                    dve.tensor_scalar(k_sb[:, 0, :], f_sb[:, 1, :], one_minus, None, ALU.mult)
                    seq(dve.tensor_scalar(f_sb[:, 0, :], f_sb[:, 0, :], one_minus, lower[:, 2, bass.ds(h, 1)],
                                          ALU.mult, ALU.add))
                    dve.tensor_scalar(f_sb[:, 0, :], f_sb[:, 0, :], LN_FLOOR, None, ALU.max)\
                        .then_inc(sems["forget_ready"], 1)
                    split()
                    unit_done()
                    split()
                    dve.wait_ge(*at("log_ready"))
                    dve.tensor_tensor_scan(b64[:, :], kcol("restart"), lg_sb[:, :], 0.0, ALU.mult, ALU.add)
                    seq(dve.tensor_tensor_scan(b256[:, :], kcol("ones"), lg_sb[:, :], 0.0, ALU.mult, ALU.add))
                    for n in range(LEVELS):
                        m = 1 << n
                        first, second = halves((b64 if m < 64 else b256)[:, :], m)
                        e_first, e_second = halves(levels[:, n, :], m)
                        ref = first[:, :, m - 1:m].to_broadcast([P, S // (2 * m), m])
                        dve.tensor_tensor(e_first, ref, first, ALU.subtract)
                        last = dve.tensor_tensor(e_second, second, ref, ALU.subtract)
                    last.then_inc(sems["decay_in_ready"], 1)
                    dve.wait_ge(*at("decay_ready"))
                    dve.wait_ge(*at("q_ready"))
                    for n in range(LEVELS):
                        m = 1 << n
                        e_first, e_second = halves(levels[:, n, :], m)
                        dve.tensor_tensor(e_first, e_first, halves(k_sb[:, 0, :], m)[0], ALU.mult)
                        last = dve.tensor_tensor(e_second, e_second, halves(q_sb[:, 0, :], m)[1], ALU.mult)
                    last.then_inc(sems["level_in_ready"], 1)
                    for r in range(4):
                        dve.wait_ge(*at("level_done"))
                        for i in range(2):
                            n = 2 * r + i
                            mask = tile2(kcol("levels")[:, n * P:(n + 1) * P])
                            got = wk[:, 2 + r % 2, i * 2 * P:(i + 1) * 2 * P].rearrange("p (t n) -> p t n", t=TB)
                            if n == 0:
                                seq(dve.tensor_tensor(at_sb[:, :, :], got, mask, ALU.mult))
                            else:
                                dve.memset(eps_sb[:, 3:4], 0.0)
                                ins = dve.copy_predicated(at_sb[:, :, :], mask.bitcast(U32), got)
                                if i == 0:
                                    seq(ins)
                                else:
                                    ins.then_inc(sems["level_merged"], 1)
                                    dve.wait_ge(*at("level_merged"))
                    dve.wait_ge(*at("o_dev_ready"))
                    seq(dve.reciprocal(stat[:, 4:6], stat[:, 2:4]))
                    for tb in range(TB):
                        dve.scalar_tensor_tensor(hid[:, tb, 0:P], wk[:, 3, tb * P:(tb + 1) * P],
                                                 stat[:, 4 + tb:5 + tb], sg_sb[:, tb, 0:P], ALU.mult, ALU.mult)\
                            .then_inc(sems["o_gated"], 1)
                    hidden(wk[:, 2, 0:S], 1, gcol("a_out_gain"))
                    unit_done()
                    split()

                at.repeat(dve, body, 0, A_HEADS)
                residual(0)

            def ple(layer):
                dve.wait_ge(*at("p_hi"))
                lower_part(pT_lo[:, :, :], wk[:, 2, :].rearrange("p (f n) -> p f n", f=2), pT_hi[:, :, :])\
                    .then_inc(sems["p_lo"], 1)
                for c in range(4):
                    unit_done()
                    split()
                unit_done()
                dve.wait_ge(*at("ple_gate_ready", 4))
                for b in range(4):
                    g = gate_sb[:, b // 2, (b % 2) * 512:(b % 2 + 1) * 512]
                    last = dve.tensor_tensor(g, g, wk[:, b, :], ALU.mult)
                seq(last)
                for tb in range(TB):
                    last = dve.tensor_tensor(res[:, tb, :], res[:, tb, :], gate_sb[:, tb, :], ALU.add)
                seq(last)
                split()

            def latent():
                unit_done()
                split()
                unit_done()
                scaled(lambda tb: wk[:, 0, tb * S:(tb + 1) * S], B_KV, banks=True)
                dve.wait_ge(*at("sin_ready", 2))
                dve.wait_ge(*at("zeros_ready", 3))
                dve.wait_ge(*at("kr_raw_ready"))
                dve.tensor_tensor(rot1[:, 0, :], kr_raw[:, :], mla_cos[:, :], ALU.mult)
                dve.wait_ge(*at("kr_rotated"))
                seq(dve.tensor_tensor(rot1[:, 1, :], wk[:, 1, S:2 * S], mla_sin[:, :], ALU.mult))
                for h in range(2):
                    r = slice(h * B_ROPE, (h + 1) * B_ROPE)
                    last = dve.tensor_tensor(krz[r, h, :], rot1[r, 0, :], rot1[r, 1, :], ALU.add)
                last.then_inc(sems["kr_ready"], 1)
                turn(2, (2,), cT_hi, cT_lo, "kv_latent_norm")
                split()

            def softmax(scale):
                dve.wait_ge(*at("scores_done"))
                seq(dve.tensor_tensor(sc[:, :, :], wk[:, 0:2, 0:SEG], tile2(kcol("causal")), ALU.add))
                dve.tensor_reduce(stat[:, 0:2], sc[:, :, 0:P], AX.X, ALU.max)
                seq(dve.tensor_reduce(stat[:, 2:4], sc[:, :, P:SEG], AX.X, ALU.max))
                dve.tensor_scalar(stat[:, 4:8], stat[:, 0:4], -scale, None, ALU.mult).then_inc(sems["max_ready"], 1)
                dve.wait_ge(*at("exp_ready"))
                seq(dve.reciprocal(stat[:, 12:16], stat[:, 8:12]))
                for h in range(2):
                    for seg, (a, b) in enumerate(((0, P), (P, SEG))):
                        c = 12 + 2 * seg + h
                        dve.tensor_scalar(prob[:, h, a:b], prob[:, h, a:b], stat[:, c:c + 1], None, ALU.mult)\
                            .then_inc(sems["probs_ready"], 1)
                dve.wait_ge(*at("probs_turned", 2))
                dve.tensor_copy(probT[:, 1, :], wk[:, 3, 0:SEG]).then_inc(sems["probsT1_ready"], 1)

            def mla():
                unit_done()
                split()
                unit_done()
                scaled(lambda tb: wk[:, tb, :], B_Q, banks=True)
                split()
                turn(4, (2, 3), fT_hi, fT_lo, "b_q_norm")

                def body(j):
                    unit_done()
                    dve.tensor_copy(v_sb[:, :, :], wk[:, 1, :].rearrange("p (t n) -> p t n", t=TB))\
                        .then_inc(sems["v_ready"], 1)
                    split()
                    unit_done()
                    dve.wait_ge(*at("qr_raw_ready"))
                    dve.tensor_tensor(rot1[:, 0, :], qr_sb[:, :], mla_cos[:, :], ALU.mult)
                    dve.wait_ge(*at("qr_rotated"))
                    seq(dve.tensor_tensor(rot1[:, 1, :], wk[:, 3, S:2 * S], mla_sin[:, :], ALU.mult))
                    dve.tensor_tensor(rot2[:, 0, :], rot1[:, 0, :], rot1[:, 1, :], ALU.add)\
                        .then_inc(sems["qr_ready"], 1)
                    split()
                    softmax((B_NOPE + B_ROPE) ** -0.5)
                    hidden(wk[:, 0, :])
                    unit_done()
                    split()

                at.repeat(dve, body, 0, B_HEADS // 2)
                residual(0)

            def branch(kind, layer):
                scale = C_DIM ** -0.5

                def values():
                    unit_done()
                    src = wk[:, 1, 0:2 * P].rearrange("p (t n) -> p t n", t=TB)
                    for h in range(2):
                        c = slice(h * C_DIM, (h + 1) * C_DIM)
                        dve.tensor_copy(vz[:, :, h, c], src[:, :, c]).then_inc(sems["v_ready"], 1)
                    split()

                def body_sb(j):
                    unit_done()
                    split()
                    values()
                    z = wk[:, 2:4, 0:SEG]
                    strict = tile2(kcol("strict"))
                    dve.wait_ge(*at("abs_ready"))
                    seq(dve.tensor_scalar(keep[:, :, :], z, scale, 0.0, ALU.mult, ALU.min))
                    dve.wait_ge(*at("softplus_ready"))
                    seq(dve.tensor_tensor(prob[:, :, :], keep[:, :, :], soft[:, :, :], ALU.subtract))
                    seq(dve.scalar_tensor_tensor(keep[:, :, :], z, -scale, prob[:, :, :], ALU.mult, ALU.add))
                    dve.tensor_tensor(keep[:, :, :], keep[:, :, :], strict, ALU.mult).then_inc(sems["keep_ready"], 1)
                    dve.wait_ge(*at("suffix_done"))
                    dve.tensor_tensor(sc[:, :, :], prob[:, :, :], wk[:, 0:2, 0:SEG], ALU.add)\
                        .then_inc(sems["weight_in_ready"], 1)
                    dve.wait_ge(*at("weight_exp"))
                    dve.tensor_tensor(probT[:, :, :], soft[:, :, :], strict, ALU.mult)\
                        .then_inc(sems["weight_ready"], 1)
                    hidden(wk[:, 2, 0:S], 1)
                    unit_done()
                    split()

                def body_moba(j):
                    unit_done()
                    split()
                    values()
                    cos, sin = tile2(kcol("moba_cos")), tile2(kcol("moba_sin"))
                    dve.wait_ge(*at("qr_raw_ready"))
                    dve.tensor_tensor(levels[:, 0:2, :], rot1[:, :, :], cos, ALU.mult)
                    dve.wait_ge(*at("qr_rotated"))
                    seq(dve.tensor_tensor(rot2[:, :, :], wk[:, 2, :].rearrange("p (a n) -> p a n", a=2), sin,
                                          ALU.mult))
                    dve.tensor_tensor(q_sb[:, 0, :], levels[:, 0, :], rot2[:, 0, :], ALU.add)\
                        .then_inc(sems["qk_roped"], 1)
                    for h in range(2):
                        r = slice(h * C_DIM, (h + 1) * C_DIM)
                        dve.tensor_tensor(kz[r, h, :], levels[r, 1, :], rot2[r, 1, :], ALU.add)\
                            .then_inc(sems["qk_roped"], 1)
                    softmax(scale)
                    hidden(wk[:, 0, 0:S], 1)
                    unit_done()
                    split()

                at.repeat(dve, body_sb if kind == "sb" else body_moba, 0, C_HEADS // 2)

            def merge(layer):
                dve.wait_ge(*at("branch_ready", 4))
                for q in range(4):
                    which, half = q // 2, q % 2
                    c = slice(half * 512, (half + 1) * 512)
                    unit_done()
                    split()
                    unit_done()
                    for tb in range(TB):
                        g = gates4[:, 2 * (q % 2) + tb, :]
                        dve.wait_ge(*at("gate_ready"))
                        if which == 0:
                            dve.tensor_tensor(tok[:, tb, c], g, gate_sb[:, tb, c], ALU.mult)\
                                .then_inc(sems["gate_used"], 1)
                        else:
                            dve.tensor_tensor(g, g, acc[:, 2 * tb + half, :], ALU.mult)\
                                .then_inc(sems["gate_used"], 1)
                    if which:
                        seq(dve.tensor_copy(stat[:, 0:1], stat[:, 1:2]))
                        for tb in range(TB):
                            last = dve.tensor_tensor(tok[:, tb, c], tok[:, tb, c], gates4[:, 2 * (q % 2) + tb, :],
                                                     ALU.add)
                            if half:
                                last.then_inc(sems["tokens_ready"], 1)
                    split()
                turn(KD, (0, 1, 2, 3), fT_hi, fT_lo)
                for c in range(4):
                    unit_done()
                    if c == 3:
                        residual(1)
                    split()

            def finish():
                if stop_after is not None:
                    dve.tensor_copy(stat[:, 0:1], stat[:, 1:2]).then_inc(sems["out_ready"], 1)

            network(Stages(setup=setup, norm=norm, ffn=ffn, hgrn=hgrn, mla=mla, ple=ple, latent=latent,
                                    final_norm=final_norm, turn_residual=turn_residual, branch=branch,
                                    merge=merge, layer_norm=layer_norm, finish=finish))


_INS = ["x", "p", "positions", "norm_gains", "a_lb_logits", "a_out_gain", "kv_norm_in", "kv_latent_norm",
        "b_q_norm", "final_norm", "ln_mix_g_2", "ln_mix_b_2", "ln_ffn_g_2", "ln_ffn_b_2"]


def layout(inputs):
    arrays = {name: np.ascontiguousarray(inputs[name]) for name in _INS}
    w = {name: np.asarray(a) for name, a in inputs.items()}
    arrays["weights"] = np.concatenate([unit.reshape(-1) for unit in stream(w)])
    arrays["const"] = constants()
    return arrays


def kernel(**inputs):
    import concourse.bacc as bacc
    from concourse.bass_utils import run_bass_kernel_spmd

    nc = bacc.Bacc("TRN2", target_bir_lowering=False, num_devices=1)
    arrays = {f"in_{name}": a for name, a in layout(inputs).items()}
    args = [nc.dram_tensor(name, a.shape, mybir.dt.from_np(a.dtype), kind="ExternalInput").ap()
            for name, a in arrays.items()]
    out = nc.dram_tensor("out", (1, S, D), F32, kind="ExternalOutput").ap()
    build(nc, *args, out)
    r = run_bass_kernel_spmd(nc, [arrays], core_ids=[0])
    return r.results[0]["out"]
```

```python
from contextlib import ExitStack, contextmanager

import numpy as np

import concourse.bass as bass
from concourse import mybir

F32 = mybir.dt.float32
F32R = mybir.dt.float32r
I32 = mybir.dt.int32
U32 = mybir.dt.uint32
ALU = mybir.AluOpType
ACT = mybir.ActivationFunctionType
AX = mybir.AxisListType

P = 128
S = 256
TB = S // P
D = 1024
KD = D // P
DFF = 2816
FC = 256
NFF = DFF // FC
PLE = 256
SLOT = 2048
RING = 3
A_HEADS, A_DIM = 8, 128
LEVELS = 8
B_HEADS, B_NOPE, B_ROPE, B_VDIM = 16, 128, 64, 128
B_Q, B_KV = 512, 256
C_HEADS, C_DIM = 8, 64
C_WIDTH = C_HEADS * C_DIM
EPS, LN_EPS = 1e-6, 1e-5
ALPHA = 4 ** 0.25
SEG = P + S
TWO_PI = 2 * np.pi
PI_HI = 6.28125
PI_MID = float(np.float32(int((TWO_PI - PI_HI) * 2 ** 21) / 2 ** 21))
PI_LO = float(TWO_PI - PI_HI - PI_MID)
MAGIC = 1.5 * 2.0 ** 23
LN_FLOOR = 2.0 ** -60

GAIN_ROWS = [("norm_gains", 64), ("kv_norm_in", 8), ("kv_latent_norm", 2), ("b_q_norm", 4),
             ("a_out_gain", 1), ("a_lb_logits", 16)]
GAIN_AT = {}
_n = 0
for _name, _rows in GAIN_ROWS:
    GAIN_AT[_name] = _n
    _n += _rows
N_GAINS = _n

CONST_AT = {}
_n = 0
for _name, _w in [("identity", P), ("rotate_mla", P), ("rotate_moba", P), ("causal", SEG), ("strict", SEG),
                  ("later", P), ("ones", S), ("levels", LEVELS * P), ("restart", S), ("moba_cos", S),
                  ("moba_sin", S), ("inv_freq", 1)]:
    CONST_AT[_name] = (_n, _w)
    _n += _w
N_CONST = _n


def constants():
    c = np.zeros((P, N_CONST), np.float32)

    def put(name, a):
        at, w = CONST_AT[name]
        c[:, at:at + w] = a

    i = np.arange(P)
    put("identity", np.eye(P))

    def rotation(group, half):
        r = np.zeros((P, P))
        for g in range(0, P, group):
            for j in range(half):
                r[g + half + j, g + j] = -1.0
                r[g + j, g + half + j] = 1.0
        return r

    put("rotate_mla", rotation(B_ROPE, B_ROPE // 2))
    put("rotate_moba", rotation(C_DIM, C_DIM // 8))
    tri = np.where(i[:, None] >= i[None, :], 0.0, -1e30)
    put("causal", np.concatenate([tri, np.zeros((P, P)), tri], 1))
    past = (i[:, None] < i[None, :]).astype(np.float32)
    put("strict", np.concatenate([past, np.ones((P, P)), past], 1))
    put("later", (i[:, None] > i[None, :]))
    put("ones", 1.0)
    levels = [np.eye(P)]
    for level in range(LEVELS - 1):
        m = 1 << level
        same = (i[:, None] // (2 * m)) == (i[None, :] // (2 * m))
        levels.append(same & (i[:, None] % (2 * m) < m) & (i[None, :] % (2 * m) >= m))
    put("levels", np.concatenate(levels, 1))
    put("restart", (np.arange(S) % 64 != 0).astype(np.float32)[None])
    pos = np.arange(S, dtype=np.float32)
    rope = C_DIM // 4
    freq = (np.float32(500000.0) ** (-np.arange(0, rope, 2, dtype=np.float32) / np.float32(rope))).astype(np.float32)
    ang = pos[None, :] * freq[:, None]
    cos, sin = np.ones((C_DIM, S), np.float32), np.zeros((C_DIM, S), np.float32)
    for h in (0, rope // 2):
        cos[h:h + rope // 2], sin[h:h + rope // 2] = np.cos(ang), np.sin(ang)
    put("moba_cos", np.tile(cos, (2, 1)))
    put("moba_sin", np.tile(sin, (2, 1)))
    e = np.arange(0, B_ROPE, 2, dtype=np.float32) / np.float32(B_ROPE)
    inv = (np.float32(1.0) / np.float32(10000.0) ** e).astype(np.float32)
    put("inv_freq", np.tile(inv, P // len(inv))[:, None])
    return c


def interleave(heads, a, b, c):
    yield a(0)
    yield b(0)
    for h in range(heads):
        if h:
            yield c(h - 1)
        if h + 1 < heads:
            yield a(h + 1)
            yield b(h + 1)
    yield c(heads - 1)


def unit_sizes():
    ffn = [SLOT] * (3 * NFF)
    for layer in range(2):
        yield from ffn
        if layer == 0:
            yield from interleave(A_HEADS, lambda h: SLOT, lambda h: SLOT, lambda h: D)
        else:
            yield from [SLOT] * 2
            yield from interleave(B_HEADS // 2, lambda j: 4 * 384, lambda j: D, lambda j: SLOT)
        yield from ffn
        yield from [SLOT] * 5
        if layer == 0:
            yield from (SLOT, KD * P)
    for layer in range(2):
        for _ in range(2):
            yield from interleave(C_HEADS // 2, lambda j: SLOT, lambda j: D, lambda j: D)
        yield from [SLOT] * 12
        yield from ffn


UNITS = list(unit_sizes())


def stream(w):
    def cut(a, k0, nk, *cols):
        b = np.concatenate([a[k0 * P:(k0 + nk) * P, c:c + n] for c, n in cols], 1)
        return b.reshape(nk, P, -1).transpose(1, 0, 2).reshape(P, -1)

    def ffn(gate, up, at, down):
        for j in range(NFF + 1):
            if j < NFF:
                for k0 in (0, 4):
                    a = cut(gate, k0, 4, (j * FC, FC)).reshape(P, 4, FC)
                    b = cut(up, k0, 4, (j * FC + at, FC)).reshape(P, 4, FC)
                    yield np.concatenate([a, b], 2).reshape(P, -1)
            if j:
                yield cut(down, 2 * (j - 1), 2, (0, D))

    def close(a, blocks):
        for k in range(0, blocks, 2):
            yield cut(a, k, 2, (0, D))

    for layer in range(2):
        w_in, w_out = w["ffn_w_in"][layer], w["ffn_w_out"][layer]
        yield from ffn(w_in[0], w_in[0], DFF, w_out[0])
        if layer == 0:
            a = w["a_w_in"][0]
            yield from interleave(A_HEADS, lambda h: cut(a, 0, KD, (h * P, P), (h * P + D, P)),
                                  lambda h: cut(a, 0, KD, (h * P + 2 * D, P), (h * P + 3 * D, P)),
                                  lambda h: cut(w["a_w_out"][0], h, 1, (0, D)))
        else:
            for k0 in (0, 4):
                yield cut(w["b_w_dq"][0], k0, 4, (0, B_Q))
            yield from interleave(B_HEADS // 2,
                                  lambda j: cut(w["b_w_uq"][0], 0, 4, (j * 384, 128), (j * 384 + 192, 128),
                                                (j * 384 + 128, 64), (j * 384 + 320, 64)),
                                  lambda j: cut(w["kv_w_up"], 0, 2, (j * 512, 512)),
                                  lambda j: cut(w["b_w_out"][0], 2 * j, 2, (0, D)))
        yield from ffn(w_in[1], w_in[1], DFF, w_out[1])
        yield from close(w["ple_w_gate"][layer], KD)
        yield from close(w["ple_w_in"][layer], 2)
        if layer == 0:
            yield cut(w["kv_w_down"], 0, KD, (0, B_KV))
            yield cut(w["kv_w_down"], 0, KD, (B_KV, B_ROPE), (B_KV, B_ROPE))
    for layer in range(2):
        a = w["w_in_2"][layer]
        for base, b in ((0, w["w_branch_sb_2"][layer]), (3 * C_WIDTH, w["w_branch_moba_2"][layer])):
            yield from interleave(C_HEADS // 2,
                                  lambda j: cut(a, 0, KD, (base + j * P, P), (base + j * P + C_WIDTH, P)),
                                  lambda j: cut(a, 0, KD, (base + j * P + 2 * C_WIDTH, P)),
                                  lambda j: cut(b, j, 1, (0, D)))
        for c in range(4):
            for k0 in (0, 4):
                yield cut(a, k0, 4, (6 * C_WIDTH + c * 512, 512))
        yield from close(w["w_out_2"][layer], KD)
        yield from ffn(w["w_ffn_gate_2"][layer], w["w_ffn_up_2"][layer], 0, w["w_ffn_down_2"][layer])


class Stages:

    def __init__(self, setup, norm, ffn, hgrn, mla, ple, latent, final_norm, turn_residual, branch, merge,
                 layer_norm, finish):
        self.setup, self.norm, self.ffn, self.hgrn, self.mla = setup, norm, ffn, hgrn, mla
        self.ple, self.latent, self.final_norm, self.turn_residual = ple, latent, final_norm, turn_residual
        self.branch, self.merge, self.layer_norm, self.finish = branch, merge, layer_norm, finish


class Follow:

    def __init__(self, sems, **behind):
        self.sems, self.n, self.rate, self.i = sems, {k: -v for k, v in behind.items()}, None, None

    def __call__(self, name, k=1):
        self.n[name] = self.n.get(name, 0) + k
        if self.i is None:
            return self.sems.get(name), self.n[name]
        return self.sems.get(name), self.i * self.rate.get(name, 0) + self.n[name]

    @contextmanager
    def loop(self, engine, start, end, rate):
        before, unit, units = dict(self.n), self.n.get("unit", 0), rate.get("unit", 0)
        assert UNITS[unit:unit + units * (end - start)] == UNITS[unit:unit + units] * (end - start)
        with engine.Fori(0, end - start) as i:
            self.i, self.rate = i, rate
            yield i + start
            self.i = None
        for name, n in self.n.items():
            assert n - before.get(name, 0) == rate.get(name, 0), (name, n, before, rate)
            self.n[name] = before.get(name, 0) + rate.get(name, 0) * (end - start)

    def repeat(self, engine, body, start, end, peel_last=False):
        before = dict(self.n)
        body(start)
        rate = {name: n - before.get(name, 0) for name, n in self.n.items()}
        stop = end - peel_last
        with self.loop(engine, start + 1, stop, rate) as i:
            body(i)
        if peel_last:
            body(end - 1)

    def pipeline(self, engine, body, n):
        body(0)
        before = dict(self.n)
        body(1)
        rate = {name: k - before.get(name, 0) for name, k in self.n.items()}
        if n > 4:
            with self.loop(engine, 2, n - 2, rate) as i:
                body(i)
        for h in range(n - 2, n):
            body(h)


SIGNALS = """
landed0 landed1 landed2 hi_ready lo_ready unit_done
const_landed gains_landed x_landed p_landed pos_landed norm_rows0_landed norm_rows1_landed norm_rows_used
out_ready out_landed gains_turned gains_ready bounds_in_ready bounds_exp angle_ready sin_ready zeros_ready
square_ready deviation_ready tokens_ready turned features_hi features_lo p_turned p_hi p_lo ple_gate_ready
gate_up_done silu_ready hidden_ready hidden_turned hidden_hi hidden_lo
kr_raw_ready kr_rotated kr_ready
sigmoids_ready q_ready forget_ready log_ready decay_in_ready decay_ready
level_in_ready level_done level_merged cross_done cross_ready o_done o_dev_ready o_gated
kn_ready v_ready qn_ready qr_raw_ready qr_rotated qr_ready scores_done max_ready exp_ready
kn_done out_gate_ready forget_done probs_ready probs_turned probsT0_ready probsT1_ready attn_done
qk_ready qk_roped z_done abs_ready softplus_ready keep_ready suffix_done weight_in_ready weight_exp weight_ready
branch_ready gate_ready gate_used dve_step act_step
""".split()


def build(nc, x, p, positions, norm_gains, a_lb_logits, a_out_gain, kv_norm_in, kv_latent_norm, b_q_norm,
          final_norm, ln_mix_g_2, ln_mix_b_2, ln_ffn_g_2, ln_ffn_b_2, weights, const, out, stop_after=None):
    ctx = ExitStack()
    with ctx:
        def sb(name, shape, dt=F32):
            return ctx.enter_context(nc.sbuf_tensor(name, shape, dt))

        raw = sb("raw", [P, RING, SLOT])
        w_hi = sb("w_hi", [P, RING, SLOT], F32R)
        w_lo = sb("w_lo", [P, RING, SLOT], F32R)
        res = sb("res", [P, TB, D])
        tok = sb("tok", [P, TB, D])
        fT_hi = sb("fT_hi", [P, KD, S], F32R)
        fT_lo = sb("fT_lo", [P, KD, S], F32R)
        hT_hi = sb("hT_hi", [P, 2, S], F32R)
        hT_lo = sb("hT_lo", [P, 2, S], F32R)
        pT_hi, pT_lo = hT_hi, hT_lo
        cT_hi = sb("cT_hi", [P, 2, S], F32R)
        cT_lo = sb("cT_lo", [P, 2, S], F32R)
        silu = sb("silu", [P, TB, FC])
        hid = sb("hid", [P, TB, FC])
        p_sb = sb("p_sb", [P, 2, TB, PLE])
        kc = sb("kc", [P, N_CONST])
        gain_rows = sb("gain_rows", [N_GAINS, P])
        gains = sb("gains", [P, N_GAINS])
        norm_g = sb("norm_g", [P, 2, D])
        norm_b = sb("norm_b", [P, 2, D])
        gate_sb = sb("gate_sb", [P, TB, D])
        stat = sb("stat", [P, 16])
        eps_sb = sb("eps_sb", [P, 4])
        bn = sb("bn", [P, TB, 2, 6])
        mv = sb("mv", [P, TB, 2])
        pos_i = sb("pos_i", [P, S], I32)
        mla_cos, mla_sin = sb("mla_cos", [P, S]), sb("mla_sin", [P, S])
        krz = sb("krz", [P, 2, S])
        q_sb, k_sb, f_sb = sb("q_sb", [P, 2, S]), sb("k_sb", [P, 2, S]), sb("f_sb", [P, 2, S])
        sg_sb, v_sb = sb("sg_sb", [P, TB, 2 * P]), sb("v_sb", [P, TB, 2 * P])
        lg_sb, b64, b256 = sb("lg_sb", [P, S]), sb("b64", [P, S]), sb("b256", [P, S])
        qr_sb = sb("qr_sb", [P, S])
        levels = sb("levels", [P, LEVELS, S])
        at_sb, cross = sb("at_sb", [P, TB, P]), sb("cross", [P, P])
        ang = levels[:, 0:4, :]
        kr_raw = qr_sb
        flat = levels[:, :, :].rearrange("p a n -> p (a n)")
        soft, keep = [flat[:, i * 2 * SEG:(i + 1) * 2 * SEG].rearrange("p (h n) -> p h n", h=2) for i in range(2)]
        gates4 = levels[:, :, :].rearrange("p a n -> p (a n)").rearrange("p (b n) -> p b n", b=4)
        rot1, rot2 = sb("rot1", [P, 2, S]), sb("rot2", [P, 2, S])
        kz, vz = sb("kz", [P, 2, S]), sb("vz", [P, TB, 2, P])
        sc, prob, probT = sb("sc", [P, 2, SEG]), sb("prob", [P, 2, SEG]), sb("probT", [P, 2, SEG])
        acc = ctx.enter_context(nc.psum_tensor("acc", [P, 4, 512], F32))
        wk = ctx.enter_context(nc.psum_tensor("wk", [P, 4, 512], F32))
        sems = {name: ctx.enter_context(nc.semaphore(name)) for name in SIGNALS}

        def kcol(name):
            at, w = CONST_AT[name]
            return kc[:, at:at + w]

        ident = kcol("identity")

        def gcol(name, n=0):
            c = GAIN_AT[name] + n
            return gains[:, c:c + 1]

        lower = sb("lower", [P, 4, A_HEADS])

        def tile2(a):
            return a.unsqueeze(1).to_broadcast([P, 2, a.shape[-1]])

        def network(e):
            e.setup()
            for layer in range(2):
                e.norm("norm_gains", (4 * layer) * KD)
                e.ffn(0)
                if stop_after == "ffn":
                    e.finish()
                    return
                e.norm("norm_gains", (4 * layer + 1) * KD)
                if layer == 0:
                    e.hgrn()
                    if stop_after == "hgrn":
                        e.finish()
                        return
                else:
                    e.mla()
                    if stop_after == "mla":
                        e.finish()
                        return
                e.norm("norm_gains", (4 * layer + 2) * KD)
                e.ffn(0)
                e.norm("norm_gains", (4 * layer + 3) * KD)
                e.ple(layer)
                if stop_after == "ple":
                    e.finish()
                    return
                if layer == 0:
                    e.norm("kv_norm_in", 0)
                    e.latent()
            e.final_norm()
            for layer in range(2):
                e.turn_residual()
                e.branch("sb", layer)
                if stop_after == "sb":
                    e.finish()
                    return
                e.branch("moba", layer)
                if stop_after == "moba":
                    e.finish()
                    return
                e.merge(layer)
                e.layer_norm(2 * layer)
                e.turn_residual()
                e.ffn(1, last=layer == 1)
                e.layer_norm(2 * layer + 1)
            e.finish()

        n_units = [0]

        def is_at(h, k):
            return isinstance(h, int) and h == k

        block = ctx.enter_context(nc.Block())

        @block.sync
        def _(sp):
            at = Follow(sems, lo_ready=RING)

            def unit():
                u = at.n.get("unit", 0)
                at.n["unit"] = u + 1
                slot, n = u % RING, UNITS[u]
                sem, value = at("lo_ready")
                if at.i is not None or value > 0:
                    sp.wait_ge(sem, value)
                start = at("floats", P * n)[1] - P * n
                sp.dma_start(raw[:, slot, 0:n], weights[bass.ds(start, P * n)].rearrange("(p n) -> p n", p=P))\
                    .then_inc(sems[f"landed{slot}"], 16)

            def units(n):
                for _ in range(n):
                    unit()

            def mixer(heads):
                units(2)
                at.pipeline(sp, lambda h: units(2 * (not is_at(h, heads - 1)) + (not is_at(h, 0))), heads)
                unit()

            def setup():
                sp.dma_start(kc[:, :], const).then_inc(sems["const_landed"], 16)
                sp.dma_start(res[:, :, :], x[0].rearrange("(t p) d -> p t d", p=P)).then_inc(sems["x_landed"], 16)
                views = {"norm_gains": norm_gains.rearrange("l i (k d) -> (l i k) d", d=P),
                         "kv_norm_in": kv_norm_in.rearrange("(k d) -> k d", d=P),
                         "kv_latent_norm": kv_latent_norm.rearrange("(k d) -> k d", d=P),
                         "b_q_norm": b_q_norm.rearrange("o (k d) -> (o k) d", d=P),
                         "a_out_gain": a_out_gain, "a_lb_logits": a_lb_logits.rearrange("l (k d) -> (l k) d", d=P)}
                for name, n in GAIN_ROWS:
                    r = GAIN_AT[name]
                    sp.dma_start(gain_rows[r:r + n, :], views[name]).then_inc(sems["gains_landed"], 16)
                sp.dma_start(pos_i[:, :], positions.to_broadcast([P, S])).then_inc(sems["pos_landed"], 16)
                for layer in range(2):
                    sp.dma_start(p_sb[:, layer, :, :], p[layer, 0].rearrange("(t p) d -> p t d", p=P))\
                        .then_inc(sems["p_landed"], 16)

            def norm_row(n):
                g, b = [(final_norm, None), (ln_mix_g_2[0], ln_mix_b_2[0]), (ln_ffn_g_2[0], ln_ffn_b_2[0]),
                        (ln_mix_g_2[1], ln_mix_b_2[1]), (ln_ffn_g_2[1], ln_ffn_b_2[1])][n]
                if n >= 2:
                    sp.wait_ge(*at("norm_rows_used"))
                for dst, src in ((norm_g, g), (norm_b, b if b is not None else g)):
                    sp.dma_start(dst[:, n % 2, :], src.rearrange("(o d) -> o d", o=1).to_broadcast([P, D]))\
                        .then_inc(sems[f"norm_rows{n % 2}_landed"], 16)

            def ffn(second, last=False):
                units(2)
                at.repeat(sp, lambda _: units(3), 1, NFF)
                unit()

            def hgrn():
                mixer(A_HEADS)

            def ple(layer):
                units(5)

            def latent():
                units(2)

            def mla():
                units(2)
                mixer(B_HEADS // 2)
                norm_row(0)
                norm_row(1)

            def branch(kind, layer):
                mixer(C_HEADS // 2)
                if kind == "sb" and layer == 1:
                    norm_row(3)

            def merge(layer):
                units(12)
                norm_row(2 * layer + 2)

            def finish():
                if stop_after:
                    units(RING)
                n_units[0] = at.n["unit"]
                sp.wait_ge(*at("out_ready"))
                sp.dma_start(out[0].rearrange("(t p) d -> p t d", p=P), res[:, :, :]).then_inc(sems["out_landed"], 16)
                sp.wait_ge(*at("out_landed", 16))

            none = lambda *a: None
            network(Stages(setup=setup, norm=none, ffn=ffn, hgrn=hgrn, mla=mla, ple=ple, latent=latent,
                                    final_norm=none, turn_residual=none, branch=branch, merge=merge,
                                    layer_norm=none, finish=finish))

        @block.tensor
        def _(pe):
            at = Follow(sems)

            def next_unit():
                slot = at.n.get("unit", 0) % RING
                at.n["unit"] = at.n.get("unit", 0) + 1
                pe.wait_ge(*at("hi_ready"))
                pe.wait_ge(*at("lo_ready"))
                return slot

            def product(o, lhs, rhs, start, stop):
                nc.tensor.matmul(o, lhs[0], rhs[0], start=start, stop=False, skip_group_check=True)
                nc.tensor.matmul(o, lhs[0], rhs[1], start=False, stop=False, skip_group_check=True)
                return nc.tensor.matmul(o, lhs[1], rhs[0], start=False, stop=stop, skip_group_check=True)

            def whole(o, lhs, rhs, start, stop):
                return nc.tensor.matmul(o, lhs, rhs, start=start, stop=stop, skip_group_check=True)

            def wt(slot, shape):
                k, n = shape
                return [t[:, slot, 0:k * n].rearrange("p (k n) -> p k n", k=k) for t in (w_hi, w_lo)]

            def done(ins):
                ins.then_inc(sems["unit_done"], 1)

            def setup():
                pe.wait_ge(*at("const_landed", 16))
                pe.wait_ge(*at("gains_landed", 16 * len(GAIN_ROWS)))
                nc.tensor.transpose(wk[:, 0, 0:N_GAINS], gain_rows[:, :], ident[0:N_GAINS, 0:N_GAINS])\
                    .then_inc(sems["gains_turned"], 1)
                pe.wait_ge(*at("gains_ready"))

            def turn(src, nf, banks, n_ready=2):
                pe.wait_ge(*at("tokens_ready", n_ready))
                for b in range(nf // 2):
                    for f in range(2):
                        for tb in range(TB):
                            c = (2 * b + f) * P
                            last = nc.tensor.transpose(wk[:, banks[b], f * S + tb * P:f * S + (tb + 1) * P],
                                                       src[:, tb, c:c + P], ident)
                    last.then_inc(sems["turned"], 1)
                pe.wait_ge(*at("features_hi", nf // 2))
                pe.wait_ge(*at("features_lo", nf // 2))

            def norm(name, n):
                turn(tok, KD, (0, 1, 2, 3))

            def turn_residual():
                turn(res, KD, (0, 1, 2, 3))

            def close(nk, first, slot=None):
                if slot is None:
                    slot = next_unit()
                w = wt(slot, (nk, D))
                for k in range(nk):
                    for tb in range(TB):
                        lhs = [t[:, k, tb * P:(tb + 1) * P] for t in (hT_hi, hT_lo)]
                        for half in range(2):
                            last = product(acc[:, 2 * tb + half, :], lhs,
                                           [t[:, k, half * 512:(half + 1) * 512] for t in w],
                                           start=first and k == 0, stop=True)
                done(last)

            def ffn(second, last=False):
                def half(k0):
                    slot = next_unit()
                    w = wt(slot, (4, 2 * FC))
                    for tb in range(TB):
                        for k in range(4):
                            ins = product(wk[:, tb, :], [t[:, k0 + k, tb * P:(tb + 1) * P] for t in (fT_hi, fT_lo)],
                                          [t[:, k, :] for t in w], start=k0 + k == 0, stop=k0 + k == KD - 1)
                        if tb:
                            done(ins)
                        elif k0:
                            ins.then_inc(sems["gate_up_done"], 1)

                def turn_hidden():
                    for f in range(2):
                        for tb in range(TB):
                            last = nc.tensor.transpose(wk[:, 2, f * S + tb * P:f * S + (tb + 1) * P],
                                                       hid[:, tb, f * P:(f + 1) * P], ident)
                    last.then_inc(sems["hidden_turned"], 1)

                def down(first):
                    pe.wait_ge(*at("hidden_hi"))
                    pe.wait_ge(*at("hidden_lo"))
                    close(2, first)

                def body(j):
                    pe.wait_ge(*at("hidden_ready", 2))
                    half(0)
                    turn_hidden()
                    half(4)
                    down(isinstance(j, int) and j == 1)

                half(0)
                half(4)
                at.repeat(pe, body, 1, NFF)
                pe.wait_ge(*at("hidden_ready", 2))
                turn_hidden()
                pe.wait_ge(*at("hidden_hi"))
                pe.wait_ge(*at("hidden_lo"))
                close(2, False)

            def hgrn():
                def feature_major(c):
                    for k in range(KD):
                        last = product(wk[:, 0, c * S:(c + 1) * S], [t[:, k, c * P:(c + 1) * P] for t in head_w[0]],
                                       [t[:, k, :] for t in (fT_hi, fT_lo)], start=k == 0, stop=k == KD - 1)
                    return last

                def token_major():
                    w = wt(next_unit(), (KD, 2 * P))
                    for tb in range(TB):
                        for k in range(KD):
                            last = product(wk[:, 1, tb * S:(tb + 1) * S],
                                           [t[:, k, tb * P:(tb + 1) * P] for t in (fT_hi, fT_lo)],
                                           [t[:, k, :] for t in w], start=k == 0, stop=k == KD - 1)
                    done(last)

                def level_scores(r):
                    for i in range(2):
                        n = 2 * r + i
                        for tb in range(TB):
                            c = slice(tb * P, (tb + 1) * P)
                            a, b = (k_sb[:, 0, c], q_sb[:, 0, c]) if n == 0 else \
                                (levels[:, n - 1, c], levels[:, n - 1, c])
                            last = whole(wk[:, 2 + r % 2, (2 * i + tb) * P:(2 * i + tb + 1) * P], a, b, True, True)
                    last.then_inc(sems["level_done"], 1)

                head_w = [None]

                def body(h):
                    more = not is_at(h, A_HEADS - 1)
                    pe.wait_ge(*at("level_in_ready"))
                    level_scores(0)
                    if not is_at(h, 0):
                        pe.wait_ge(*at("hidden_hi"))
                        pe.wait_ge(*at("hidden_lo"))
                    level_scores(1)
                    pe.wait_ge(*at("v_ready"))
                    pe.wait_ge(*at("out_gate_ready"))
                    whole(wk[:, 1, 0:P], levels[:, 7, 0:P], levels[:, 7, P:S], True, True)\
                        .then_inc(sems["cross_done"], 1)
                    if not is_at(h, 0):
                        closing = next_unit()
                    if more:
                        head_w[0] = wt(next_unit(), (KD, 2 * P))
                        feature_major(1).then_inc(sems["forget_done"], 1)
                    pe.wait_ge(*at("level_merged"))
                    level_scores(2)
                    pe.wait_ge(*at("level_merged"))
                    level_scores(3)
                    if not is_at(h, 0):
                        close(1, is_at(h, 1), closing)
                    if more:
                        pe.wait_ge(*at("sigmoids_ready", 2))
                        done(feature_major(0))
                    pe.wait_ge(*at("level_merged", 2))
                    pe.wait_ge(*at("cross_ready"))
                    whole(wk[:, 2, 0:P], at_sb[:, 0, :], v_sb[:, 0, 0:P], True, True)
                    whole(wk[:, 2, P:2 * P], at_sb[:, 1, :], v_sb[:, 1, 0:P], True, False)
                    whole(wk[:, 2, P:2 * P], cross[:, :], v_sb[:, 0, 0:P], False, True).then_inc(sems["o_done"], 1)
                    if more:
                        token_major()
                    pe.wait_ge(*at("o_gated", 2))
                    for tb in range(TB):
                        last = nc.tensor.transpose(wk[:, 3, tb * P:(tb + 1) * P], hid[:, tb, 0:P], ident)
                    last.then_inc(sems["hidden_turned"], 1)

                head_w[0] = wt(next_unit(), (KD, 2 * P))
                feature_major(1).then_inc(sems["forget_done"], 1)
                pe.wait_ge(*at("sigmoids_ready", 2))
                done(feature_major(0))
                token_major()
                at.pipeline(pe, body, A_HEADS)
                pe.wait_ge(*at("hidden_hi"))
                pe.wait_ge(*at("hidden_lo"))
                close(1, False)

            def ple(layer):
                if layer == 0:
                    pe.wait_ge(*at("p_landed", 32))
                for f in range(2):
                    for tb in range(TB):
                        last = nc.tensor.transpose(wk[:, 2, f * S + tb * P:f * S + (tb + 1) * P],
                                                   p_sb[:, layer, tb, f * P:(f + 1) * P], ident)
                last.then_inc(sems["p_turned"], 1)
                for c in range(4):
                    w = wt(next_unit(), (2, D))
                    for k in range(2):
                        for tb in range(TB):
                            for half in range(2):
                                last = product(acc[:, 2 * tb + half, :],
                                               [t[:, 2 * c + k, tb * P:(tb + 1) * P] for t in (fT_hi, fT_lo)],
                                               [t[:, k, half * 512:(half + 1) * 512] for t in w],
                                               start=c + k == 0, stop=c == 3 and k == 1)
                    done(last)
                pe.wait_ge(*at("p_hi"))
                pe.wait_ge(*at("p_lo"))
                w = wt(next_unit(), (2, D))
                for k in range(2):
                    for tb in range(TB):
                        for half in range(2):
                            last = product(wk[:, 2 * tb + half, :],
                                           [t[:, k, tb * P:(tb + 1) * P] for t in (pT_hi, pT_lo)],
                                           [t[:, k, half * 512:(half + 1) * 512] for t in w],
                                           start=k == 0, stop=k == 1)
                done(last)

            def latent():
                w = wt(next_unit(), (KD, B_KV))
                for tb in range(TB):
                    for k in range(KD):
                        last = product(wk[:, 0, tb * S:(tb + 1) * S],
                                       [t[:, k, tb * P:(tb + 1) * P] for t in (fT_hi, fT_lo)],
                                       [t[:, k, :] for t in w], start=k == 0, stop=k == KD - 1)
                done(last)
                w = wt(next_unit(), (KD, P))
                for k in range(KD):
                    last = product(wk[:, 1, 0:S], [t[:, k, :] for t in w],
                                   [t[:, k, :] for t in (fT_hi, fT_lo)], start=k == 0, stop=k == KD - 1)
                done(last)
                pe.wait_ge(*at("kr_raw_ready"))
                whole(wk[:, 1, S:2 * S], kcol("rotate_mla"), kr_raw[:, :], True, True).then_inc(sems["kr_rotated"], 1)
                turn(tok, 2, (2,))
                pe.wait_ge(*at("kr_ready"))

            def softmax_turn():
                pe.wait_ge(*at("probs_ready", 4))
                for h in range(2):
                    for dst, src in ((0, 0), (P, P), (2 * P, 2 * P)):
                        last = nc.tensor.transpose(wk[:, 2 + h, dst:dst + P], prob[:, h, src:src + P], ident)
                    last.then_inc(sems["probs_turned"], 1)

            def softmax_turned():
                pe.wait_ge(*at("probsT0_ready"))
                pe.wait_ge(*at("probsT1_ready"))

            def mla():
                for k0 in (0, 4):
                    w = wt(next_unit(), (4, B_Q))
                    for tb in range(TB):
                        for k in range(4):
                            last = product(wk[:, tb, :], [t[:, k0 + k, tb * P:(tb + 1) * P] for t in (fT_hi, fT_lo)],
                                           [t[:, k, :] for t in w], start=k0 + k == 0, stop=k0 + k == KD - 1)
                    done(last)
                turn(tok, 4, (2, 3))

                def queries():
                    w = wt(next_unit(), (4, 384))
                    for h in range(3):
                        for k in range(4):
                            last = product(wk[:, h // 2, h % 2 * S:h % 2 * S + S], [t[:, k, h * P:(h + 1) * P] for t in w],
                                           [t[:, k, :] for t in (fT_hi, fT_lo)], start=k == 0, stop=k == 3)
                    done(last)

                def rotate():
                    pe.wait_ge(*at("qr_raw_ready"))
                    whole(wk[:, 1, S:2 * S], kcol("rotate_mla"), qr_sb[:, :], True, True)\
                        .then_inc(sems["qr_rotated"], 1)

                def keys():
                    w = wt(next_unit(), (2, 512))
                    pe.wait_ge(*at("qn_ready"))
                    for h in range(2):
                        for k in range(2):
                            last = product(wk[:, 0, h * S:(h + 1) * S], [t[:, k, h * 256:h * 256 + P] for t in w],
                                           [t[:, k, :] for t in (cT_hi, cT_lo)], start=k == 0, stop=k == 1)
                    last.then_inc(sems["kn_done"], 1)
                    return [t.rearrange("p k (h n) -> p k h n", h=2)[:, :, :, P:2 * P] for t in w]

                def values(w):
                    pe.wait_ge(*at("qr_ready"))
                    for tb in range(TB):
                        for k in range(2):
                            last = product(wk[:, 1, tb * S:(tb + 1) * S],
                                           [t[:, k, tb * P:(tb + 1) * P] for t in (cT_hi, cT_lo)],
                                           [t[:, k] for t in w], start=k == 0, stop=k == 1)
                    done(last)

                def body(j):
                    more = not is_at(j, B_HEADS // 2 - 1)
                    pe.wait_ge(*at("kn_ready"))
                    if not is_at(j, 0):
                        pe.wait_ge(*at("hidden_hi"))
                        pe.wait_ge(*at("hidden_lo"))
                    for h in range(2):
                        for tb in range(TB):
                            nk = (tb + 1) * P
                            o = wk[:, 2 + h, tb * P:tb * P + nk]
                            whole(o, q_sb[:, h, tb * P:(tb + 1) * P], k_sb[:, h, 0:nk], True, False)
                            last = whole(o, rot2[:, 0, tb * P:(tb + 1) * P], krz[:, h, 0:nk], False, True)
                    last.then_inc(sems["scores_done"], 1)
                    if not is_at(j, 0):
                        close(2, is_at(j, 1))
                    pe.wait_ge(*at("v_ready"))
                    if more:
                        queries()
                    softmax_turn()
                    if more:
                        rotate()
                        vw = keys()
                    softmax_turned()
                    for h in range(2):
                        whole(wk[:, 2, h * S:(h + 1) * S], v_sb[:, 0, h * P:(h + 1) * P], probT[:, h, 0:S], True, False)
                        last = whole(wk[:, 2, h * S + P:(h + 1) * S], v_sb[:, 1, h * P:(h + 1) * P],
                                     probT[:, h, S:SEG], False, True)
                    last.then_inc(sems["attn_done"], 1)
                    if more:
                        values(vw)

                queries()
                rotate()
                values(keys())
                at.pipeline(pe, body, B_HEADS // 2)
                pe.wait_ge(*at("hidden_hi"))
                pe.wait_ge(*at("hidden_lo"))
                close(2, False)

            def branch(kind, layer):
                def queries_keys():
                    w = wt(next_unit(), (KD, 2 * P))
                    for c in range(2):
                        for k in range(KD):
                            last = product(wk[:, 0, c * S:(c + 1) * S], [t[:, k, c * P:(c + 1) * P] for t in w],
                                           [t[:, k, :] for t in (fT_hi, fT_lo)], start=k == 0, stop=k == KD - 1)
                    done(last)

                def values():
                    w = wt(next_unit(), (KD, P))
                    for tb in range(TB):
                        for k in range(KD):
                            last = product(wk[:, 1, tb * P:(tb + 1) * P],
                                           [t[:, k, tb * P:(tb + 1) * P] for t in (fT_hi, fT_lo)],
                                           [t[:, k, :] for t in w], start=k == 0, stop=k == KD - 1)
                    done(last)

                def attend():
                    for h in range(2):
                        whole(wk[:, 1, S:2 * S], vz[:, 0, h, :], probT[:, h, 0:S], h == 0, False)
                        last = whole(wk[:, 1, S + P:2 * S], vz[:, 1, h, :], probT[:, h, S:SEG], False, h == 1)
                    last.then_inc(sems["attn_done"], 1)

                def close_before(j):
                    pe.wait_ge(*at("hidden_hi"))
                    pe.wait_ge(*at("hidden_lo"))
                    if kind == "moba" and is_at(j, 1):
                        pe.wait_ge(*at("branch_ready", 4))
                    close(1, is_at(j, 1))

                def body_sb(j):
                    more = not is_at(j, C_HEADS // 2 - 1)
                    pe.wait_ge(*at("qk_ready", 3))
                    for h in range(2):
                        whole(wk[:, 2 + h, 0:S], kz[:, h, 0:P], q_sb[:, 0, :], True, True)
                        last = whole(wk[:, 2 + h, S:SEG], kz[:, h, P:S], q_sb[:, 0, P:S], True, True)
                    last.then_inc(sems["z_done"], 1)
                    if not is_at(j, 0):
                        close_before(j)
                    if more:
                        queries_keys()
                    pe.wait_ge(*at("keep_ready"))
                    for h in range(2):
                        whole(wk[:, 2 + h, 0:S], kcol("later"), keep[:, h, 0:S], True, False)
                        whole(wk[:, 2 + h, P:S], kcol("ones")[:, 0:P], keep[:, h, S:SEG], False, True)
                        last = whole(wk[:, 2 + h, S:SEG], kcol("later"), keep[:, h, S:SEG], True, True)
                    last.then_inc(sems["suffix_done"], 1)
                    pe.wait_ge(*at("v_ready", 2))
                    if more:
                        values()
                    pe.wait_ge(*at("weight_ready"))
                    attend()

                def rotate():
                    pe.wait_ge(*at("qr_raw_ready"))
                    whole(wk[:, 0, :].rearrange("p (a n) -> p a n", a=2), kcol("rotate_moba"), rot1[:, :, :],
                          True, True).then_inc(sems["qr_rotated"], 1)

                def body_moba(j):
                    more = not is_at(j, C_HEADS // 2 - 1)
                    pe.wait_ge(*at("qk_roped", 3))
                    for h in range(2):
                        for tb in range(TB):
                            nk = (tb + 1) * P
                            last = whole(wk[:, 2 + h, tb * P:tb * P + nk], q_sb[:, 0, tb * P:(tb + 1) * P],
                                         kz[:, h, 0:nk], True, True)
                    last.then_inc(sems["scores_done"], 1)
                    if not is_at(j, 0):
                        close_before(j)
                    if more:
                        queries_keys()
                    softmax_turn()
                    pe.wait_ge(*at("v_ready", 2))
                    if more:
                        rotate()
                        values()
                    softmax_turned()
                    attend()

                queries_keys()
                if kind == "moba":
                    rotate()
                values()
                at.pipeline(pe, body_sb if kind == "sb" else body_moba, C_HEADS // 2)
                close_before(C_HEADS // 2)

            def merge(layer):
                for q in range(4):
                    bank = 2 * (q % 2)
                    if q >= 2:
                        pe.wait_ge(*at("gate_ready", 2))
                    for k0 in (0, 4):
                        w = wt(next_unit(), (4, 512))
                        for tb in range(TB):
                            for k in range(4):
                                last = product(wk[:, bank + tb, :],
                                               [t[:, k0 + k, tb * P:(tb + 1) * P] for t in (fT_hi, fT_lo)],
                                               [t[:, k, :] for t in w], start=k0 + k == 0, stop=k0 + k == KD - 1)
                        done(last)
                pe.wait_ge(*at("gate_ready", 4))
                turn(tok, KD, (0, 1, 2, 3))
                for c in range(4):
                    w = wt(next_unit(), (2, D))
                    for k in range(2):
                        for tb in range(TB):
                            for half in range(2):
                                last = product(acc[:, 2 * tb + half, :],
                                               [t[:, 2 * c + k, tb * P:(tb + 1) * P] for t in (fT_hi, fT_lo)],
                                               [t[:, k, half * 512:(half + 1) * 512] for t in w],
                                               start=c + k == 0, stop=c == 3 and k == 1)
                    done(last)

            none = lambda *a: None
            network(Stages(setup=setup, norm=norm, ffn=ffn, hgrn=hgrn, mla=mla, ple=ple, latent=latent,
                                    final_norm=none, turn_residual=turn_residual, branch=branch, merge=merge,
                                    layer_norm=none, finish=none))

        @block.scalar
        def _(act):
            at = Follow(sems)
            total = n_units[0]

            def seq(ins):
                ins.then_inc(sems["act_step"], 1)
                act.wait_ge(*at("act_step"))

            def split():
                n = at.n.get("unit", 0)
                if n >= total:
                    return
                at.n["unit"] = n + 1
                slot, size = n % RING, UNITS[n]
                act.wait_ge(*at(f"landed{slot}", 16))
                act.copy(w_hi[:, slot, 0:size], raw[:, slot, 0:size]).then_inc(sems["hi_ready"], 1)

            def unit_done():
                act.wait_ge(*at("unit_done"))

            def upper(dst, src, scale=None):
                if scale is None:
                    return act.copy(dst, src)
                return act.activation(dst, src, ACT.Copy, scale=scale)

            def setup():
                for _ in range(RING):
                    split()
                act.wait_ge(*at("gains_turned"))
                act.copy(gains[:, :], wk[:, 0, 0:N_GAINS]).then_inc(sems["gains_ready"], 1)
                act.wait_ge(*at("bounds_in_ready"))
                act.activation(lower[:, 0:2, :], lower[:, 0:2, :], ACT.Exp).then_inc(sems["bounds_exp"], 1)
                act.wait_ge(*at("angle_ready"))
                act.activation(mla_sin[:, :], ang[:, 2, :], ACT.Sin).then_inc(sems["sin_ready"], 1)
                act.activation(mla_cos[:, :], ang[:, 3, :], ACT.Sin).then_inc(sems["sin_ready"], 1)

            def deviation(n, eps):
                act.wait_ge(*at("square_ready"))
                act.activation(stat[:, 2:2 + n], stat[:, 0:n], ACT.Sqrt, bias=eps_sb[:, eps:eps + 1])\
                    .then_inc(sems["deviation_ready"], 1)

            def turn(nf, banks, hi, name=None, c0=0):
                for b in range(nf // 2):
                    act.wait_ge(*at("turned"))
                    if name is None:
                        act.copy(hi[:, 2 * b:2 * b + 2, :], wk[:, banks[b], :].rearrange("p (f n) -> p f n", f=2))\
                            .then_inc(sems["features_hi"], 1)
                        continue
                    for f in range(2):
                        last = upper(hi[:, 2 * b + f, :], wk[:, banks[b], f * S:(f + 1) * S],
                                     gcol(name, c0 + 2 * b + f))
                    last.then_inc(sems["features_hi"], 1)

            def norm(name, c0):
                deviation(TB, 0)
                turn(KD, (0, 1, 2, 3), fT_hi, name, c0)

            def turn_residual():
                turn(KD, (0, 1, 2, 3), fT_hi)

            def layer_norm(n):
                deviation(TB, 1)

            def final_norm():
                deviation(TB, 0)

            def hidden(src, nk=2, scale=None):
                upper(hT_hi[:, 0:nk, :], src.rearrange("p (f n) -> p f n", f=nk), scale)\
                    .then_inc(sems["hidden_hi"], 1)

            def ffn(second, last=False):
                def gate():
                    act.wait_ge(*at("gate_up_done"))
                    act.activation(silu[:, 0, :], wk[:, 0, 0:FC], ACT.Silu).then_inc(sems["silu_ready"], 1)
                    unit_done()
                    act.activation(silu[:, 1, :], wk[:, 1, 0:FC], ACT.Silu).then_inc(sems["silu_ready"], 1)
                    split()

                def body(j):
                    unit_done()
                    act.wait_ge(*at("hidden_turned"))
                    hidden(wk[:, 2, :])
                    split()
                    gate()
                    unit_done()
                    split()

                unit_done()
                split()
                gate()
                at.repeat(act, body, 1, NFF, peel_last=True)
                act.wait_ge(*at("hidden_turned"))
                hidden(wk[:, 2, :])
                unit_done()
                split()

            def hgrn():
                def forget():
                    act.wait_ge(*at("forget_done"))
                    act.activation(f_sb[:, 0, :], wk[:, 0, S:2 * S], ACT.Sigmoid).then_inc(sems["sigmoids_ready"], 1)
                    act.activation(f_sb[:, 1, :], wk[:, 0, S:2 * S], ACT.Sigmoid, scale=-1.0)\
                        .then_inc(sems["sigmoids_ready"], 1)

                def logarithms():
                    act.wait_ge(*at("forget_ready"))
                    act.activation(lg_sb[:, :], f_sb[:, 0, :], ACT.Ln).then_inc(sems["log_ready"], 1)

                def queries():
                    unit_done()
                    act.activation(q_sb[:, 0, :], wk[:, 0, 0:S], ACT.Copy, scale=A_DIM ** -0.5)\
                        .then_inc(sems["q_ready"], 1)
                    split()

                def decays():
                    act.wait_ge(*at("decay_in_ready"))
                    act.activation(levels[:, :, :], levels[:, :, :], ACT.Exp).then_inc(sems["decay_ready"], 1)

                def inputs():
                    unit_done()
                    act.copy(v_sb[:, :, 0:P], wk[:, 1, :].rearrange("p (t n) -> p t n", t=TB)[:, :, 0:P])\
                        .then_inc(sems["v_ready"], 1)
                    split()

                def out_gates():
                    act.activation(sg_sb[:, :, 0:P], wk[:, 1, :].rearrange("p (t n) -> p t n", t=TB)[:, :, P:2 * P],
                                   ACT.Sigmoid).then_inc(sems["out_gate_ready"], 1)

                def body(h):
                    more = not is_at(h, A_HEADS - 1)
                    act.wait_ge(*at("cross_done"))
                    act.copy(cross[:, :], wk[:, 1, 0:P]).then_inc(sems["cross_ready"], 1)
                    if not is_at(h, 0):
                        unit_done()
                        split()
                    if more:
                        forget()
                        logarithms()
                        queries()
                    act.wait_ge(*at("o_done"))
                    for tb in range(TB):
                        last = act.activation(rot1[:, tb, 0:P], wk[:, 2, tb * P:(tb + 1) * P], ACT.Square,
                                              scale=A_DIM ** -0.5, accum_out=stat[:, tb:tb + 1])
                    seq(last)
                    seq(act.activation(stat[:, 2:4], stat[:, 0:2], ACT.Ln, bias=eps_sb[:, 0:1]))
                    act.activation(stat[:, 4:6], stat[:, 2:4], ACT.Exp, scale=-0.5)\
                        .then_inc(sems["o_dev_ready"], 1)
                    if more:
                        decays()
                        inputs()
                    act.wait_ge(*at("hidden_turned"))
                    hidden(wk[:, 3, 0:S], 1, gcol("a_out_gain"))
                    if more:
                        out_gates()

                forget()
                logarithms()
                queries()
                decays()
                inputs()
                out_gates()
                at.pipeline(act, body, A_HEADS)
                unit_done()
                split()

            def ple(layer):
                act.wait_ge(*at("p_turned"))
                act.copy(pT_hi[:, :, :], wk[:, 2, :].rearrange("p (f n) -> p f n", f=2)).then_inc(sems["p_hi"], 1)
                for c in range(4):
                    unit_done()
                    if c == 3:
                        for b in range(4):
                            act.activation(gate_sb[:, b // 2, (b % 2) * 512:(b % 2 + 1) * 512], acc[:, b, :],
                                           ACT.Sigmoid).then_inc(sems["ple_gate_ready"], 1)
                    split()
                unit_done()
                split()

            def latent():
                unit_done()
                split()
                unit_done()
                act.copy(kr_raw[:, :], wk[:, 1, 0:S]).then_inc(sems["kr_raw_ready"], 1)
                deviation(TB, 0)
                split()
                turn(2, (2,), cT_hi, "kv_latent_norm")

            def softmax(scale):
                act.wait_ge(*at("max_ready"))
                for h in range(2):
                    for seg, (a, b) in enumerate(((0, P), (P, SEG))):
                        c = 2 * seg + h
                        last = act.activation(prob[:, h, a:b], sc[:, h, a:b], ACT.Exp, bias=stat[:, 4 + c:5 + c],
                                              scale=scale, accum_out=stat[:, 8 + c:9 + c])
                last.then_inc(sems["exp_ready"], 1)

            def first_probs():
                act.wait_ge(*at("probs_turned"))
                act.copy(probT[:, 0, :], wk[:, 2, 0:SEG]).then_inc(sems["probsT0_ready"], 1)
                at("probs_turned")

            def mla():
                unit_done()
                split()
                unit_done()
                deviation(TB, 0)
                split()
                turn(4, (2, 3), fT_hi, "b_q_norm")

                def queries():
                    unit_done()
                    act.copy(qr_sb[:, :], wk[:, 1, 0:S]).then_inc(sems["qr_raw_ready"], 1)
                    act.copy(q_sb[:, :, :], wk[:, 0, :].rearrange("p (h n) -> p h n", h=2))\
                        .then_inc(sems["qn_ready"], 1)

                def keys():
                    act.wait_ge(*at("kn_done"))
                    act.copy(k_sb[:, :, :], wk[:, 0, :].rearrange("p (h n) -> p h n", h=2))\
                        .then_inc(sems["kn_ready"], 1)

                def body(j):
                    more = not is_at(j, B_HEADS // 2 - 1)
                    softmax((B_NOPE + B_ROPE) ** -0.5)
                    if not is_at(j, 0):
                        unit_done()
                        split()
                    if more:
                        queries()
                    first_probs()
                    if more:
                        split()
                        keys()
                    act.wait_ge(*at("attn_done"))
                    hidden(wk[:, 2, :])
                    if more:
                        unit_done()
                        split()

                queries()
                split()
                keys()
                unit_done()
                split()
                at.pipeline(act, body, B_HEADS // 2)
                unit_done()
                split()

            def branch(kind, layer):
                scale = C_DIM ** -0.5

                def queries_keys():
                    unit_done()
                    if kind == "moba":
                        act.copy(rot1[:, :, :], wk[:, 0, :].rearrange("p (a n) -> p a n", a=2))\
                            .then_inc(sems["qr_raw_ready"], 1)
                        return
                    act.copy(q_sb[:, 0, :], wk[:, 0, 0:S]).then_inc(sems["qk_ready"], 1)
                    for h in range(2):
                        r = slice(h * C_DIM, (h + 1) * C_DIM)
                        act.copy(kz[r, h, :], wk[r, 0, S:2 * S]).then_inc(sems["qk_ready"], 1)

                def body_sb(j):
                    more = not is_at(j, C_HEADS // 2 - 1)
                    act.wait_ge(*at("z_done"))
                    act.activation(sc[:, :, :], wk[:, 2:4, 0:SEG], ACT.Abs).then_inc(sems["abs_ready"], 1)
                    act.wait_ge(*at("abs_ready"))
                    seq(act.activation(sc[:, :, :], sc[:, :, :], ACT.Exp, scale=-scale))
                    act.activation(soft[:, :, :], sc[:, :, :], ACT.Ln, bias=1.0).then_inc(sems["softplus_ready"], 1)
                    if not is_at(j, 0):
                        unit_done()
                        split()
                    if more:
                        queries_keys()
                        split()
                    act.wait_ge(*at("weight_in_ready"))
                    act.activation(soft[:, :, :], sc[:, :, :], ACT.Exp).then_inc(sems["weight_exp"], 1)
                    if more:
                        unit_done()
                        split()
                    act.wait_ge(*at("attn_done"))
                    hidden(wk[:, 1, S:2 * S], 1)

                def body_moba(j):
                    more = not is_at(j, C_HEADS // 2 - 1)
                    softmax(scale)
                    if not is_at(j, 0):
                        unit_done()
                        split()
                    if more:
                        queries_keys()
                    first_probs()
                    if more:
                        split()
                        unit_done()
                        split()
                    act.wait_ge(*at("attn_done"))
                    hidden(wk[:, 1, S:2 * S], 1)

                if kind == "sb" and layer == 0:
                    act.wait_ge(*at("zeros_ready", 3))
                queries_keys()
                split()
                unit_done()
                split()
                at.pipeline(act, body_sb if kind == "sb" else body_moba, C_HEADS // 2)
                unit_done()
                split()
                if kind == "sb":
                    for b in range(4):
                        act.copy(gate_sb[:, b // 2, (b % 2) * 512:(b % 2 + 1) * 512], acc[:, b, :])\
                            .then_inc(sems["branch_ready"], 1)

            def merge(layer):
                for q in range(4):
                    unit_done()
                    split()
                    unit_done()
                    if q >= 2:
                        act.wait_ge(*at("gate_used", 2))
                    for tb in range(TB):
                        act.activation(gates4[:, 2 * (q % 2) + tb, :], wk[:, 2 * (q % 2) + tb, :], ACT.Sigmoid)\
                            .then_inc(sems["gate_ready"], 1)
                    split()
                at("gate_used", 4)
                turn(KD, (0, 1, 2, 3), fT_hi)
                for _ in range(4):
                    unit_done()
                    split()

            none = lambda *a: None
            network(Stages(setup=setup, norm=norm, ffn=ffn, hgrn=hgrn, mla=mla, ple=ple, latent=latent,
                                    final_norm=final_norm, turn_residual=turn_residual, branch=branch,
                                    merge=merge, layer_norm=layer_norm, finish=none))

        @block.gpsimd
        def _(pool):
            for t in (kz, vz, krz):
                pool.memset(t[:], 0.0).then_inc(sems["zeros_ready"], 1)

        @block.vector
        def _(dve):
            at = Follow(sems)
            total = n_units[0]

            def seq(ins):
                ins.then_inc(sems["dve_step"], 1)
                dve.wait_ge(*at("dve_step"))

            def split():
                n = at.n.get("unit", 0)
                if n >= total:
                    return
                at.n["unit"] = n + 1
                slot, size = n % RING, UNITS[n]
                dve.wait_ge(*at("hi_ready"))
                dve.tensor_tensor(w_lo[:, slot, 0:size], raw[:, slot, 0:size], w_hi[:, slot, 0:size].bitcast(F32),
                                  ALU.subtract)\
                    .then_inc(sems["lo_ready"], 1)

            def unit_done():
                dve.wait_ge(*at("unit_done"))

            def lower_part(lo, src, hi, scale=None):
                hi = hi.bitcast(F32)
                if scale is None:
                    return dve.tensor_tensor(lo, src, hi, ALU.subtract)
                return dve.scalar_tensor_tensor(lo, src, scale, hi, ALU.mult, ALU.subtract)

            def setup():
                dve.memset(eps_sb[:, 0:1], EPS)
                dve.memset(eps_sb[:, 1:2], LN_EPS)
                dve.memset(eps_sb[:, 2:3], 1.0)
                dve.memset(eps_sb[:, 3:4], 0.0).then_inc(sems["dve_step"], 1)
                dve.wait_ge(*at("dve_step"))
                for _ in range(RING):
                    split()
                dve.wait_ge(*at("gains_ready"))
                c = GAIN_AT["a_lb_logits"]
                l0, l1 = gains[:, c:c + 8], gains[:, c + 8:c + 16]
                seq(dve.tensor_tensor(lower[:, 2, :], l0, l1, ALU.max))
                dve.tensor_tensor(lower[:, 0, :], l0, lower[:, 2, :], ALU.subtract)
                dve.tensor_tensor(lower[:, 1, :], l1, lower[:, 2, :], ALU.subtract)\
                    .then_inc(sems["bounds_in_ready"], 1)
                dve.wait_ge(*at("bounds_exp"))
                seq(dve.tensor_tensor(lower[:, 2, :], lower[:, 0, :], lower[:, 1, :], ALU.add))
                seq(dve.reciprocal(lower[:, 3, :], lower[:, 2, :]))
                seq(dve.tensor_tensor(lower[:, 2, :], lower[:, 0, :], lower[:, 3, :], ALU.mult))
                seq(dve.tensor_scalar(lower[:, 3, :], lower[:, 2, :], -1.0, 1.0, ALU.mult, ALU.add))
                dve.wait_ge(*at("pos_landed", 16))
                dve.wait_ge(*at("const_landed", 16))
                seq(dve.tensor_copy(ang[:, 0, :], pos_i[:, :]))
                seq(dve.tensor_scalar(ang[:, 1, :], ang[:, 0, :], kcol("inv_freq"), None, ALU.mult))
                seq(dve.tensor_scalar(ang[:, 0, :], ang[:, 1, :], 1.0 / TWO_PI, MAGIC, ALU.mult, ALU.add))
                seq(dve.tensor_scalar(ang[:, 0, :], ang[:, 0, :], MAGIC, None, ALU.subtract))
                for part in (PI_HI, PI_MID, PI_LO):
                    seq(dve.scalar_tensor_tensor(ang[:, 1, :], ang[:, 0, :], -part, ang[:, 1, :], ALU.mult, ALU.add))
                pi = float(np.nextafter(np.float32(np.pi), np.float32(0)))
                seq(dve.tensor_scalar(ang[:, 2, :], ang[:, 1, :], pi, -pi, ALU.min, ALU.max))
                seq(dve.tensor_scalar(ang[:, 0, :], ang[:, 2, :], np.pi / 2, -TWO_PI, ALU.is_gt, ALU.mult))
                seq(dve.scalar_tensor_tensor(ang[:, 3, :], ang[:, 2, :], np.pi / 2, ang[:, 0, :], ALU.add, ALU.add))
                dve.tensor_scalar(ang[:, 3, :], ang[:, 3, :], pi, -pi, ALU.min, ALU.max)\
                    .then_inc(sems["angle_ready"], 1)
                dve.wait_ge(*at("x_landed", 16))

            def squares(src, n):
                for tb in range(TB):
                    last = dve.tensor_tensor_reduce(gate_sb[:, tb, 0:n], src(tb), src(tb), 1.0 / n, 0.0,
                                                    ALU.mult, ALU.add, stat[:, tb:tb + 1])
                last.then_inc(sems["square_ready"], 1)
                dve.wait_ge(*at("deviation_ready"))
                seq(dve.reciprocal(stat[:, 4:6], stat[:, 2:4]))

            def scaled(src, n, banks=False):
                if banks:
                    for tb in range(TB):
                        last = dve.tensor_copy(tok[:, tb, 0:n], src(tb))
                    seq(last)
                    src = lambda tb: tok[:, tb, 0:n]
                squares(src, n)
                for tb in range(TB):
                    dve.tensor_scalar(tok[:, tb, 0:n], src(tb), stat[:, 4 + tb:5 + tb], None, ALU.mult)\
                        .then_inc(sems["tokens_ready"], 1)

            def turn(nf, banks, hi, lo, name=None, c0=0):
                for b in range(nf // 2):
                    dve.wait_ge(*at("features_hi"))
                    if name is None:
                        lower_part(lo[:, 2 * b:2 * b + 2, :], wk[:, banks[b], :].rearrange("p (f n) -> p f n", f=2),
                                   hi[:, 2 * b:2 * b + 2, :]).then_inc(sems["features_lo"], 1)
                        continue
                    for f in range(2):
                        last = lower_part(lo[:, 2 * b + f, :], wk[:, banks[b], f * S:(f + 1) * S],
                                          hi[:, 2 * b + f, :], gcol(name, c0 + 2 * b + f))
                    last.then_inc(sems["features_lo"], 1)

            def norm(name, c0):
                scaled(lambda tb: res[:, tb, :], D)
                turn(KD, (0, 1, 2, 3), fT_hi, fT_lo, name, c0)

            def turn_residual():
                turn(KD, (0, 1, 2, 3), fT_hi, fT_lo)

            def norm_row(n):
                dve.wait_ge(*at(f"norm_rows{n % 2}_landed", 32))

            def final_norm():
                squares(lambda tb: res[:, tb, :], D)
                norm_row(0)
                for tb in range(TB):
                    last = dve.scalar_tensor_tensor(res[:, tb, :], res[:, tb, :], stat[:, 4 + tb:5 + tb],
                                                    norm_g[:, 0, :], ALU.mult, ALU.mult)
                    last.then_inc(sems["tokens_ready"], 1)
                seq(dve.tensor_copy(stat[:, 0:1], stat[:, 1:2]))
                dve.tensor_copy(stat[:, 0:1], stat[:, 1:2]).then_inc(sems["norm_rows_used"], 1)

            def layer_norm(n):
                for tb in range(TB):
                    for half in range(2):
                        last = dve.bn_stats(bn[:, tb, half, :], res[:, tb, half * 512:(half + 1) * 512])
                seq(last)
                for tb in range(TB):
                    last = dve.bn_aggr(mv[:, tb, :], bn[:, tb, :, :])
                seq(last)
                dve.tensor_copy(stat[:, 0:2], mv[:, :, 1]).then_inc(sems["square_ready"], 1)
                dve.wait_ge(*at("deviation_ready"))
                seq(dve.reciprocal(stat[:, 4:6], stat[:, 2:4]))
                norm_row(n + 1)
                for tb in range(TB):
                    last = dve.tensor_scalar(res[:, tb, :], res[:, tb, :], mv[:, tb, 0:1], stat[:, 4 + tb:5 + tb],
                                             ALU.subtract, ALU.mult)
                seq(last)
                for tb in range(TB):
                    last = dve.tensor_tensor(res[:, tb, :], res[:, tb, :], norm_g[:, (n + 1) % 2, :], ALU.mult)
                seq(last)
                for tb in range(TB):
                    last = dve.tensor_tensor(res[:, tb, :], res[:, tb, :], norm_b[:, (n + 1) % 2, :], ALU.add)
                    last.then_inc(sems["out_ready" if n == 3 and tb else "tokens_ready"], 1)
                if n < 3:
                    dve.tensor_copy(stat[:, 0:1], stat[:, 1:2]).then_inc(sems["norm_rows_used"], 1)

            def residual(second, scale=1.0):
                for b in range(4):
                    r = res[:, b // 2, (b % 2) * 512:(b % 2 + 1) * 512]
                    if second:
                        last = dve.scalar_tensor_tensor(r, r, ALPHA, acc[:, b, :], ALU.mult, ALU.add)
                    else:
                        last = dve.scalar_tensor_tensor(r, acc[:, b, :], scale, r, ALU.mult, ALU.add)
                seq(last)

            def hidden(src, nk=2, scale=None):
                dve.wait_ge(*at("hidden_hi"))
                lower_part(hT_lo[:, 0:nk, :], src.rearrange("p (f n) -> p f n", f=nk), hT_hi[:, 0:nk, :], scale)\
                    .then_inc(sems["hidden_lo"], 1)

            def ffn(second, last=False):
                def gate():
                    for tb in range(TB):
                        dve.wait_ge(*at("silu_ready"))
                        dve.tensor_tensor(hid[:, tb, :], silu[:, tb, :], wk[:, tb, FC:2 * FC], ALU.mult)\
                            .then_inc(sems["hidden_ready"], 1)
                    unit_done()
                    split()

                def body(j):
                    unit_done()
                    hidden(wk[:, 2, :])
                    split()
                    gate()
                    unit_done()
                    split()

                unit_done()
                split()
                gate()
                at.repeat(dve, body, 1, NFF, peel_last=True)
                hidden(wk[:, 2, :])
                unit_done()
                residual(second, 0.5)
                split()

            def hgrn():
                def halves(t, m):
                    v = t.rearrange("p (n a m) -> p n a m", a=2, m=m)
                    return v[:, :, 0, :], v[:, :, 1, :]

                def forget(h):
                    dve.wait_ge(*at("sigmoids_ready", 2))
                    one_minus = lower[:, 3, bass.ds(h, 1)]
                    seq(dve.tensor_scalar(f_sb[:, 0, :], f_sb[:, 0, :], one_minus, lower[:, 2, bass.ds(h, 1)],
                                          ALU.mult, ALU.add))
                    dve.tensor_scalar(f_sb[:, 0, :], f_sb[:, 0, :], LN_FLOOR, None, ALU.max)\
                        .then_inc(sems["forget_ready"], 1)
                    dve.tensor_scalar(k_sb[:, 0, :], f_sb[:, 1, :], one_minus, None, ALU.mult)

                def queries():
                    unit_done()
                    split()

                def decays():
                    dve.wait_ge(*at("log_ready"))
                    dve.tensor_tensor_scan(b64[:, :], kcol("restart"), lg_sb[:, :], 0.0, ALU.mult, ALU.add)
                    seq(dve.tensor_tensor_scan(b256[:, :], kcol("ones"), lg_sb[:, :], 0.0, ALU.mult, ALU.add))
                    for n in range(LEVELS):
                        m = 1 << n
                        first, second = halves((b64 if m < 64 else b256)[:, :], m)
                        e_first, e_second = halves(levels[:, n, :], m)
                        ref = first[:, :, m - 1:m].to_broadcast([P, S // (2 * m), m])
                        dve.tensor_tensor(e_first, ref, first, ALU.subtract)
                        last = dve.tensor_tensor(e_second, second, ref, ALU.subtract)
                    last.then_inc(sems["decay_in_ready"], 1)

                def decayed():
                    dve.wait_ge(*at("decay_ready"))
                    dve.wait_ge(*at("q_ready"))
                    for n in range(LEVELS):
                        m = 1 << n
                        e_first, e_second = halves(levels[:, n, :], m)
                        dve.tensor_tensor(e_first, e_first, halves(k_sb[:, 0, :], m)[0], ALU.mult)
                        last = dve.tensor_tensor(e_second, e_second, halves(q_sb[:, 0, :], m)[1], ALU.mult)
                    last.then_inc(sems["level_in_ready"], 1)

                def merge_scores(r):
                    dve.wait_ge(*at("level_done"))
                    for i in range(2):
                        n = 2 * r + i
                        mask = tile2(kcol("levels")[:, n * P:(n + 1) * P])
                        got = wk[:, 2 + r % 2, i * 2 * P:(i + 1) * 2 * P].rearrange("p (t n) -> p t n", t=TB)
                        if n == 0:
                            seq(dve.tensor_tensor(at_sb[:, :, :], got, mask, ALU.mult))
                            continue
                        dve.memset(eps_sb[:, 3:4], 0.0)
                        ins = dve.copy_predicated(at_sb[:, :, :], mask.bitcast(U32), got)
                        if i == 0:
                            seq(ins)
                        else:
                            ins.then_inc(sems["level_merged"], 1)
                            dve.wait_ge(*at("level_merged"))

                def body(h):
                    more = not is_at(h, A_HEADS - 1)
                    merge_scores(0)
                    merge_scores(1)
                    if not is_at(h, 0):
                        unit_done()
                        split()
                    if more:
                        forget(h + 1)
                    merge_scores(2)
                    merge_scores(3)
                    if more:
                        decays()
                        queries()
                    dve.wait_ge(*at("o_dev_ready"))
                    for tb in range(TB):
                        dve.scalar_tensor_tensor(hid[:, tb, 0:P], wk[:, 2, tb * P:(tb + 1) * P],
                                                 stat[:, 4 + tb:5 + tb], sg_sb[:, tb, 0:P], ALU.mult, ALU.mult)\
                            .then_inc(sems["o_gated"], 1)
                    if more:
                        decayed()
                        unit_done()
                        split()
                    hidden(wk[:, 3, 0:S], 1, gcol("a_out_gain"))

                forget(0)
                queries()
                decays()
                decayed()
                unit_done()
                split()
                at.pipeline(dve, body, A_HEADS)
                unit_done()
                split()
                residual(0)

            def ple(layer):
                dve.wait_ge(*at("p_hi"))
                lower_part(pT_lo[:, :, :], wk[:, 2, :].rearrange("p (f n) -> p f n", f=2), pT_hi[:, :, :])\
                    .then_inc(sems["p_lo"], 1)
                for c in range(4):
                    unit_done()
                    split()
                unit_done()
                dve.wait_ge(*at("ple_gate_ready", 4))
                for b in range(4):
                    g = gate_sb[:, b // 2, (b % 2) * 512:(b % 2 + 1) * 512]
                    last = dve.tensor_tensor(g, g, wk[:, b, :], ALU.mult)
                seq(last)
                for tb in range(TB):
                    last = dve.tensor_tensor(res[:, tb, :], res[:, tb, :], gate_sb[:, tb, :], ALU.add)
                seq(last)
                split()

            def latent():
                unit_done()
                split()
                unit_done()
                scaled(lambda tb: wk[:, 0, tb * S:(tb + 1) * S], B_KV, banks=True)
                dve.wait_ge(*at("sin_ready", 2))
                dve.wait_ge(*at("zeros_ready", 3))
                dve.wait_ge(*at("kr_raw_ready"))
                dve.tensor_tensor(rot1[:, 0, :], kr_raw[:, :], mla_cos[:, :], ALU.mult)
                dve.wait_ge(*at("kr_rotated"))
                seq(dve.tensor_tensor(rot1[:, 1, :], wk[:, 1, S:2 * S], mla_sin[:, :], ALU.mult))
                for h in range(2):
                    r = slice(h * B_ROPE, (h + 1) * B_ROPE)
                    last = dve.tensor_tensor(krz[r, h, :], rot1[r, 0, :], rot1[r, 1, :], ALU.add)
                last.then_inc(sems["kr_ready"], 1)
                turn(2, (2,), cT_hi, cT_lo, "kv_latent_norm")
                split()

            def softmax(scale):
                dve.wait_ge(*at("scores_done"))
                seq(dve.tensor_tensor(sc[:, :, :], wk[:, 2:4, 0:SEG], tile2(kcol("causal")), ALU.add))
                dve.tensor_reduce(stat[:, 0:2], sc[:, :, 0:P], AX.X, ALU.max)
                seq(dve.tensor_reduce(stat[:, 2:4], sc[:, :, P:SEG], AX.X, ALU.max))
                dve.tensor_scalar(stat[:, 4:8], stat[:, 0:4], -scale, None, ALU.mult).then_inc(sems["max_ready"], 1)
                dve.wait_ge(*at("exp_ready"))
                seq(dve.reciprocal(stat[:, 12:16], stat[:, 8:12]))
                for h in range(2):
                    for seg, (a, b) in enumerate(((0, P), (P, SEG))):
                        c = 12 + 2 * seg + h
                        dve.tensor_scalar(prob[:, h, a:b], prob[:, h, a:b], stat[:, c:c + 1], None, ALU.mult)\
                            .then_inc(sems["probs_ready"], 1)

            def second_probs():
                dve.wait_ge(*at("probs_turned", 2))
                dve.tensor_copy(probT[:, 1, :], wk[:, 3, 0:SEG]).then_inc(sems["probsT1_ready"], 1)

            def mla():
                unit_done()
                split()
                unit_done()
                scaled(lambda tb: wk[:, tb, :], B_Q, banks=True)
                split()
                turn(4, (2, 3), fT_hi, fT_lo, "b_q_norm")

                def rotate():
                    unit_done()
                    dve.wait_ge(*at("qr_raw_ready"))
                    dve.tensor_tensor(rot1[:, 0, :], qr_sb[:, :], mla_cos[:, :], ALU.mult)

                def rotated():
                    dve.wait_ge(*at("qr_rotated"))
                    seq(dve.tensor_tensor(rot1[:, 1, :], wk[:, 1, S:2 * S], mla_sin[:, :], ALU.mult))
                    dve.tensor_tensor(rot2[:, 0, :], rot1[:, 0, :], rot1[:, 1, :], ALU.add)\
                        .then_inc(sems["qr_ready"], 1)
                    split()

                def values():
                    unit_done()
                    dve.tensor_copy(v_sb[:, :, :], wk[:, 1, :].rearrange("p (t n) -> p t n", t=TB))\
                        .then_inc(sems["v_ready"], 1)
                    split()

                def body(j):
                    more = not is_at(j, B_HEADS // 2 - 1)
                    softmax((B_NOPE + B_ROPE) ** -0.5)
                    if not is_at(j, 0):
                        unit_done()
                        split()
                    if more:
                        rotate()
                    second_probs()
                    if more:
                        rotated()
                    hidden(wk[:, 2, :])
                    if more:
                        values()

                rotate()
                rotated()
                values()
                at.pipeline(dve, body, B_HEADS // 2)
                unit_done()
                split()
                residual(0)

            def branch(kind, layer):
                scale = C_DIM ** -0.5

                def values():
                    src = wk[:, 1, 0:2 * P].rearrange("p (t n) -> p t n", t=TB)
                    for h in range(2):
                        c = slice(h * C_DIM, (h + 1) * C_DIM)
                        dve.tensor_copy(vz[:, :, h, c], src[:, :, c]).then_inc(sems["v_ready"], 1)

                def body_sb(j):
                    more = not is_at(j, C_HEADS // 2 - 1)
                    z = wk[:, 2:4, 0:SEG]
                    strict = tile2(kcol("strict"))
                    dve.wait_ge(*at("abs_ready"))
                    seq(dve.tensor_scalar(keep[:, :, :], z, scale, 0.0, ALU.mult, ALU.min))
                    dve.wait_ge(*at("softplus_ready"))
                    seq(dve.tensor_tensor(prob[:, :, :], keep[:, :, :], soft[:, :, :], ALU.subtract))
                    seq(dve.scalar_tensor_tensor(keep[:, :, :], z, -scale, prob[:, :, :], ALU.mult, ALU.add))
                    dve.tensor_tensor(keep[:, :, :], keep[:, :, :], strict, ALU.mult).then_inc(sems["keep_ready"], 1)
                    if not is_at(j, 0):
                        unit_done()
                        split()
                    dve.wait_ge(*at("suffix_done"))
                    dve.tensor_tensor(sc[:, :, :], prob[:, :, :], wk[:, 2:4, 0:SEG], ALU.add)\
                        .then_inc(sems["weight_in_ready"], 1)
                    if more:
                        unit_done()
                        split()
                    dve.wait_ge(*at("weight_exp"))
                    dve.tensor_tensor(probT[:, :, :], soft[:, :, :], strict, ALU.mult)\
                        .then_inc(sems["weight_ready"], 1)
                    if more:
                        unit_done()
                    hidden(wk[:, 1, S:2 * S], 1)
                    if more:
                        values()
                        split()

                def rotate():
                    unit_done()
                    dve.wait_ge(*at("qr_raw_ready"))
                    dve.tensor_tensor(levels[:, 0:2, :], rot1[:, :, :], tile2(kcol("moba_cos")), ALU.mult)

                def rotated():
                    dve.wait_ge(*at("qr_rotated"))
                    seq(dve.tensor_tensor(rot2[:, :, :], wk[:, 0, :].rearrange("p (a n) -> p a n", a=2),
                                          tile2(kcol("moba_sin")), ALU.mult))
                    dve.tensor_tensor(q_sb[:, 0, :], levels[:, 0, :], rot2[:, 0, :], ALU.add)\
                        .then_inc(sems["qk_roped"], 1)
                    for h in range(2):
                        r = slice(h * C_DIM, (h + 1) * C_DIM)
                        dve.tensor_tensor(kz[r, h, :], levels[r, 1, :], rot2[r, 1, :], ALU.add)\
                            .then_inc(sems["qk_roped"], 1)
                    split()

                def body_moba(j):
                    more = not is_at(j, C_HEADS // 2 - 1)
                    softmax(scale)
                    if not is_at(j, 0):
                        unit_done()
                        split()
                    if more:
                        rotate()
                    second_probs()
                    if more:
                        rotated()
                        unit_done()
                    hidden(wk[:, 1, S:2 * S], 1)
                    if more:
                        values()
                        split()

                if kind == "sb":
                    unit_done()
                    split()
                else:
                    rotate()
                    rotated()
                unit_done()
                values()
                split()
                at.pipeline(dve, body_sb if kind == "sb" else body_moba, C_HEADS // 2)
                unit_done()
                split()

            def merge(layer):
                dve.wait_ge(*at("branch_ready", 4))
                for q in range(4):
                    which, half = q // 2, q % 2
                    c = slice(half * 512, (half + 1) * 512)
                    unit_done()
                    split()
                    unit_done()
                    for tb in range(TB):
                        g = gates4[:, 2 * (q % 2) + tb, :]
                        dve.wait_ge(*at("gate_ready"))
                        if which == 0:
                            dve.tensor_tensor(tok[:, tb, c], g, gate_sb[:, tb, c], ALU.mult)\
                                .then_inc(sems["gate_used"], 1)
                        else:
                            dve.tensor_tensor(g, g, acc[:, 2 * tb + half, :], ALU.mult)\
                                .then_inc(sems["gate_used"], 1)
                    if which:
                        seq(dve.tensor_copy(stat[:, 0:1], stat[:, 1:2]))
                        for tb in range(TB):
                            last = dve.tensor_tensor(tok[:, tb, c], tok[:, tb, c], gates4[:, 2 * (q % 2) + tb, :],
                                                     ALU.add)
                            if half:
                                last.then_inc(sems["tokens_ready"], 1)
                    split()
                turn(KD, (0, 1, 2, 3), fT_hi, fT_lo)
                for c in range(4):
                    unit_done()
                    if c == 3:
                        residual(1)
                    split()

            def finish():
                if stop_after is not None:
                    dve.tensor_copy(stat[:, 0:1], stat[:, 1:2]).then_inc(sems["out_ready"], 1)

            network(Stages(setup=setup, norm=norm, ffn=ffn, hgrn=hgrn, mla=mla, ple=ple, latent=latent,
                                    final_norm=final_norm, turn_residual=turn_residual, branch=branch,
                                    merge=merge, layer_norm=layer_norm, finish=finish))


_INS = ["x", "p", "positions", "norm_gains", "a_lb_logits", "a_out_gain", "kv_norm_in", "kv_latent_norm",
        "b_q_norm", "final_norm", "ln_mix_g_2", "ln_mix_b_2", "ln_ffn_g_2", "ln_ffn_b_2"]


def layout(inputs):
    arrays = {name: np.ascontiguousarray(inputs[name]) for name in _INS}
    w = {name: np.asarray(a) for name, a in inputs.items()}
    arrays["weights"] = np.concatenate([unit.reshape(-1) for unit in stream(w)])
    arrays["const"] = constants()
    return arrays


def kernel(**inputs):
    import concourse.bacc as bacc
    from concourse.bass_utils import run_bass_kernel_spmd

    nc = bacc.Bacc("TRN2", target_bir_lowering=False, num_devices=1)
    arrays = {f"in_{name}": a for name, a in layout(inputs).items()}
    args = [nc.dram_tensor(name, a.shape, mybir.dt.from_np(a.dtype), kind="ExternalInput").ap()
            for name, a in arrays.items()]
    out = nc.dram_tensor("out", (1, S, D), F32, kind="ExternalOutput").ap()
    build(nc, *args, out)
    r = run_bass_kernel_spmd(nc, [arrays], core_ids=[0])
    return r.results[0]["out"]
```

```python
from contextlib import ExitStack, contextmanager

import numpy as np

import concourse.bass as bass
from concourse import mybir

F32 = mybir.dt.float32
F32R = mybir.dt.float32r
I32 = mybir.dt.int32
U32 = mybir.dt.uint32
ALU = mybir.AluOpType
ACT = mybir.ActivationFunctionType
AX = mybir.AxisListType

P = 128
S = 256
TB = S // P
D = 1024
KD = D // P
DFF = 2816
FC = 256
NFF = DFF // FC
PLE = 256
SLOT = 2048
RING = 3
A_HEADS, A_DIM = 8, 128
LEVELS = 8
B_HEADS, B_NOPE, B_ROPE, B_VDIM = 16, 128, 64, 128
B_Q, B_KV = 512, 256
C_HEADS, C_DIM = 8, 64
C_WIDTH = C_HEADS * C_DIM
EPS, LN_EPS = 1e-6, 1e-5
ALPHA = 4 ** 0.25
SEG = P + S
TWO_PI = 2 * np.pi
PI_HI = 6.28125
PI_MID = float(np.float32(int((TWO_PI - PI_HI) * 2 ** 21) / 2 ** 21))
PI_LO = float(TWO_PI - PI_HI - PI_MID)
MAGIC = 1.5 * 2.0 ** 23
LN_FLOOR = 2.0 ** -60

GAIN_ROWS = [("kv_latent_norm", 2), ("b_q_norm", 4), ("a_out_gain", 1), ("a_lb_logits", 16)]
GAIN_AT = {}
_n = 0
for _name, _rows in GAIN_ROWS:
    GAIN_AT[_name] = _n
    _n += _rows
N_GAINS = _n
BUSY_BEFORE, BUSY_BETWEEN, BUSY_FIRST = 8, 6, 14
PAIRS = C_HEADS // 2
NORMS = 14

CONST_AT = {}
_n = 0
for _name, _w in [("identity", P), ("rotate_mla", P), ("rotate_moba", P), ("causal", SEG), ("strict", SEG),
                  ("later", P), ("ones", S), ("levels", LEVELS * P), ("restart", S), ("moba_cos", S),
                  ("moba_sin", S), ("inv_freq", 1)]:
    CONST_AT[_name] = (_n, _w)
    _n += _w
N_CONST = _n


def constants():
    c = np.zeros((P, N_CONST), np.float32)

    def put(name, a):
        at, w = CONST_AT[name]
        c[:, at:at + w] = a

    i = np.arange(P)
    put("identity", np.eye(P))

    def rotation(group, half):
        r = np.zeros((P, P))
        for g in range(0, P, group):
            for j in range(half):
                r[g + half + j, g + j] = -1.0
                r[g + j, g + half + j] = 1.0
        return r

    put("rotate_mla", rotation(B_ROPE, B_ROPE // 2))
    put("rotate_moba", rotation(C_DIM, C_DIM // 8))
    tri = np.where(i[:, None] >= i[None, :], 0.0, -1e30)
    put("causal", np.concatenate([tri, np.zeros((P, P)), tri], 1))
    past = np.where(i[:, None] < i[None, :], 0.0, -1e30)
    put("strict", np.concatenate([past, np.zeros((P, P)), past], 1))
    put("later", (i[:, None] > i[None, :]))
    put("ones", 1.0)
    levels = [np.eye(P)]
    for level in range(LEVELS - 1):
        m = 1 << level
        same = (i[:, None] // (2 * m)) == (i[None, :] // (2 * m))
        levels.append(same & (i[:, None] % (2 * m) < m) & (i[None, :] % (2 * m) >= m))
    put("levels", np.concatenate(levels, 1))
    put("restart", (np.arange(S) % 64 != 0).astype(np.float32)[None])
    pos = np.arange(S, dtype=np.float32)
    rope = C_DIM // 4
    freq = (np.float32(500000.0) ** (-np.arange(0, rope, 2, dtype=np.float32) / np.float32(rope))).astype(np.float32)
    ang = pos[None, :] * freq[:, None]
    cos, sin = np.ones((C_DIM, S), np.float32), np.zeros((C_DIM, S), np.float32)
    for h in (0, rope // 2):
        cos[h:h + rope // 2], sin[h:h + rope // 2] = np.cos(ang), np.sin(ang)
    put("moba_cos", np.tile(cos, (2, 1)))
    put("moba_sin", np.tile(sin, (2, 1)))
    e = np.arange(0, B_ROPE, 2, dtype=np.float32) / np.float32(B_ROPE)
    inv = (np.float32(1.0) / np.float32(10000.0) ** e).astype(np.float32)
    put("inv_freq", np.tile(inv, P // len(inv))[:, None])
    return c


def interleave(heads, a, b, c, extra=()):
    yield a(0)
    yield b(0)
    for h in range(heads):
        if h:
            yield c(h - 1)
        if h + 1 < heads:
            yield a(h + 1)
            yield b(h + 1)
    yield from extra
    yield c(heads - 1)


def unit_sizes():
    ffn = [SLOT] * (3 * NFF)
    for layer in range(2):
        yield from ffn
        if layer == 0:
            yield from interleave(A_HEADS, lambda h: SLOT, lambda h: SLOT, lambda h: D)
        else:
            yield from [SLOT] * 2
            yield from interleave(B_HEADS // 2, lambda j: 4 * 384, lambda j: D, lambda j: SLOT)
        yield from ffn
        yield from [SLOT] * 5
        if layer == 0:
            yield from (SLOT, KD * P)
    for layer in range(2):
        yield from interleave(C_HEADS, lambda j: SLOT, lambda j: D, lambda j: D, [SLOT] * 2)
        yield from [SLOT] * 10
        yield from ffn


UNITS = list(unit_sizes())


def stream(w):
    def cut(a, k0, nk, *cols):
        b = np.concatenate([a[k0 * P:(k0 + nk) * P, c:c + n] for c, n in cols], 1)
        return b.reshape(nk, P, -1).transpose(1, 0, 2).reshape(P, -1)

    def ffn(gate, up, at, down):
        for j in range(NFF + 1):
            if j < NFF:
                for k0 in (0, 4):
                    a = cut(gate, k0, 4, (j * FC, FC)).reshape(P, 4, FC)
                    b = cut(up, k0, 4, (j * FC + at, FC)).reshape(P, 4, FC)
                    yield np.concatenate([a, b], 2).reshape(P, -1)
            if j:
                yield cut(down, 2 * (j - 1), 2, (0, D))

    def close(a, blocks):
        for k in range(0, blocks, 2):
            yield cut(a, k, 2, (0, D))

    for layer in range(2):
        w_in, w_out = w["ffn_w_in"][layer], w["ffn_w_out"][layer]
        yield from ffn(w_in[0], w_in[0], DFF, w_out[0])
        if layer == 0:
            a = w["a_w_in"][0]
            yield from interleave(A_HEADS, lambda h: cut(a, 0, KD, (h * P, P), (h * P + D, P)),
                                  lambda h: cut(a, 0, KD, (h * P + 2 * D, P), (h * P + 3 * D, P)),
                                  lambda h: cut(w["a_w_out"][0], h, 1, (0, D)))
        else:
            for k0 in (0, 4):
                yield cut(w["b_w_dq"][0], k0, 4, (0, B_Q))
            yield from interleave(B_HEADS // 2,
                                  lambda j: cut(w["b_w_uq"][0], 0, 4, (j * 384, 128), (j * 384 + 192, 128),
                                                (j * 384 + 128, 64), (j * 384 + 320, 64)),
                                  lambda j: cut(w["kv_w_up"], 0, 2, (j * 512, 512)),
                                  lambda j: cut(w["b_w_out"][0], 2 * j, 2, (0, D)))
        yield from ffn(w_in[1], w_in[1], DFF, w_out[1])
        yield from close(w["ple_w_gate"][layer], KD)
        yield from close(w["ple_w_in"][layer], 2)
        if layer == 0:
            yield cut(w["kv_w_down"], 0, KD, (0, B_KV))
            yield cut(w["kv_w_down"], 0, KD, (B_KV, B_ROPE), (B_KV, B_ROPE))
    for layer in range(2):
        a = w["w_in_2"][layer]

        def first(j):
            return j // 4 * 3 * C_WIDTH + j % 4 * P

        out = [w["w_branch_sb_2"][layer], w["w_branch_moba_2"][layer]]
        gates = [cut(a, k0, 4, (6 * C_WIDTH + c * 512, 512)) for c in range(4) for k0 in (0, 4)]
        yield from interleave(C_HEADS, lambda j: cut(a, 0, KD, (first(j), P), (first(j) + C_WIDTH, P)),
                              lambda j: cut(a, 0, KD, (first(j) + 2 * C_WIDTH, P)),
                              lambda j: cut(out[j // 4], j % 4, 1, (0, D)), gates[0:2])
        yield from gates[2:]
        yield from close(w["w_out_2"][layer], KD)
        yield from ffn(w["w_ffn_gate_2"][layer], w["w_ffn_up_2"][layer], 0, w["w_ffn_down_2"][layer])


class Stages:

    def __init__(self, setup, norm, ffn, hgrn, mla, ple, latent, branches, merge, finish):
        self.setup, self.norm, self.ffn, self.hgrn, self.mla = setup, norm, ffn, hgrn, mla
        self.ple, self.latent, self.branches, self.merge, self.finish = ple, latent, branches, merge, finish


class Follow:

    def __init__(self, sems, **behind):
        self.sems, self.n, self.rate, self.i = sems, {k: -v for k, v in behind.items()}, None, None

    def __call__(self, name, k=1):
        self.n[name] = self.n.get(name, 0) + k
        if self.i is None:
            return self.sems.get(name), self.n[name]
        return self.sems.get(name), self.i * self.rate.get(name, 0) + self.n[name]

    @contextmanager
    def loop(self, engine, start, end, rate):
        before, unit, units = dict(self.n), self.n.get("unit", 0), rate.get("unit", 0)
        assert UNITS[unit:unit + units * (end - start)] == UNITS[unit:unit + units] * (end - start)
        with engine.Fori(0, end - start) as i:
            self.i, self.rate = i, rate
            yield i + start
            self.i = None
        for name, n in self.n.items():
            assert n - before.get(name, 0) == rate.get(name, 0), (name, n, before, rate)
            self.n[name] = before.get(name, 0) + rate.get(name, 0) * (end - start)

    def repeat(self, engine, body, start, end, peel_last=False):
        before = dict(self.n)
        body(start)
        rate = {name: n - before.get(name, 0) for name, n in self.n.items()}
        stop = end - peel_last
        with self.loop(engine, start + 1, stop, rate) as i:
            body(i)
        if peel_last:
            body(end - 1)

    def pipeline(self, engine, body, n):
        body(0)
        before = dict(self.n)
        body(1)
        rate = {name: k - before.get(name, 0) for name, k in self.n.items()}
        if n > 4:
            with self.loop(engine, 2, n - 2, rate) as i:
                body(i)
        for h in range(n - 2, n):
            body(h)


SIGNALS = """
landed0 landed1 landed2 hi_ready lo_ready unit_done
constants_ready ident_landed const_landed gains_landed x0_landed x1_landed p_landed pos_landed norm_rows0_landed norm_rows1_landed norm_rows_used
out_ready out_landed gains_turned gains_ready bounds_in_ready bounds_exp angle_ready sin_ready zeros_ready
sums_ready res_ready root_ready deviation_ready tokens_ready turned features_hi features_lo p_turned p_hi p_lo ple_gate_ready
silu_ready hidden_ready hidden_turned hidden_hi hidden_lo
kr_raw_ready kr_rotated kr_ready
sigmoids_ready q_ready forget_ready log_ready decay_in_ready decay_ready
level_in_ready level_done level_merged cross_done cross_ready o_done o_dev_ready o_gated
kn_ready v_ready gate_up_done qn_ready qr_raw_ready qr_rotated qr_ready scores_done max_ready exp_ready
kn_done out_gate_ready forget_done probs_ready probs_turned probsT0_ready probsT1_ready attn_done
qk_ready qk_roped z_done scores_ready softplus_ready keep_ready suffix_done weight_in_ready weight_ready
branch_ready gate_ready gate_used dve_step act_step
""".split()


def build(nc, x, p, positions, norm_gains, a_lb_logits, a_out_gain, kv_norm_in, kv_latent_norm, b_q_norm,
          final_norm, ln_mix_g_2, ln_mix_b_2, ln_ffn_g_2, ln_ffn_b_2, weights, const, out, stop_after=None):
    ctx = ExitStack()
    with ctx:
        def sb(name, shape, dt=F32):
            return ctx.enter_context(nc.sbuf_tensor(name, shape, dt))

        raw = sb("raw", [P, RING, SLOT])
        w_hi = sb("w_hi", [P, RING, SLOT], F32R)
        w_lo = sb("w_lo", [P, RING, SLOT], F32R)
        res = sb("res", [P, TB, D])
        tok = sb("tok", [P, TB, D])
        fT_hi = sb("fT_hi", [P, KD, S], F32R)
        fT_lo = sb("fT_lo", [P, KD, S], F32R)
        hT_hi = sb("hT_hi", [P, 2, S], F32R)
        hT_lo = sb("hT_lo", [P, 2, S], F32R)
        hT2_hi = sb("hT2_hi", [P, 2, S], F32R)
        hT2_lo = sb("hT2_lo", [P, 2, S], F32R)
        pT_hi, pT_lo = hT_hi, hT_lo
        cT_hi = sb("cT_hi", [P, 2, S], F32R)
        cT_lo = sb("cT_lo", [P, 2, S], F32R)
        silu = sb("silu", [P, TB, FC])
        hid = sb("hid", [P, TB, FC])
        p_sb = sb("p_sb", [P, 2, TB, PLE])
        kc = sb("kc", [P, N_CONST])
        gain_rows = sb("gain_rows", [N_GAINS, P])
        gains = sb("gains", [P, N_GAINS])
        norm_g = sb("norm_g", [P, 2, D])
        norm_b = sb("norm_b", [P, 2, D])
        gate_sb = sb("gate_sb", [P, TB, D])
        stat = sb("stat", [P, 16])
        eps_sb = sb("eps_sb", [P, 8])
        bn = sb("bn", [P, TB, 2, 6])
        mv = sb("mv", [P, TB, 2])
        pos_i = sb("pos_i", [P, S], I32)
        mla_cos, mla_sin = sb("mla_cos", [P, S]), sb("mla_sin", [P, S])
        krz = sb("krz", [P, 2, S])
        q_sb, k_sb, f_sb = sb("q_sb", [P, 2, S]), sb("k_sb", [P, 2, S]), sb("f_sb", [P, 2, S])
        sg_sb, v_sb = sb("sg_sb", [P, TB, 2 * P]), sb("v_sb", [P, TB, 2 * P])
        lg_sb, b64, b256 = sb("lg_sb", [P, S]), sb("b64", [P, S]), sb("b256", [P, S])
        qr_sb = sb("qr_sb", [P, S])
        levels = sb("levels", [P, LEVELS, S])
        at_sb, cross = sb("at_sb", [P, TB, P]), sb("cross", [P, P])
        ang = levels[:, 0:4, :]
        kr_raw = qr_sb
        flat = levels[:, :, :].rearrange("p a n -> p (a n)")
        soft, keep = [flat[:, i * 2 * SEG:(i + 1) * 2 * SEG].rearrange("p (h n) -> p h n", h=2) for i in range(2)]
        gates4 = levels[:, :, :].rearrange("p a n -> p (a n)").rearrange("p (b n) -> p b n", b=4)
        rot1, rot2 = sb("rot1", [P, 2, S]), sb("rot2", [P, 2, S])
        kz, vz = sb("kz", [P, 2, S]), sb("vz", [P, TB, 2, P])
        sc, prob, probT = sb("sc", [P, 2, SEG]), sb("prob", [P, 2, SEG]), sb("probT", [P, 2, SEG])
        acc = ctx.enter_context(nc.psum_tensor("acc", [P, 4, 512], F32))
        wk = ctx.enter_context(nc.psum_tensor("wk", [P, 4, 512], F32))
        sems = {name: ctx.enter_context(nc.semaphore(name)) for name in SIGNALS}

        def kcol(name):
            at, w = CONST_AT[name]
            return kc[:, at:at + w]

        ident = kcol("identity")

        def gcol(name, n=0):
            c = GAIN_AT[name] + n
            return gains[:, c:c + 1]

        lower = sb("lower", [P, 4, A_HEADS])

        def tile2(a):
            return a.unsqueeze(1).to_broadcast([P, 2, a.shape[-1]])

        def network(e):
            e.setup()
            for layer in range(2):
                e.norm("rms", before_ffn=True)
                e.ffn(0, first=layer == 0)
                if stop_after == "ffn":
                    break
                e.norm("rms")
                if layer == 0:
                    e.hgrn()
                else:
                    e.mla()
                if stop_after == ("hgrn", "mla")[layer]:
                    break
                e.norm("rms", before_ffn=True)
                e.ffn(0)
                e.norm("rms")
                e.ple(layer)
                if stop_after == "ple":
                    break
                if layer == 0:
                    e.norm("rms")
                    e.latent()
            if stop_after in ("ffn", "hgrn", "mla", "ple"):
                e.finish()
                return
            e.norm("rms_in_place")
            for layer in range(2):
                e.branches(layer)
                e.merge(layer)
                e.norm("layer", before_ffn=True)
                e.ffn(1, last=layer == 1)
                e.norm("layer" if layer == 0 else "layer_last")
                if stop_after == "half":
                    e.finish()
                    return
            e.finish()


        def norm_bank(tb, b, before_ffn):
            return (2 if tb == 0 or before_ffn else 0) + b

        n_units = [0]

        def is_at(h, k):
            return isinstance(h, int) and h == k

        block = ctx.enter_context(nc.Block())

        @block.sync
        def _(sp):
            at = Follow(sems, lo_ready=RING)

            def unit():
                u = at.n.get("unit", 0)
                at.n["unit"] = u + 1
                slot, n = u % RING, UNITS[u]
                sem, value = at("lo_ready")
                if at.i is not None or value > 0:
                    sp.wait_ge(sem, value)
                start = at("floats", P * n)[1] - P * n
                sp.dma_start(raw[:, slot, 0:n], weights[bass.ds(start, P * n)].rearrange("(p n) -> p n", p=P))\
                    .then_inc(sems[f"landed{slot}"], 16)

            def units(n):
                for _ in range(n):
                    unit()

            def mixer(heads):
                units(2)
                at.pipeline(sp, lambda h: units(2 * (not is_at(h, heads - 1)) + (not is_at(h, 0))), heads)
                unit()

            def rows(n):
                if n >= NORMS:
                    return
                if n >= 2:
                    sp.wait_ge(*at("norm_rows_used"))
                if n < 9:
                    pairs = [(norm_g, kv_norm_in if n == 4 else norm_gains[n // 5, n % 5])]
                elif n == 9:
                    pairs = [(norm_g, final_norm)]
                else:
                    i, (g, b) = (n - 10) // 2, ((ln_mix_g_2, ln_mix_b_2), (ln_ffn_g_2, ln_ffn_b_2))[n % 2]
                    pairs = [(norm_g, g[i]), (norm_b, b[i])]
                for dst, src in pairs:
                    sp.dma_start(dst[:, n % 2, :], src.rearrange("(o d) -> o d", o=1).to_broadcast([P, D]))\
                        .then_inc(sems[f"norm_rows{n % 2}_landed"], 16)

            def norm(kind, before_ffn=False):
                at.n["norm"] = at.n.get("norm", 0) + 1
                rows(at.n["norm"])

            def setup():
                def tokens(tb):
                    sp.dma_start(res[:, tb, :], x[0, tb * P:(tb + 1) * P, :]).then_inc(sems[f"x{tb}_landed"], 16)

                tokens(0)
                sp.dma_start(kc[:, 0:P], const[:, 0:P]).then_inc(sems["ident_landed"], 16)
                rows(0)
                unit()
                tokens(1)
                unit()

            def late_loads():
                views = {"kv_latent_norm": kv_latent_norm.rearrange("(k d) -> k d", d=P),
                         "b_q_norm": b_q_norm.rearrange("o (k d) -> (o k) d", d=P),
                         "a_out_gain": a_out_gain, "a_lb_logits": a_lb_logits.rearrange("l (k d) -> (l k) d", d=P)}
                for name, n in GAIN_ROWS:
                    r = GAIN_AT[name]
                    sp.dma_start(gain_rows[r:r + n, :], views[name]).then_inc(sems["gains_landed"], 16)
                sp.dma_start(pos_i[:, :], positions.to_broadcast([P, S])).then_inc(sems["pos_landed"], 16)
                sp.dma_start(kc[:, P:N_CONST], const[:, P:N_CONST]).then_inc(sems["const_landed"], 16)
                for layer in range(2):
                    sp.dma_start(p_sb[:, layer, :, :], p[layer, 0].rearrange("(t p) d -> p t d", p=P))\
                        .then_inc(sems["p_landed"], 16)

            def ffn(second, last=False, first=False):
                def body(j):
                    unit()
                    if first and is_at(j, 1):
                        late_loads()
                    units(2)

                if not first:
                    units(2)
                at.repeat(sp, body, 1, NFF)
                unit()

            def hgrn():
                mixer(A_HEADS)

            def ple(layer):
                units(5)

            def latent():
                units(2)

            def mla():
                units(2)
                mixer(B_HEADS // 2)

            def branches(layer):
                units(2 + 3 * (C_HEADS - 1) + 3)

            def merge(layer):
                units(10)

            def finish():
                if stop_after:
                    units(RING)
                n_units[0] = at.n["unit"]
                for tb in range(TB):
                    sp.wait_ge(*at("out_ready"))
                    sp.dma_start(out[0, tb * P:(tb + 1) * P, :], res[:, tb, :]).then_inc(sems["out_landed"], 16)
                sp.wait_ge(*at("out_landed", 16 * TB))

            network(Stages(setup=setup, norm=norm, ffn=ffn, hgrn=hgrn, mla=mla, ple=ple, latent=latent,
                           branches=branches, merge=merge, finish=finish))

        @block.tensor
        def _(pe):
            at = Follow(sems)

            def next_unit():
                slot = at.n.get("unit", 0) % RING
                at.n["unit"] = at.n.get("unit", 0) + 1
                pe.wait_ge(*at("hi_ready"))
                pe.wait_ge(*at("lo_ready"))
                return slot

            def product(o, lhs, rhs, start, stop):
                nc.tensor.matmul(o, lhs[0], rhs[0], start=start, stop=False, skip_group_check=True)
                nc.tensor.matmul(o, lhs[0], rhs[1], start=False, stop=False, skip_group_check=True)
                return nc.tensor.matmul(o, lhs[1], rhs[0], start=False, stop=stop, skip_group_check=True)

            def whole(o, lhs, rhs, start, stop):
                return nc.tensor.matmul(o, lhs, rhs, start=start, stop=stop, skip_group_check=True)

            def wt(slot, shape):
                k, n = shape
                return [t[:, slot, 0:k * n].rearrange("p (k n) -> p k n", k=k) for t in (w_hi, w_lo)]

            def done(ins):
                ins.then_inc(sems["unit_done"], 1)

            def late_setup():
                pe.wait_ge(*at("const_landed", 16))
                pe.wait_ge(*at("gains_landed", 16 * len(GAIN_ROWS)))
                nc.tensor.transpose(wk[:, 3, 0:N_GAINS], gain_rows[:, :], ident[0:N_GAINS, 0:N_GAINS])\
                    .then_inc(sems["gains_turned"], 1)

            def turn(src, nf, banks, f0=0, out=True):
                pe.wait_ge(*at("tokens_ready", TB))
                for b in range(nf // 2):
                    for f in range(2):
                        for tb in range(TB):
                            c = (f0 + 2 * b + f) * P
                            last = nc.tensor.transpose(wk[:, banks[b], f * S + tb * P:f * S + (tb + 1) * P],
                                                       src[:, tb, c:c + P], ident)
                    last.then_inc(sems["turned"], 1)
                if out:
                    turned_out(nf // 2)

            def turn_block(tb, before_ffn):
                pe.wait_ge(*at("tokens_ready"))
                for b in range(2):
                    for i in range(4):
                        c = (4 * b + i) * P
                        last = nc.tensor.transpose(wk[:, norm_bank(tb, b, before_ffn), i * P:(i + 1) * P],
                                                   normed[0][:, tb, c:c + P], ident)
                    last.then_inc(sems["turned"], 1)

            def keep_busy(n):
                for _ in range(n):
                    nc.tensor.matmul(wk[:, 0, 0:P], ident, ident, start=True, stop=True, skip_group_check=True)

            def turned_out(banks=2):
                pe.wait_ge(*at("features_hi", banks))
                pe.wait_ge(*at("features_lo", banks))

            normed = [tok]
            after_ple = [False]

            def norm(kind, before_ffn=False):
                if at.n.get("norm", 0) == 0:
                    pe.wait_ge(*at("ident_landed", 16))
                at.n["norm"] = at.n.get("norm", 0) + 1
                if kind == "layer_last":
                    return
                normed[0] = tok if kind == "rms" else res
                first = at.n["norm"] == 1
                if not after_ple[0]:
                    keep_busy(0 if first else BUSY_BEFORE)
                after_ple[0] = False
                turn_block(0, before_ffn)
                if before_ffn:
                    keep_busy(BUSY_FIRST if first else BUSY_BETWEEN)
                if not before_ffn:
                    turn_block(1, before_ffn)
                    turned_out()
                turned_out()

            def close(nk, first, slot=None, final=False, operand=(hT_hi, hT_lo)):
                if slot is None:
                    slot = next_unit()
                w = wt(slot, (nk, D))
                order = [(k, tb) for tb in range(TB) for k in range(nk)] if final else \
                    [(k, tb) for k in range(nk) for tb in range(TB)]
                for k, tb in order:
                    lhs = [t[:, k, tb * P:(tb + 1) * P] for t in operand]
                    for half in range(2):
                        last = product(acc[:, 2 * tb + half, :], lhs,
                                       [t[:, k, half * 512:(half + 1) * 512] for t in w],
                                       start=first and k == 0, stop=True)
                    if final and (k, tb) == (nk - 1, 0):
                        last.then_inc(sems["sums_ready"], 1)
                done(last)

            def whole_width(dst, lhs, k0, first, last_unit):
                w = wt(next_unit(), (2, D))
                order = [(k, tb) for tb in range(TB) for k in range(2)] if last_unit else \
                    [(k, tb) for k in range(2) for tb in range(TB)]
                for k, tb in order:
                    for half in range(2):
                        last = product(dst(tb, half), [t[:, k0 + k, tb * P:(tb + 1) * P] for t in lhs],
                                       [t[:, k, half * 512:(half + 1) * 512] for t in w],
                                       start=first and k == 0, stop=last_unit and k == 1)
                    if last_unit and (k, tb) == (1, 0):
                        last.then_inc(sems["sums_ready"], 1)
                done(last)

            def ffn(second, last=False, first=False):
                def part(slot, k0):
                    w = wt(slot, (4, 2 * FC))
                    for f in range(4):
                        o = wk[:, f // 2, f % 2 * S:(f % 2 + 1) * S]
                        for k in range(4):
                            ins = product(o, [t[:, k, f * P:(f + 1) * P] for t in w],
                                          [t[:, k0 + k, :] for t in (fT_hi, fT_lo)],
                                          start=k0 + k == 0 and f % 2 == 0, stop=k0 + k == KD - 1)
                    return ins

                def by_tokens(slot, k0, tb):
                    w = wt(slot, (4, 2 * FC))
                    for k in range(4):
                        ins = product(wk[:, tb, :], [t[:, k0 + k, tb * P:(tb + 1) * P] for t in (fT_hi, fT_lo)],
                                      [t[:, k, :] for t in w], start=k0 + k == 0, stop=k0 + k == KD - 1)
                    return ins

                def first_step():
                    a = next_unit()
                    by_tokens(a, 0, 0)
                    turn_block(1, True)
                    b = next_unit()
                    by_tokens(b, 4, 0).then_inc(sems["gate_up_done"], 1)
                    turned_out()
                    done(by_tokens(a, 0, 1))
                    done(by_tokens(b, 4, 1))
                    if first:
                        late_setup()

                def body(j):
                    pe.wait_ge(*at("hidden_ready", 2 if is_at(j, 1) else 1))
                    done(part(next_unit(), 0))
                    if is_at(j, 1):
                        for f in range(2):
                            for tb in range(TB):
                                last = nc.tensor.transpose(wk[:, 2, f * S + tb * P:f * S + (tb + 1) * P],
                                                           hid[:, tb, f * P:(f + 1) * P], ident)
                        last.then_inc(sems["hidden_turned"], 1)
                    done(part(next_unit(), 4))
                    pe.wait_ge(*at("hidden_hi"))
                    pe.wait_ge(*at("hidden_lo"))
                    close(2, is_at(j, 1))

                first_step()
                body(1)
                at.repeat(pe, body, 2, NFF)
                if first:
                    pe.wait_ge(*at("gains_ready"))
                pe.wait_ge(*at("hidden_ready"))
                pe.wait_ge(*at("hidden_hi"))
                pe.wait_ge(*at("hidden_lo"))
                close(2, False, final=True, operand=(hT2_hi, hT2_lo))

            def hgrn():
                def feature_major(c):
                    for k in range(KD):
                        last = product(wk[:, 0, c * S:(c + 1) * S], [t[:, k, c * P:(c + 1) * P] for t in head_w[0]],
                                       [t[:, k, :] for t in (fT_hi, fT_lo)], start=k == 0, stop=k == KD - 1)
                    return last

                def token_major():
                    w = wt(next_unit(), (KD, 2 * P))
                    for tb in range(TB):
                        for k in range(KD):
                            last = product(wk[:, 1, tb * S:(tb + 1) * S],
                                           [t[:, k, tb * P:(tb + 1) * P] for t in (fT_hi, fT_lo)],
                                           [t[:, k, :] for t in w], start=k == 0, stop=k == KD - 1)
                    done(last)

                def level_scores(r):
                    for i in range(2):
                        n = 2 * r + i
                        for tb in range(TB):
                            c = slice(tb * P, (tb + 1) * P)
                            a, b = (k_sb[:, 0, c], q_sb[:, 0, c]) if n == 0 else \
                                (levels[:, n - 1, c], levels[:, n - 1, c])
                            last = whole(wk[:, 2 + r % 2, (2 * i + tb) * P:(2 * i + tb + 1) * P], a, b, True, True)
                    last.then_inc(sems["level_done"], 1)

                head_w = [None]

                def body(h):
                    more = not is_at(h, A_HEADS - 1)
                    if not is_at(h, 0):
                        closing = next_unit()
                    if more:
                        head_w[0] = wt(next_unit(), (KD, 2 * P))
                        pe.wait_ge(*at("q_ready"))
                        feature_major(1).then_inc(sems["forget_done"], 1)
                    pe.wait_ge(*at("level_in_ready"))
                    level_scores(0)
                    if not is_at(h, 0):
                        pe.wait_ge(*at("hidden_hi"))
                        pe.wait_ge(*at("hidden_lo"))
                    level_scores(1)
                    pe.wait_ge(*at("v_ready"))
                    pe.wait_ge(*at("out_gate_ready"))
                    whole(wk[:, 1, 0:P], levels[:, 7, 0:P], levels[:, 7, P:S], True, True)\
                        .then_inc(sems["cross_done"], 1)
                    pe.wait_ge(*at("level_merged"))
                    level_scores(2)
                    pe.wait_ge(*at("level_merged"))
                    level_scores(3)
                    if not is_at(h, 0):
                        close(1, is_at(h, 1), closing)
                    if more:
                        pe.wait_ge(*at("sigmoids_ready", 2))
                        done(feature_major(0))
                    pe.wait_ge(*at("level_merged", 2))
                    pe.wait_ge(*at("cross_ready"))
                    whole(wk[:, 2, 0:P], at_sb[:, 0, :], v_sb[:, 0, 0:P], True, True)
                    whole(wk[:, 2, P:2 * P], at_sb[:, 1, :], v_sb[:, 1, 0:P], True, False)
                    whole(wk[:, 2, P:2 * P], cross[:, :], v_sb[:, 0, 0:P], False, True).then_inc(sems["o_done"], 1)
                    if more:
                        token_major()
                    pe.wait_ge(*at("o_gated", 2))
                    for tb in range(TB):
                        last = nc.tensor.transpose(wk[:, 3, tb * P:(tb + 1) * P], hid[:, tb, 0:P], ident)
                    last.then_inc(sems["hidden_turned"], 1)

                head_w[0] = wt(next_unit(), (KD, 2 * P))
                feature_major(1).then_inc(sems["forget_done"], 1)
                pe.wait_ge(*at("sigmoids_ready", 2))
                done(feature_major(0))
                token_major()
                at.pipeline(pe, body, A_HEADS)
                pe.wait_ge(*at("hidden_hi"))
                pe.wait_ge(*at("hidden_lo"))
                close(1, False, final=True)

            def ple(layer):
                if layer == 0:
                    pe.wait_ge(*at("p_landed", 32))
                for f in range(2):
                    for tb in range(TB):
                        last = nc.tensor.transpose(wk[:, 2, f * S + tb * P:f * S + (tb + 1) * P],
                                                   p_sb[:, layer, tb, f * P:(f + 1) * P], ident)
                last.then_inc(sems["p_turned"], 1)
                for c in range(4):
                    whole_width(lambda tb, half: acc[:, 2 * tb + half, :], (fT_hi, fT_lo), 2 * c, c == 0, False)
                pe.wait_ge(*at("p_hi"))
                pe.wait_ge(*at("p_lo"))
                whole_width(lambda tb, half: wk[:, 2 - 2 * tb + half, :], (pT_hi, pT_lo), 0, True, True)
                after_ple[0] = True

            def latent():
                w = wt(next_unit(), (KD, B_KV))
                for tb in range(TB):
                    for k in range(KD):
                        last = product(wk[:, 0, tb * S:(tb + 1) * S],
                                       [t[:, k, tb * P:(tb + 1) * P] for t in (fT_hi, fT_lo)],
                                       [t[:, k, :] for t in w], start=k == 0, stop=k == KD - 1)
                done(last)
                w = wt(next_unit(), (KD, P))
                for k in range(KD):
                    last = product(wk[:, 1, 0:S], [t[:, k, :] for t in w],
                                   [t[:, k, :] for t in (fT_hi, fT_lo)], start=k == 0, stop=k == KD - 1)
                done(last)
                pe.wait_ge(*at("kr_raw_ready"))
                whole(wk[:, 1, S:2 * S], kcol("rotate_mla"), kr_raw[:, :], True, True).then_inc(sems["kr_rotated"], 1)
                turn(tok, 2, (2,))
                pe.wait_ge(*at("kr_ready"))

            def softmax_turn():
                pe.wait_ge(*at("probs_ready", 4))
                for h in range(2):
                    for dst, src in ((0, 0), (P, P), (2 * P, 2 * P)):
                        last = nc.tensor.transpose(wk[:, 2 + h, dst:dst + P], prob[:, h, src:src + P], ident)
                    last.then_inc(sems["probs_turned"], 1)

            def softmax_turned():
                pe.wait_ge(*at("probsT0_ready"))
                pe.wait_ge(*at("probsT1_ready"))

            def mla():
                for k0 in (0, 4):
                    w = wt(next_unit(), (4, B_Q))
                    for tb in range(TB):
                        for k in range(4):
                            last = product(wk[:, tb, :], [t[:, k0 + k, tb * P:(tb + 1) * P] for t in (fT_hi, fT_lo)],
                                           [t[:, k, :] for t in w], start=k0 + k == 0, stop=k0 + k == KD - 1)
                    done(last)
                turn(tok, 4, (2, 3))

                def queries():
                    w = wt(next_unit(), (4, 384))
                    for h in range(3):
                        for k in range(4):
                            last = product(wk[:, h // 2, h % 2 * S:(h % 2 + 1) * S],
                                           [t[:, k, h * P:(h + 1) * P] for t in w],
                                           [t[:, k, :] for t in (fT_hi, fT_lo)], start=k == 0, stop=k == 3)
                    done(last)

                def rotate():
                    pe.wait_ge(*at("qr_raw_ready"))
                    whole(wk[:, 1, S:2 * S], kcol("rotate_mla"), qr_sb[:, :], True, True)\
                        .then_inc(sems["qr_rotated"], 1)

                def keys():
                    w = wt(next_unit(), (2, 512))
                    pe.wait_ge(*at("qn_ready"))
                    for h in range(2):
                        for k in range(2):
                            last = product(wk[:, 0, h * S:(h + 1) * S], [t[:, k, h * 256:h * 256 + P] for t in w],
                                           [t[:, k, :] for t in (cT_hi, cT_lo)], start=k == 0, stop=k == 1)
                    last.then_inc(sems["kn_done"], 1)
                    return [t.rearrange("p k (h n) -> p k h n", h=2)[:, :, :, P:2 * P] for t in w]

                def values(w):
                    pe.wait_ge(*at("qr_ready"))
                    for tb in range(TB):
                        for k in range(2):
                            last = product(wk[:, 1, tb * S:(tb + 1) * S],
                                           [t[:, k, tb * P:(tb + 1) * P] for t in (cT_hi, cT_lo)],
                                           [t[:, k] for t in w], start=k == 0, stop=k == 1)
                    done(last)

                def body(j):
                    more = not is_at(j, B_HEADS // 2 - 1)
                    pe.wait_ge(*at("kn_ready"))
                    if not is_at(j, 0):
                        pe.wait_ge(*at("hidden_hi"))
                        pe.wait_ge(*at("hidden_lo"))
                    for h in range(2):
                        for tb in range(TB):
                            nk = (tb + 1) * P
                            o = wk[:, 2 + h, tb * P:tb * P + nk]
                            whole(o, q_sb[:, h, tb * P:(tb + 1) * P], k_sb[:, h, 0:nk], True, False)
                            last = whole(o, rot2[:, 0, tb * P:(tb + 1) * P], krz[:, h, 0:nk], False, True)
                    last.then_inc(sems["scores_done"], 1)
                    if not is_at(j, 0):
                        close(2, is_at(j, 1))
                    pe.wait_ge(*at("v_ready"))
                    if more:
                        queries()
                    softmax_turn()
                    if more:
                        rotate()
                        vw = keys()
                    softmax_turned()
                    for h in range(2):
                        whole(wk[:, 2, h * S:(h + 1) * S], v_sb[:, 0, h * P:(h + 1) * P], probT[:, h, 0:S], True, False)
                        last = whole(wk[:, 2, h * S + P:(h + 1) * S], v_sb[:, 1, h * P:(h + 1) * P],
                                     probT[:, h, S:SEG], False, True)
                    last.then_inc(sems["attn_done"], 1)
                    if more:
                        values(vw)

                queries()
                rotate()
                values(keys())
                at.pipeline(pe, body, B_HEADS // 2)
                pe.wait_ge(*at("hidden_hi"))
                pe.wait_ge(*at("hidden_lo"))
                close(2, False, final=True)

            def gates(q, k0):
                w = wt(next_unit(), (4, 512))
                for tb in range(TB):
                    for k in range(4):
                        last = product(wk[:, 2 * (q % 2) + tb, :],
                                       [t[:, k0 + k, tb * P:(tb + 1) * P] for t in (fT_hi, fT_lo)],
                                       [t[:, k, :] for t in w], start=k0 + k == 0, stop=k0 + k == KD - 1)
                done(last)

            def branches(layer):
                def queries_keys():
                    w = wt(next_unit(), (KD, 2 * P))
                    for c in range(2):
                        for k in range(KD):
                            last = product(wk[:, 0, c * S:(c + 1) * S], [t[:, k, c * P:(c + 1) * P] for t in w],
                                           [t[:, k, :] for t in (fT_hi, fT_lo)], start=k == 0, stop=k == KD - 1)
                    done(last)

                def values():
                    w = wt(next_unit(), (KD, P))
                    for tb in range(TB):
                        for k in range(KD):
                            last = product(wk[:, 1, tb * P:(tb + 1) * P],
                                           [t[:, k, tb * P:(tb + 1) * P] for t in (fT_hi, fT_lo)],
                                           [t[:, k, :] for t in w], start=k == 0, stop=k == KD - 1)
                    done(last)

                def attend(bank=1):
                    o = wk[:, bank, S:2 * S]
                    for h in range(2):
                        whole(o, vz[:, 0, h, :], probT[:, h, 0:S], h == 0, False)
                        last = whole(o[:, P:S], vz[:, 1, h, :], probT[:, h, S:SEG], False, h == 1)
                    last.then_inc(sems["attn_done"], 1)

                def close_before(j):
                    pe.wait_ge(*at("hidden_hi"))
                    pe.wait_ge(*at("hidden_lo"))
                    if j == PAIRS + 1:
                        pe.wait_ge(*at("branch_ready", 4))
                    close(1, j % PAIRS == 1)

                def body_sb(j):
                    pe.wait_ge(*at("qk_ready", 3))
                    for h in range(2):
                        whole(wk[:, 2 + h, 0:S], kz[:, h, 0:P], q_sb[:, 0, :], True, True)
                        last = whole(wk[:, 2 + h, S:SEG], kz[:, h, P:S], q_sb[:, 0, P:S], True, True)
                    last.then_inc(sems["z_done"], 1)
                    if j:
                        close_before(j)
                    queries_keys()
                    pe.wait_ge(*at("keep_ready"))
                    for h in range(2):
                        whole(wk[:, 2 + h, 0:S], kcol("later"), keep[:, h, 0:S], True, False)
                        whole(wk[:, 2 + h, P:S], kcol("ones")[:, 0:P], keep[:, h, S:SEG], False, True)
                        last = whole(wk[:, 2 + h, S:SEG], kcol("later"), keep[:, h, S:SEG], True, True)
                    last.then_inc(sems["suffix_done"], 1)
                    pe.wait_ge(*at("v_ready", 2))
                    if j + 1 == PAIRS:
                        rotate()
                    values()
                    pe.wait_ge(*at("weight_ready"))
                    attend()

                def rotate():
                    pe.wait_ge(*at("qr_raw_ready"))
                    whole(wk[:, 0, :].rearrange("p (a n) -> p a n", a=2), kcol("rotate_moba"), rot1[:, :, :],
                          True, True).then_inc(sems["qr_rotated"], 1)

                def body_moba(j):
                    more = j + 1 < 2 * PAIRS
                    pe.wait_ge(*at("qk_roped", 3))
                    for h in range(2):
                        for tb in range(TB):
                            nk = (tb + 1) * P
                            last = whole(wk[:, 2 + h, tb * P:tb * P + nk], q_sb[:, 0, tb * P:(tb + 1) * P],
                                         kz[:, h, 0:nk], True, True)
                    last.then_inc(sems["scores_done"], 1)
                    close_before(j)
                    pe.wait_ge(*at("v_ready", 2))
                    if more:
                        queries_keys()
                    else:
                        gates(0, 0)
                    softmax_turn()
                    if more:
                        rotate()
                        values()
                    else:
                        gates(0, 4)
                    softmax_turned()
                    attend(1 if more else 2)

                queries_keys()
                values()
                for j in range(PAIRS):
                    body_sb(j)
                for j in range(PAIRS, 2 * PAIRS):
                    body_moba(j)
                close_before(2 * PAIRS + 2)

            def merge(layer):
                gates(1, 0)
                gates(1, 4)
                pe.wait_ge(*at("gate_ready", 2))
                gates(2, 0)
                gates(2, 4)
                pe.wait_ge(*at("gate_ready", 2))
                gates(3, 0)
                pe.wait_ge(*at("gate_ready", 2))
                turn(tok, 4, (0, 1), out=False)
                gates(3, 4)
                turned_out()
                pe.wait_ge(*at("gate_ready", 2))
                pe.wait_ge(*at("gate_used", 4 * TB))
                for c in range(4):
                    whole_width(lambda tb, half: acc[:, 2 * tb + half, :], (fT_hi, fT_lo), 2 * c, c == 0, c == 3)
                    if c == 0:
                        turn(tok, 4, (2, 3), f0=4, out=False)
                    if c == 1:
                        turned_out()

            none = lambda *a: None
            network(Stages(setup=none, norm=norm, ffn=ffn, hgrn=hgrn, mla=mla, ple=ple, latent=latent,
                           branches=branches, merge=merge, finish=none))

        @block.scalar
        def _(act):
            at = Follow(sems)
            total = n_units[0]

            def seq(ins):
                ins.then_inc(sems["act_step"], 1)
                act.wait_ge(*at("act_step"))

            def split():
                n = at.n.get("unit", 0)
                if n >= total:
                    return
                at.n["unit"] = n + 1
                slot, size = n % RING, UNITS[n]
                act.wait_ge(*at(f"landed{slot}", 16))
                act.copy(w_hi[:, slot, 0:size], raw[:, slot, 0:size]).then_inc(sems["hi_ready"], 1)

            def unit_done():
                act.wait_ge(*at("unit_done"))

            def upper(dst, src, scale=None):
                if scale is None:
                    return act.copy(dst, src)
                return act.activation(dst, src, ACT.Copy, scale=scale)

            def late_setup():
                act.wait_ge(*at("gains_turned"))
                act.copy(gains[:, :], wk[:, 3, 0:N_GAINS]).then_inc(sems["gains_ready"], 1)
                act.wait_ge(*at("bounds_in_ready"))
                act.activation(lower[:, 0:2, :], lower[:, 0:2, :], ACT.Exp).then_inc(sems["bounds_exp"], 1)
                act.wait_ge(*at("angle_ready"))
                act.activation(mla_sin[:, :], ang[:, 2, :], ACT.Sin).then_inc(sems["sin_ready"], 1)
                act.activation(mla_cos[:, :], ang[:, 3, :], ACT.Sin).then_inc(sems["sin_ready"], 1)

            def deviation(n, src):
                for tb in range(TB):
                    last = act.activation(gate_sb[:, tb, 0:n], src(tb), ACT.Square, scale=n ** -0.5,
                                          accum_out=stat[:, tb:tb + 1])
                seq(last)
                act.activation(stat[:, 2:4], stat[:, 0:2], ACT.Sqrt, bias=eps_sb[:, 0:1])\
                    .then_inc(sems["deviation_ready"], 1)

            def turn(nf, banks, hi, name=None, c0=0):
                for b in range(nf // 2):
                    act.wait_ge(*at("turned"))
                    if name is None:
                        act.copy(hi[:, 2 * b:2 * b + 2, :], wk[:, banks[b], :].rearrange("p (f n) -> p f n", f=2))\
                            .then_inc(sems["features_hi"], 1)
                        continue
                    for f in range(2):
                        last = upper(hi[:, 2 * b + f, :], wk[:, banks[b], f * S:(f + 1) * S],
                                     gcol(name, c0 + 2 * b + f))
                    last.then_inc(sems["features_hi"], 1)

            owed = [RING, 0]

            def settle_up(n):
                for _ in range(owed[1]):
                    unit_done()
                owed[1] = 0
                for _ in range(min(n, owed[0])):
                    split()
                    owed[0] -= 1

            def norm(kind, before_ffn=False):
                at.n["norm"] = at.n.get("norm", 0) + 1
                if at.n["norm"] == 1:
                    act.wait_ge(*at("constants_ready"))
                seq(act.activation(stat[:, 15:16], eps_sb[:, 2:3], ACT.Sqrt))
                def root(tb):
                    act.wait_ge(*at("res_ready"))
                    if kind.startswith("rms"):
                        seq(act.activation(gate_sb[:, tb, :], res[:, tb, :], ACT.Square, scale=D ** -0.5,
                                           accum_out=stat[:, tb:tb + 1]))
                        act.activation(stat[:, 2 + tb:3 + tb], stat[:, tb:tb + 1], ACT.Sqrt, bias=eps_sb[:, 0:1])\
                            .then_inc(sems["root_ready"], 1)
                    else:
                        act.activation(stat[:, 2 + tb:3 + tb], mv[:, tb, 1:2], ACT.Sqrt, bias=eps_sb[:, 1:2])\
                            .then_inc(sems["root_ready"], 1)

                def upper_parts(tb):
                    for b in range(2):
                        act.wait_ge(*at("turned"))
                        act.copy(fT_hi[:, 4 * b:4 * b + 4, tb * P:(tb + 1) * P],
                                 wk[:, norm_bank(tb, b, before_ffn), :].rearrange("p (f n) -> p f n", f=4))\
                            .then_inc(sems["features_hi"], 1)

                root(0)
                if kind == "layer_last":
                    root(1)
                elif before_ffn:
                    upper_parts(0)
                    root(1)
                    settle_up(2 if at.n["norm"] == 1 else 1)
                    upper_parts(1)
                else:
                    root(1)
                    upper_parts(0)
                    upper_parts(1)
                settle_up(owed[0])

            def hidden(src, nk=2, scale=None):
                upper(hT_hi[:, 0:nk, :], src.rearrange("p (f n) -> p f n", f=nk), scale)\
                    .then_inc(sems["hidden_hi"], 1)

            def ffn(second, last=False, first=False):
                def gate():
                    unit_done()
                    act.activation(silu[:, :, :], wk[:, 0, :].rearrange("p (f n) -> p f n", f=2), ACT.Silu)\
                        .then_inc(sems["silu_ready"], 1)
                    split()

                def hidden_upper(dst=hT_hi):
                    act.wait_ge(*at("hidden_ready"))
                    act.copy(dst[:, :, :], hid[:, :, :]).then_inc(sems["hidden_hi"], 1)

                def first_gate():
                    act.wait_ge(*at("gate_up_done"))
                    act.activation(silu[:, 0, :], wk[:, 0, 0:FC], ACT.Silu).then_inc(sems["silu_ready"], 1)
                    unit_done()
                    split()
                    unit_done()
                    act.activation(silu[:, 1, :], wk[:, 1, 0:FC], ACT.Silu).then_inc(sems["silu_ready"], 1)
                    split()

                def body(j):
                    unit_done()
                    if is_at(j, 1):
                        act.wait_ge(*at("hidden_turned"))
                        hidden(wk[:, 2, :])
                    split()
                    gate()
                    if is_at(j, NFF - 1):
                        hidden_upper(hT2_hi)
                        unit_done()
                    else:
                        unit_done()
                        hidden_upper()
                    split()

                first_gate()
                at("hidden_ready", 2)
                if first:
                    late_setup()
                body(1)
                at.repeat(act, body, 2, NFF, peel_last=True)
                owed[0], owed[1] = 1, 1

            def hgrn():
                def forget():
                    act.wait_ge(*at("forget_done"))
                    act.activation(f_sb[:, 0, :], wk[:, 0, S:2 * S], ACT.Sigmoid).then_inc(sems["sigmoids_ready"], 1)
                    act.activation(f_sb[:, 1, :], wk[:, 0, S:2 * S], ACT.Sigmoid, scale=-1.0)\
                        .then_inc(sems["sigmoids_ready"], 1)

                def logarithms():
                    act.wait_ge(*at("forget_ready"))
                    act.activation(lg_sb[:, :], f_sb[:, 0, :], ACT.Ln).then_inc(sems["log_ready"], 1)

                def queries():
                    unit_done()
                    act.activation(q_sb[:, 0, :], wk[:, 0, 0:S], ACT.Copy, scale=A_DIM ** -0.5)\
                        .then_inc(sems["q_ready"], 1)
                    split()

                def decays():
                    for n in range(0, LEVELS, 4):
                        act.wait_ge(*at("decay_in_ready"))
                        act.activation(levels[:, n:n + 4, :], levels[:, n:n + 4, :], ACT.Exp)\
                            .then_inc(sems["decay_ready"], 1)

                def inputs():
                    unit_done()
                    act.copy(v_sb[:, :, 0:P], wk[:, 1, :].rearrange("p (t n) -> p t n", t=TB)[:, :, 0:P])\
                        .then_inc(sems["v_ready"], 1)
                    split()

                def out_gates():
                    act.activation(sg_sb[:, :, 0:P], wk[:, 1, :].rearrange("p (t n) -> p t n", t=TB)[:, :, P:2 * P],
                                   ACT.Sigmoid).then_inc(sems["out_gate_ready"], 1)

                def body(h):
                    more = not is_at(h, A_HEADS - 1)
                    if more:
                        forget()
                    act.wait_ge(*at("cross_done"))
                    act.copy(cross[:, :], wk[:, 1, 0:P]).then_inc(sems["cross_ready"], 1)
                    if more:
                        logarithms()
                    if more and not is_at(h, 0):
                        unit_done()
                        split()
                    if more:
                        queries()
                    act.wait_ge(*at("o_done"))
                    for tb in range(TB):
                        last = act.activation(rot1[:, tb, 0:P], wk[:, 2, tb * P:(tb + 1) * P], ACT.Square,
                                              scale=A_DIM ** -0.5, accum_out=stat[:, tb:tb + 1])
                    seq(last)
                    seq(act.activation(stat[:, 2:4], stat[:, 0:2], ACT.Ln, bias=eps_sb[:, 0:1]))
                    act.activation(stat[:, 4:6], stat[:, 2:4], ACT.Exp, scale=-0.5)\
                        .then_inc(sems["o_dev_ready"], 1)
                    if more:
                        decays()
                        inputs()
                    else:
                        unit_done()
                        split()
                    act.wait_ge(*at("hidden_turned"))
                    hidden(wk[:, 3, 0:S], 1, gcol("a_out_gain"))
                    if more:
                        out_gates()

                forget()
                logarithms()
                queries()
                decays()
                inputs()
                out_gates()
                at.pipeline(act, body, A_HEADS)
                owed[0], owed[1] = 1, 1

            def ple(layer):
                act.wait_ge(*at("p_turned"))
                act.copy(pT_hi[:, :, :], wk[:, 2, :].rearrange("p (f n) -> p f n", f=2)).then_inc(sems["p_hi"], 1)
                for c in range(4):
                    unit_done()
                    if c == 3:
                        for b in range(4):
                            act.activation(gate_sb[:, b // 2, (b % 2) * 512:(b % 2 + 1) * 512], acc[:, b, :],
                                           ACT.Sigmoid).then_inc(sems["ple_gate_ready"], 1)
                    split()
                owed[0], owed[1] = 1, 1

            def latent():
                unit_done()
                deviation(B_KV, lambda tb: wk[:, 0, tb * S:(tb + 1) * S])
                unit_done()
                act.copy(kr_raw[:, :], wk[:, 1, 0:S]).then_inc(sems["kr_raw_ready"], 1)
                turn(2, (2,), cT_hi, "kv_latent_norm")
                owed[0], owed[1] = 2, 0

            def softmax(scale):
                act.wait_ge(*at("max_ready"))
                for h in range(2):
                    for seg, (a, b) in enumerate(((0, P), (P, SEG))):
                        c = 2 * seg + h
                        last = act.activation(prob[:, h, a:b], sc[:, h, a:b], ACT.Exp, bias=stat[:, 4 + c:5 + c],
                                              scale=scale, accum_out=stat[:, 8 + c:9 + c])
                last.then_inc(sems["exp_ready"], 1)

            def first_probs():
                act.wait_ge(*at("probs_turned"))
                act.copy(probT[:, 0, :], wk[:, 2, 0:SEG]).then_inc(sems["probsT0_ready"], 1)
                at("probs_turned")

            def mla():
                unit_done()
                split()
                unit_done()
                deviation(B_Q, lambda tb: wk[:, tb, :])
                split()
                turn(4, (2, 3), fT_hi, "b_q_norm")

                def queries():
                    unit_done()
                    act.copy(qr_sb[:, :], wk[:, 1, 0:S]).then_inc(sems["qr_raw_ready"], 1)
                    act.copy(q_sb[:, :, :], wk[:, 0, :].rearrange("p (h n) -> p h n", h=2))\
                        .then_inc(sems["qn_ready"], 1)

                def keys():
                    act.wait_ge(*at("kn_done"))
                    act.copy(k_sb[:, :, :], wk[:, 0, :].rearrange("p (h n) -> p h n", h=2))\
                        .then_inc(sems["kn_ready"], 1)

                def body(j):
                    more = not is_at(j, B_HEADS // 2 - 1)
                    softmax((B_NOPE + B_ROPE) ** -0.5)
                    if not is_at(j, 0):
                        unit_done()
                        split()
                    if more:
                        queries()
                    first_probs()
                    if more:
                        split()
                        keys()
                    act.wait_ge(*at("attn_done"))
                    hidden(wk[:, 2, :])
                    if more:
                        unit_done()
                        split()

                queries()
                split()
                keys()
                unit_done()
                split()
                at.pipeline(act, body, B_HEADS // 2)
                owed[0], owed[1] = 1, 1

            def gates(q):
                if q >= 2:
                    act.wait_ge(*at("gate_used", 2))
                for tb in range(TB):
                    act.activation(gates4[:, 2 * (q % 2) + tb, :], wk[:, 2 * (q % 2) + tb, :], ACT.Sigmoid)\
                        .then_inc(sems["gate_ready"], 1)

            def branches(layer):
                scale = C_DIM ** -0.5

                def queries_keys(j):
                    unit_done()
                    if j >= PAIRS:
                        act.copy(rot1[:, :, :], wk[:, 0, :].rearrange("p (a n) -> p a n", a=2))\
                            .then_inc(sems["qr_raw_ready"], 1)
                        return
                    act.copy(q_sb[:, 0, :], wk[:, 0, 0:S]).then_inc(sems["qk_ready"], 1)
                    for h in range(2):
                        r = slice(h * C_DIM, (h + 1) * C_DIM)
                        act.copy(kz[r, h, :], wk[r, 0, S:2 * S]).then_inc(sems["qk_ready"], 1)

                def body_sb(j):
                    act.wait_ge(*at("scores_ready"))
                    seq(act.activation(soft[:, :, :], sc[:, :, :], ACT.Abs))
                    seq(act.activation(soft[:, :, :], soft[:, :, :], ACT.Exp, scale=-1.0))
                    act.activation(soft[:, :, :], soft[:, :, :], ACT.Ln, bias=1.0).then_inc(sems["softplus_ready"], 1)
                    seq(act.activation(stat[:, 15:16], eps_sb[:, 2:3], ACT.Exp))
                    if j:
                        unit_done()
                        split()
                    queries_keys(j + 1)
                    act.wait_ge(*at("weight_in_ready"))
                    act.activation(probT[:, :, :], sc[:, :, :], ACT.Exp).then_inc(sems["weight_ready"], 1)
                    split()
                    unit_done()
                    act.wait_ge(*at("attn_done"))
                    hidden(wk[:, 1, S:2 * S], 1)
                    split()

                def body_moba(j):
                    more = j + 1 < 2 * PAIRS
                    softmax(scale)
                    unit_done()
                    split()
                    if j == PAIRS:
                        for b in range(4):
                            act.copy(gate_sb[:, b // 2, (b % 2) * 512:(b % 2 + 1) * 512], acc[:, b, :])\
                                .then_inc(sems["branch_ready"], 1)
                    if more:
                        queries_keys(j + 1)
                        first_probs()
                        split()
                        unit_done()
                        split()
                    else:
                        unit_done()
                        split()
                        first_probs()
                        unit_done()
                    act.wait_ge(*at("attn_done"))
                    hidden(wk[:, 1 if more else 2, S:2 * S], 1)
                    if not more:
                        gates(0)
                        split()

                if layer == 0:
                    act.wait_ge(*at("zeros_ready", 3))
                queries_keys(0)
                split()
                unit_done()
                split()
                for j in range(PAIRS):
                    body_sb(j)
                for j in range(PAIRS, 2 * PAIRS):
                    body_moba(j)
                unit_done()
                split()

            def merge(layer):
                for q in range(1, 4):
                    unit_done()
                    if q == 3:
                        turn(4, (0, 1), fT_hi[:, 0:4, :])
                    split()
                    unit_done()
                    gates(q)
                    split()
                at("gate_used", 4)
                for c in range(3):
                    unit_done()
                    if c == 0:
                        turn(4, (2, 3), fT_hi[:, 4:8, :])
                    split()
                owed[0], owed[1] = 1, 1

            none = lambda *a: None
            network(Stages(setup=none, norm=norm, ffn=ffn, hgrn=hgrn, mla=mla, ple=ple, latent=latent,
                           branches=branches, merge=merge, finish=none))

        @block.gpsimd
        def _(pool):
            for t in (kz, vz, krz):
                pool.memset(t[:], 0.0).then_inc(sems["zeros_ready"], 1)

        @block.vector
        def _(dve):
            at = Follow(sems)
            total = n_units[0]

            def seq(ins):
                ins.then_inc(sems["dve_step"], 1)
                dve.wait_ge(*at("dve_step"))

            def split():
                n = at.n.get("unit", 0)
                if n >= total:
                    return
                at.n["unit"] = n + 1
                slot, size = n % RING, UNITS[n]
                dve.wait_ge(*at("hi_ready"))
                dve.tensor_tensor(w_lo[:, slot, 0:size], raw[:, slot, 0:size], w_hi[:, slot, 0:size].bitcast(F32),
                                  ALU.subtract)\
                    .then_inc(sems["lo_ready"], 1)

            def unit_done():
                dve.wait_ge(*at("unit_done"))

            def lower_part(lo, src, hi, scale=None):
                hi = hi.bitcast(F32)
                if scale is None:
                    return dve.tensor_tensor(lo, src, hi, ALU.subtract)
                return dve.scalar_tensor_tensor(lo, src, scale, hi, ALU.mult, ALU.subtract)

            def setup():
                dve.memset(eps_sb[:, 0:1], EPS)
                dve.memset(eps_sb[:, 1:2], LN_EPS)
                dve.memset(eps_sb[:, 2:3], 1.0)
                seq(dve.memset(eps_sb[:, 3:4], 0.0))
                dve.memset(eps_sb[:, 7:8], 0.0).then_inc(sems["constants_ready"], 1)

            def late_setup():
                dve.wait_ge(*at("gains_ready"))
                c = GAIN_AT["a_lb_logits"]
                l0, l1 = gains[:, c:c + 8], gains[:, c + 8:c + 16]
                seq(dve.tensor_tensor(lower[:, 2, :], l0, l1, ALU.max))
                dve.tensor_tensor(lower[:, 0, :], l0, lower[:, 2, :], ALU.subtract)
                dve.tensor_tensor(lower[:, 1, :], l1, lower[:, 2, :], ALU.subtract)\
                    .then_inc(sems["bounds_in_ready"], 1)
                dve.wait_ge(*at("bounds_exp"))
                seq(dve.tensor_tensor(lower[:, 2, :], lower[:, 0, :], lower[:, 1, :], ALU.add))
                seq(dve.reciprocal(lower[:, 3, :], lower[:, 2, :]))
                seq(dve.tensor_tensor(lower[:, 2, :], lower[:, 0, :], lower[:, 3, :], ALU.mult))
                seq(dve.tensor_scalar(lower[:, 3, :], lower[:, 2, :], -1.0, 1.0, ALU.mult, ALU.add))
                dve.wait_ge(*at("pos_landed", 16))
                dve.wait_ge(*at("const_landed", 16))
                seq(dve.tensor_copy(ang[:, 0, :], pos_i[:, :]))
                seq(dve.tensor_scalar(ang[:, 1, :], ang[:, 0, :], kcol("inv_freq"), None, ALU.mult))
                seq(dve.tensor_scalar(ang[:, 0, :], ang[:, 1, :], 1.0 / TWO_PI, MAGIC, ALU.mult, ALU.add))
                seq(dve.tensor_scalar(ang[:, 0, :], ang[:, 0, :], MAGIC, None, ALU.subtract))
                for part in (PI_HI, PI_MID, PI_LO):
                    seq(dve.scalar_tensor_tensor(ang[:, 1, :], ang[:, 0, :], -part, ang[:, 1, :], ALU.mult, ALU.add))
                pi = float(np.nextafter(np.float32(np.pi), np.float32(0)))
                seq(dve.tensor_scalar(ang[:, 2, :], ang[:, 1, :], pi, -pi, ALU.min, ALU.max))
                seq(dve.tensor_scalar(ang[:, 0, :], ang[:, 2, :], np.pi / 2, -TWO_PI, ALU.is_gt, ALU.mult))
                seq(dve.scalar_tensor_tensor(ang[:, 3, :], ang[:, 2, :], np.pi / 2, ang[:, 0, :], ALU.add, ALU.add))
                dve.tensor_scalar(ang[:, 3, :], ang[:, 3, :], pi, -pi, ALU.min, ALU.max)\
                    .then_inc(sems["angle_ready"], 1)

            def scaled(src, n):
                dve.wait_ge(*at("deviation_ready"))
                seq(dve.reciprocal(stat[:, 4:6], stat[:, 2:4]))
                for tb in range(TB):
                    dve.tensor_scalar(tok[:, tb, 0:n], src(tb), stat[:, 4 + tb:5 + tb], None, ALU.mult)\
                        .then_inc(sems["tokens_ready"], 1)

            def turn(nf, banks, hi, lo, name=None, c0=0):
                for b in range(nf // 2):
                    dve.wait_ge(*at("features_hi"))
                    if name is None:
                        lower_part(lo[:, 2 * b:2 * b + 2, :], wk[:, banks[b], :].rearrange("p (f n) -> p f n", f=2),
                                   hi[:, 2 * b:2 * b + 2, :]).then_inc(sems["features_lo"], 1)
                        continue
                    for f in range(2):
                        last = lower_part(lo[:, 2 * b + f, :], wk[:, banks[b], f * S:(f + 1) * S],
                                          hi[:, 2 * b + f, :], gcol(name, c0 + 2 * b + f))
                    last.then_inc(sems["features_lo"], 1)

            def unchanged(tb):
                if at.n.get("norm", 0) == 1:
                    dve.wait_ge(*at(f"x{tb}_landed", 16))
                return dve.memset(eps_sb[:, 4 + tb:5 + tb], 0.0)

            def sums(tb):
                if tb == 0:
                    dve.wait_ge(*at("sums_ready"))
                else:
                    unit_done()

            def adds(scale, alpha=1.0):
                def add(tb):
                    sums(tb)
                    r, a = res[:, tb, :], acc[:, 2 * tb:2 * tb + 2, :].rearrange("p b n -> p (b n)")
                    if alpha != 1.0:
                        return dve.scalar_tensor_tensor(r, r, alpha, a, ALU.mult, ALU.add)
                    return dve.scalar_tensor_tensor(r, a, scale, r, ALU.mult, ALU.add)
                pending[0] = add
                owed[0] = 1

            pending = [unchanged]
            owed = [RING]

            def norm(kind, before_ffn=False):
                n = at.n.get("norm", 0)
                at.n["norm"] = n + 1
                g, b = norm_g[:, n % 2, :], norm_b[:, n % 2, :]
                dst = tok if kind == "rms" else res

                def lower_parts(tb):
                    if kind == "layer_last":
                        return
                    for b in range(2):
                        dve.wait_ge(*at("features_hi"))
                        lower_part(fT_lo[:, 4 * b:4 * b + 4, tb * P:(tb + 1) * P],
                                   wk[:, norm_bank(tb, b, before_ffn), :].rearrange("p (f n) -> p f n", f=4),
                                   fT_hi[:, 4 * b:4 * b + 4, tb * P:(tb + 1) * P]).then_inc(sems["features_lo"], 1)

                def rows_landed(tb):
                    if tb == 0:
                        dve.wait_ge(*at(f"norm_rows{n % 2}_landed", 16 if kind.startswith("rms") else 32))

                def settle(tb):
                    ins = pending[0](tb)
                    if kind.startswith("rms"):
                        ins.then_inc(sems["res_ready"], 1)
                    else:
                        seq(ins)

                def scale(tb):
                    r, root, inverse = res[:, tb, :], stat[:, 2 + tb:3 + tb], stat[:, 4 + tb:5 + tb]
                    if kind.startswith("rms"):
                        dve.wait_ge(*at("root_ready"))
                        seq(dve.reciprocal(inverse, root))
                        rows_landed(tb)
                        dve.scalar_tensor_tensor(dst[:, tb, :], r, inverse, g, ALU.mult, ALU.mult)\
                            .then_inc(sems["tokens_ready"], 1)
                        return
                    for half in range(2):
                        last = dve.bn_stats(bn[:, tb, half, :], r[:, half * 512:(half + 1) * 512])
                    seq(last)
                    dve.bn_aggr(mv[:, tb, :], bn[:, tb, :, :]).then_inc(sems["res_ready"], 1)
                    rows_landed(tb)
                    dve.wait_ge(*at("root_ready"))
                    seq(dve.reciprocal(inverse, root))
                    seq(dve.scalar_tensor_tensor(r, r, mv[:, tb, 0:1], g, ALU.subtract, ALU.mult))
                    dve.scalar_tensor_tensor(r, r, inverse, b, ALU.mult, ALU.add)\
                        .then_inc(sems["tokens_ready" if kind == "layer" else "out_ready"], 1)

                settle(0)
                scale(0)
                settle(1)
                if before_ffn:
                    lower_parts(0)
                scale(1)
                if kind != "layer_last":
                    dve.memset(eps_sb[:, 6:7], 0.0).then_inc(sems["norm_rows_used"], 1)
                if not before_ffn:
                    lower_parts(0)
                if before_ffn:
                    for _ in range(2 if n == 0 else 1):
                        split()
                        owed[0] -= 1
                lower_parts(1)
                for _ in range(owed[0]):
                    split()
                owed[0] = 0
                pending[0] = unchanged

            def hidden(src, nk=2, scale=None):
                dve.wait_ge(*at("hidden_hi"))
                lower_part(hT_lo[:, 0:nk, :], src.rearrange("p (f n) -> p f n", f=nk), hT_hi[:, 0:nk, :], scale)\
                    .then_inc(sems["hidden_lo"], 1)
                at("hidden_lo")

            def ffn(second, last=False, first=False):
                def gate():
                    unit_done()
                    if started[0]:
                        dve.wait_ge(*at("hidden_lo"))
                    started[0] = True
                    dve.wait_ge(*at("silu_ready"))
                    dve.tensor_tensor(hid[:, :, :], silu[:, :, :], wk[:, 1, :].rearrange("p (f n) -> p f n", f=2),
                                      ALU.mult).then_inc(sems["hidden_ready"], 1)

                def hidden_lower(dst=hT_lo, hi=hT_hi):
                    dve.wait_ge(*at("hidden_hi"))
                    lower_part(dst[:, :, :], hid[:, :, :], hi[:, :, :]).then_inc(sems["hidden_lo"], 1)

                def first_gate():
                    for tb in range(TB):
                        dve.wait_ge(*at("silu_ready"))
                        dve.tensor_tensor(hid[:, tb, :], silu[:, tb, :], wk[:, tb, FC:2 * FC], ALU.mult)\
                            .then_inc(sems["hidden_ready"], 1)
                    for _ in range(2):
                        unit_done()
                        split()

                def body(j):
                    unit_done()
                    if is_at(j, 1):
                        hidden(wk[:, 2, :])
                    split()
                    gate()
                    if is_at(j, NFF - 1):
                        hidden_lower(hT2_lo, hT2_hi)
                        split()
                        unit_done()
                    else:
                        split()
                        unit_done()
                        hidden_lower()
                        split()

                started = [False]
                first_gate()
                if first:
                    late_setup()
                body(1)
                at.repeat(dve, body, 2, NFF, peel_last=True)
                at("hidden_lo")
                adds(0.5, ALPHA if second else 1.0)
                owed[0] = 2

            def hgrn():
                def halves(t, m):
                    v = t.rearrange("p (n a m) -> p n a m", a=2, m=m)
                    return v[:, :, 0, :], v[:, :, 1, :]

                def forget(h):
                    dve.wait_ge(*at("sigmoids_ready", 2))
                    one_minus = lower[:, 3, bass.ds(h, 1)]
                    seq(dve.tensor_scalar(f_sb[:, 0, :], f_sb[:, 0, :], one_minus, lower[:, 2, bass.ds(h, 1)],
                                          ALU.mult, ALU.add))
                    dve.tensor_scalar(f_sb[:, 0, :], f_sb[:, 0, :], LN_FLOOR, None, ALU.max)\
                        .then_inc(sems["forget_ready"], 1)
                    dve.tensor_scalar(k_sb[:, 0, :], f_sb[:, 1, :], one_minus, None, ALU.mult)

                def queries():
                    unit_done()
                    split()

                def decays():
                    dve.wait_ge(*at("log_ready"))
                    dve.tensor_tensor_scan(b64[:, :], kcol("restart"), lg_sb[:, :], 0.0, ALU.mult, ALU.add)
                    seq(dve.tensor_tensor_scan(b256[:, :], kcol("ones"), lg_sb[:, :], 0.0, ALU.mult, ALU.add))
                    for n in range(LEVELS):
                        m = 1 << n
                        first, second = halves((b64 if m < 64 else b256)[:, :], m)
                        e_first, e_second = halves(levels[:, n, :], m)
                        ref = first[:, :, m - 1:m].to_broadcast([P, S // (2 * m), m])
                        dve.tensor_tensor(e_first, ref, first, ALU.subtract)
                        last = dve.tensor_tensor(e_second, second, ref, ALU.subtract)
                        if n % 4 == 3:
                            last.then_inc(sems["decay_in_ready"], 1)

                def decayed():
                    dve.wait_ge(*at("q_ready"))
                    for n in range(LEVELS):
                        m = 1 << n
                        if n % 4 == 0:
                            dve.wait_ge(*at("decay_ready"))
                        e_first, e_second = halves(levels[:, n, :], m)
                        dve.tensor_tensor(e_first, e_first, halves(k_sb[:, 0, :], m)[0], ALU.mult)
                        last = dve.tensor_tensor(e_second, e_second, halves(q_sb[:, 0, :], m)[1], ALU.mult)
                    last.then_inc(sems["level_in_ready"], 1)

                def merge_scores(r):
                    dve.wait_ge(*at("level_done"))
                    for i in range(2):
                        n = 2 * r + i
                        mask = tile2(kcol("levels")[:, n * P:(n + 1) * P])
                        got = wk[:, 2 + r % 2, i * 2 * P:(i + 1) * 2 * P].rearrange("p (t n) -> p t n", t=TB)
                        if n == 0:
                            seq(dve.tensor_tensor(at_sb[:, :, :], got, mask, ALU.mult))
                            continue
                        dve.memset(eps_sb[:, 3:4], 0.0)
                        ins = dve.copy_predicated(at_sb[:, :, :], mask.bitcast(U32), got)
                        if i == 0:
                            seq(ins)
                        else:
                            ins.then_inc(sems["level_merged"], 1)
                            dve.wait_ge(*at("level_merged"))

                def body(h):
                    more = not is_at(h, A_HEADS - 1)
                    merge_scores(0)
                    merge_scores(1)
                    if more:
                        forget(h + 1)
                    merge_scores(2)
                    merge_scores(3)
                    if more:
                        decays()
                    if more and not is_at(h, 0):
                        unit_done()
                        split()
                    if more:
                        queries()
                    dve.wait_ge(*at("o_dev_ready"))
                    for tb in range(TB):
                        dve.scalar_tensor_tensor(hid[:, tb, 0:P], wk[:, 2, tb * P:(tb + 1) * P],
                                                 stat[:, 4 + tb:5 + tb], sg_sb[:, tb, 0:P], ALU.mult, ALU.mult)\
                            .then_inc(sems["o_gated"], 1)
                    if more:
                        decayed()
                    hidden(wk[:, 3, 0:S], 1, gcol("a_out_gain"))
                    unit_done()
                    split()

                forget(0)
                queries()
                decays()
                decayed()
                unit_done()
                split()
                at.pipeline(dve, body, A_HEADS)
                adds(1.0)

            def ple(layer):
                dve.wait_ge(*at("p_hi"))
                lower_part(pT_lo[:, :, :], wk[:, 2, :].rearrange("p (f n) -> p f n", f=2), pT_hi[:, :, :])\
                    .then_inc(sems["p_lo"], 1)
                for c in range(4):
                    unit_done()
                    if c < 3:
                        split()

                def add(tb):
                    sums(tb)
                    dve.wait_ge(*at("ple_gate_ready", 2))
                    seq(dve.tensor_tensor(gate_sb[:, tb, :], gate_sb[:, tb, :],
                                          wk[:, 2 - 2 * tb:4 - 2 * tb, :].rearrange("p b n -> p (b n)"), ALU.mult))
                    return dve.tensor_tensor(res[:, tb, :], res[:, tb, :], gate_sb[:, tb, :], ALU.add)
                pending[0] = add
                owed[0] = 2

            def latent():
                unit_done()
                scaled(lambda tb: wk[:, 0, tb * S:(tb + 1) * S], B_KV)
                unit_done()
                dve.wait_ge(*at("sin_ready", 2))
                dve.wait_ge(*at("zeros_ready", 3))
                dve.wait_ge(*at("kr_raw_ready"))
                dve.tensor_tensor(rot1[:, 0, :], kr_raw[:, :], mla_cos[:, :], ALU.mult)
                dve.wait_ge(*at("kr_rotated"))
                seq(dve.tensor_tensor(rot1[:, 1, :], wk[:, 1, S:2 * S], mla_sin[:, :], ALU.mult))
                for h in range(2):
                    r = slice(h * B_ROPE, (h + 1) * B_ROPE)
                    last = dve.tensor_tensor(krz[r, h, :], rot1[r, 0, :], rot1[r, 1, :], ALU.add)
                last.then_inc(sems["kr_ready"], 1)
                turn(2, (2,), cT_hi, cT_lo, "kv_latent_norm")
                owed[0] = 2

            def softmax(scale, between=None):
                dve.wait_ge(*at("scores_done"))
                seq(dve.tensor_tensor(sc[:, :, :], wk[:, 2:4, 0:SEG], tile2(kcol("causal")), ALU.add))
                dve.tensor_reduce(stat[:, 0:2], sc[:, :, 0:P], AX.X, ALU.max)
                seq(dve.tensor_reduce(stat[:, 2:4], sc[:, :, P:SEG], AX.X, ALU.max))
                dve.tensor_scalar(stat[:, 4:8], stat[:, 0:4], -scale, None, ALU.mult).then_inc(sems["max_ready"], 1)
                if between is not None:
                    between()
                dve.wait_ge(*at("exp_ready"))
                seq(dve.reciprocal(stat[:, 12:16], stat[:, 8:12]))
                for h in range(2):
                    for seg, (a, b) in enumerate(((0, P), (P, SEG))):
                        c = 12 + 2 * seg + h
                        dve.tensor_scalar(prob[:, h, a:b], prob[:, h, a:b], stat[:, c:c + 1], None, ALU.mult)\
                            .then_inc(sems["probs_ready"], 1)

            def second_probs():
                dve.wait_ge(*at("probs_turned", 2))
                dve.tensor_copy(probT[:, 1, :], wk[:, 3, 0:SEG]).then_inc(sems["probsT1_ready"], 1)

            def mla():
                unit_done()
                split()
                unit_done()
                scaled(lambda tb: wk[:, tb, :], B_Q)
                turn(4, (2, 3), fT_hi, fT_lo, "b_q_norm")
                split()

                def rotate():
                    unit_done()
                    dve.wait_ge(*at("qr_raw_ready"))
                    dve.tensor_tensor(rot1[:, 0, :], qr_sb[:, :], mla_cos[:, :], ALU.mult)

                def rotated():
                    dve.wait_ge(*at("qr_rotated"))
                    seq(dve.tensor_tensor(rot1[:, 1, :], wk[:, 1, S:2 * S], mla_sin[:, :], ALU.mult))
                    dve.tensor_tensor(rot2[:, 0, :], rot1[:, 0, :], rot1[:, 1, :], ALU.add)\
                        .then_inc(sems["qr_ready"], 1)
                    split()

                def values():
                    unit_done()
                    dve.tensor_copy(v_sb[:, :, :], wk[:, 1, :].rearrange("p (t n) -> p t n", t=TB))\
                        .then_inc(sems["v_ready"], 1)

                def body(j):
                    more = not is_at(j, B_HEADS // 2 - 1)
                    softmax((B_NOPE + B_ROPE) ** -0.5, split)
                    if not is_at(j, 0):
                        unit_done()
                        split()
                    if more:
                        rotate()
                    second_probs()
                    if more:
                        rotated()
                    hidden(wk[:, 2, :])
                    if more:
                        values()

                rotate()
                rotated()
                values()
                at.pipeline(dve, body, B_HEADS // 2)
                adds(1.0)

            def gated(q):
                which, half = q // 2, q % 2
                c = slice(half * 512, (half + 1) * 512)
                if q == 0:
                    dve.wait_ge(*at("branch_ready", 4))
                for tb in range(TB):
                    g = gates4[:, 2 * (q % 2) + tb, :]
                    dve.wait_ge(*at("gate_ready"))
                    if which == 0:
                        dve.tensor_tensor(tok[:, tb, c], g, gate_sb[:, tb, c], ALU.mult)\
                            .then_inc(sems["gate_used"], 1)
                    else:
                        dve.tensor_tensor(g, g, acc[:, 2 * tb + half, :], ALU.mult)\
                            .then_inc(sems["gate_used"], 1)
                if which:
                    seq(dve.tensor_copy(stat[:, 0:1], stat[:, 1:2]))
                    for tb in range(TB):
                        last = dve.tensor_tensor(tok[:, tb, c], tok[:, tb, c], gates4[:, 2 * (q % 2) + tb, :],
                                                 ALU.add)
                        last.then_inc(sems["tokens_ready"], 1)

            def branches(layer):
                scale = C_DIM ** -0.5

                def values():
                    src = wk[:, 1, 0:2 * P].rearrange("p (t n) -> p t n", t=TB)
                    for h in range(2):
                        c = slice(h * C_DIM, (h + 1) * C_DIM)
                        dve.tensor_copy(vz[:, :, h, c], src[:, :, c]).then_inc(sems["v_ready"], 1)

                def body_sb(j):
                    dve.wait_ge(*at("z_done"))
                    dve.scalar_tensor_tensor(sc[:, :, :], wk[:, 2:4, 0:SEG], scale, tile2(kcol("strict")),
                                             ALU.mult, ALU.add).then_inc(sems["scores_ready"], 1)
                    split()
                    dve.wait_ge(*at("softplus_ready"))
                    dve.scalar_tensor_tensor(keep[:, :, :], sc[:, :, :], 0.0, soft[:, :, :], ALU.max, ALU.add)\
                        .then_inc(sems["keep_ready"], 1)
                    seq(dve.scalar_tensor_tensor(prob[:, :, :], sc[:, :, :], 0.0, soft[:, :, :],
                                                 ALU.min, ALU.subtract))
                    if j:
                        unit_done()
                        split()
                    dve.wait_ge(*at("suffix_done"))
                    dve.tensor_tensor(sc[:, :, :], prob[:, :, :], wk[:, 2:4, 0:SEG], ALU.subtract)\
                        .then_inc(sems["weight_in_ready"], 1)
                    if j + 1 == PAIRS:
                        rotate()
                        rotated()
                    else:
                        unit_done()
                        split()
                    unit_done()
                    hidden(wk[:, 1, S:2 * S], 1)
                    values()

                def rotate():
                    unit_done()
                    dve.wait_ge(*at("qr_raw_ready"))
                    dve.tensor_tensor(levels[:, 0:2, :], rot1[:, :, :], tile2(kcol("moba_cos")), ALU.mult)

                def rotated():
                    dve.wait_ge(*at("qr_rotated"))
                    seq(dve.tensor_tensor(rot2[:, :, :], wk[:, 0, :].rearrange("p (a n) -> p a n", a=2),
                                          tile2(kcol("moba_sin")), ALU.mult))
                    dve.tensor_tensor(q_sb[:, 0, :], levels[:, 0, :], rot2[:, 0, :], ALU.add)\
                        .then_inc(sems["qk_roped"], 1)
                    for h in range(2):
                        r = slice(h * C_DIM, (h + 1) * C_DIM)
                        dve.tensor_tensor(kz[r, h, :], levels[r, 1, :], rot2[r, 1, :], ALU.add)\
                            .then_inc(sems["qk_roped"], 1)
                    split()

                def body_moba(j):
                    more = j + 1 < 2 * PAIRS
                    softmax(scale, split)
                    unit_done()
                    split()
                    if more:
                        rotate()
                        second_probs()
                        rotated()
                        unit_done()
                        hidden(wk[:, 1, S:2 * S], 1)
                        values()
                    else:
                        unit_done()
                        split()
                        second_probs()
                        unit_done()
                        hidden(wk[:, 2, S:2 * S], 1)
                        gated(0)
                        split()

                unit_done()
                split()
                unit_done()
                values()
                for j in range(PAIRS):
                    body_sb(j)
                for j in range(PAIRS, 2 * PAIRS):
                    body_moba(j)
                unit_done()
                split()

            def merge(layer):
                for q in range(1, 4):
                    unit_done()
                    if q == 3:
                        turn(4, (0, 1), fT_hi[:, 0:4, :], fT_lo[:, 0:4, :])
                    split()
                    unit_done()
                    gated(q)
                    split()
                for c in range(3):
                    unit_done()
                    if c == 0:
                        turn(4, (2, 3), fT_hi[:, 4:8, :], fT_lo[:, 4:8, :])
                    split()
                adds(1.0, ALPHA)

            def finish():
                if stop_after is not None:
                    for tb in range(TB):
                        pending[0](tb).then_inc(sems["out_ready"], 1)

            network(Stages(setup=setup, norm=norm, ffn=ffn, hgrn=hgrn, mla=mla, ple=ple, latent=latent,
                           branches=branches, merge=merge, finish=finish))


_INS = ["x", "p", "positions", "norm_gains", "a_lb_logits", "a_out_gain", "kv_norm_in", "kv_latent_norm",
        "b_q_norm", "final_norm", "ln_mix_g_2", "ln_mix_b_2", "ln_ffn_g_2", "ln_ffn_b_2"]


def layout(inputs):
    arrays = {name: np.ascontiguousarray(inputs[name]) for name in _INS}
    w = {name: np.asarray(a) for name, a in inputs.items()}
    arrays["weights"] = np.concatenate([unit.reshape(-1) for unit in stream(w)])
    arrays["const"] = constants()
    return arrays


def kernel(**inputs):
    import concourse.bacc as bacc
    from concourse.bass_utils import run_bass_kernel_spmd

    nc = bacc.Bacc("TRN2", target_bir_lowering=False, num_devices=1)
    arrays = {f"in_{name}": a for name, a in layout(inputs).items()}
    args = [nc.dram_tensor(name, a.shape, mybir.dt.from_np(a.dtype), kind="ExternalInput").ap()
            for name, a in arrays.items()]
    out = nc.dram_tensor("out", (1, S, D), F32, kind="ExternalOutput").ap()
    build(nc, *args, out)
    r = run_bass_kernel_spmd(nc, [arrays], core_ids=[0])
    return r.results[0]["out"]
```
